# Optimizing a Trainium2 kernel written in Bass

```python
import math
import jax, jax.numpy as jnp
from jax import lax
import numpy as np

D_MODEL = 1024
BATCH = 1
SEQ = 256
DEPTH = 2
DEC_BATCH = 8
DEC_SEQ = 4
PAST_LEN = 256
PAGE_SIZE = 128

SSD_EXPAND = 2
D_INNER = SSD_EXPAND * D_MODEL
SSD_HEAD_DIM = 64
SSD_HEADS = D_INNER // SSD_HEAD_DIM
SSD_GROUPS = 8
SSD_HPG = SSD_HEADS // SSD_GROUPS
D_STATE = 128
CONV_WIDTH = 4
CONV_DIM = D_INNER + 2 * SSD_GROUPS * D_STATE
SSD_CHUNK = 128
ATTN_HEAD_DIM = 64
HEADS_PER_GROUP = 4
WINDOWS = (128, 512, 2048)
DILATIONS = (1, 4, 16)
N_DIL_GROUPS = 3
ATTN_HEADS = N_DIL_GROUPS * HEADS_PER_GROUP
ATTN_WIDTH = ATTN_HEADS * ATTN_HEAD_DIM
ATTN_OUT_WIDTH = HEADS_PER_GROUP * ATTN_HEAD_DIM
ATTN_BLOCK = 128
ATTN_SCALE = ATTN_HEAD_DIM ** -0.5
REL_BUCKETS = 32
REL_MAX_DIST = 2048
D_FF = 2816
FFN_RES = 0.5
NORM_EPS = 1e-6
IN_SIZES = (D_INNER, CONV_DIM, SSD_HEADS, ATTN_WIDTH, ATTN_WIDTH, ATTN_WIDTH, D_MODEL, D_MODEL)
IN_WIDTH = D_INNER + CONV_DIM + SSD_HEADS + 3 * ATTN_WIDTH + 2 * D_MODEL

kernel_name = 'hybrid_ssd_dilated_attn_decoder'

def split_cols(t, sizes):
    out, start = [], 0
    for s in sizes:
        out.append(t[..., start:start + s])
        start += s
    return out

def rmsnorm(x, g):
    xf = x.astype(jnp.float32)
    y = xf * lax.rsqrt(jnp.mean(xf * xf, axis=-1, keepdims=True) + NORM_EPS)
    return (y * g.astype(jnp.float32)).astype(x.dtype)

def grouped_rmsnorm(x, g, n_groups):
    shp = x.shape
    xf = x.astype(jnp.float32).reshape(shp[:-1] + (n_groups, shp[-1] // n_groups))
    y = xf * lax.rsqrt(jnp.mean(xf * xf, axis=-1, keepdims=True) + NORM_EPS)
    return (y.reshape(shp) * g.astype(jnp.float32)).astype(x.dtype)

def swiglu(x, w13, w2):
    a, b = jnp.split(x @ w13, 2, axis=-1)
    return (jax.nn.silu(a) * b) @ w2

def rel_bucket(dist):
    max_exact = REL_BUCKETS // 2
    d = jnp.maximum(dist, 1).astype(jnp.float32)
    large = max_exact + (jnp.log(d / max_exact) / math.log(REL_MAX_DIST / max_exact)
                         * (REL_BUCKETS - max_exact)).astype(jnp.int32)
    large = jnp.minimum(large, REL_BUCKETS - 1)
    return jnp.where(dist < max_exact, dist, large)

def dilated_attn_prompt(q, k, v, bias_tab, dil, window):
    b, s, h, e = q.shape
    n_sub = s // dil
    reach = window // dil
    blk = ATTN_BLOCK
    nb = -(-n_sub // blk)
    pad_end = nb * blk - n_sub

    def fold(t):
        return t.reshape(b, n_sub, dil, h, e).transpose(0, 2, 1, 3, 4).reshape(b * dil, n_sub, h, e)

    qf = jnp.pad(fold(q), ((0, 0), (0, pad_end), (0, 0), (0, 0)))
    kf = jnp.pad(fold(k), ((0, 0), (blk, pad_end), (0, 0), (0, 0)))
    vf = jnp.pad(fold(v), ((0, 0), (blk, pad_end), (0, 0), (0, 0)))
    qb = qf.reshape(b * dil, nb, blk, h, e)
    kb = kf.reshape(b * dil, nb + 1, blk, h, e)
    vb = vf.reshape(b * dil, nb + 1, blk, h, e)
    kb = jnp.concatenate([kb[:, :-1], kb[:, 1:]], axis=2)
    vb = jnp.concatenate([vb[:, :-1], vb[:, 1:]], axis=2)
    qi = jnp.arange(blk)[:, None] + blk
    ki = jnp.arange(2 * blk)[None, :]
    step = qi - ki
    blk_start = jnp.arange(nb)[:, None, None] * blk
    valid = (step >= 0) & (step <= reach) & (blk_start + ki[None] - blk >= 0)
    bias = bias_tab[rel_bucket(jnp.maximum(step, 0) * dil)].transpose(2, 0, 1)
    logits = jnp.einsum('znqhe,znkhe->znhqk', qb, kb).astype(jnp.float32) * ATTN_SCALE
    logits = logits + bias.astype(jnp.float32)[None, None]
    logits = jnp.where(valid[None, :, None], logits, -jnp.inf)
    lse = jax.nn.logsumexp(logits, axis=-1)
    p = jnp.exp(logits - lse[..., None])
    o = jnp.einsum('znhqk,znkhe->znqhe', p.astype(vb.dtype), vb)
    o = o.reshape(b * dil, nb * blk, h, e)[:, :n_sub]
    o = o.reshape(b, dil, n_sub, h, e).transpose(0, 2, 1, 3, 4).reshape(b, s, h, e)
    lse = lse.transpose(0, 1, 3, 2).reshape(b * dil, nb * blk, h)[:, :n_sub]
    lse = lse.reshape(b, dil, n_sub, h).transpose(0, 2, 1, 3).reshape(b, s, h)
    return o, lse

def dilated_attn_sample(q, k, v, kv_buf, bias_tab, dil, window):
    t = q.shape[1]
    lb = kv_buf.shape[1]
    k_all = jnp.concatenate([kv_buf[:, :, 0].astype(k.dtype), k], axis=1)
    v_all = jnp.concatenate([kv_buf[:, :, 1].astype(v.dtype), v], axis=1)
    n_keys = window // dil + 1
    j = jnp.arange(n_keys)
    idx = lb + jnp.arange(t)[:, None] - j[None, :] * dil
    valid = idx >= 0
    idx_c = jnp.maximum(idx, 0)
    kg = k_all[:, idx_c]
    vg = v_all[:, idx_c]
    bias = bias_tab[rel_bucket(j * dil)].T
    logits = jnp.einsum('bthe,btjhe->bthj', q, kg).astype(jnp.float32) * ATTN_SCALE
    logits = logits + bias.astype(jnp.float32)[None, None]
    logits = jnp.where(valid[None, :, None, :], logits, -jnp.inf)
    lse = jax.nn.logsumexp(logits, axis=-1)
    p = jnp.exp(logits - lse[..., None])
    o = jnp.einsum('bthj,btjhe->bthe', p.astype(vg.dtype), vg)
    return o, lse

def ssd_scan(x, dt, a_head, bmat, cmat, h0):
    bsz, seqlen = x.shape[:2]
    cl = min(SSD_CHUNK, seqlen)
    nc = -(-seqlen // cl)
    pad = nc * cl - seqlen

    def chunk(t):
        t = jnp.pad(t, [(0, 0), (0, pad)] + [(0, 0)] * (t.ndim - 2))
        return t.reshape((bsz, nc, cl) + t.shape[2:])

    xdt = chunk(x.astype(jnp.float32) * dt[..., None])
    a = chunk(dt * a_head)
    bc = chunk(bmat)
    cc = chunk(cmat)
    a_cs = jnp.cumsum(a, axis=2)
    causal = jnp.tril(jnp.ones((cl, cl), dtype=bool))
    seg = a_cs[:, :, :, None] - a_cs[:, :, None, :]
    decay = jnp.exp(jnp.where(causal[:, :, None, None], seg, -jnp.inf))
    cb = jnp.einsum('bclgn,bcsgn->bclsg', cc, bc).astype(jnp.float32)
    y_diag = jnp.einsum('bclsgr,bcsgrp->bclgrp', cb[..., None] * decay, xdt)
    to_end = jnp.exp(a_cs[:, :, -1:] - a_cs)
    states = jnp.einsum('bclgn,bclgrp->bcgrpn', bc.astype(jnp.float32), xdt * to_end[..., None])
    chunk_decay = jnp.exp(a_cs[:, :, -1])

    def step(h, inp):
        s_c, d_c = inp
        return h * d_c[..., None, None] + s_c, h

    h_last, h_prev = lax.scan(step, h0.astype(jnp.float32),
                              (jnp.moveaxis(states, 1, 0), jnp.moveaxis(chunk_decay, 1, 0)))
    h_prev = jnp.moveaxis(h_prev, 0, 1)
    y_off = jnp.einsum('bclgn,bcgrpn->bclgrp', cc.astype(jnp.float32), h_prev) * jnp.exp(a_cs)[..., None]
    y = (y_diag + y_off).reshape((bsz, nc * cl) + x.shape[2:])[:, :seqlen]
    return y.astype(x.dtype), h_last.astype(h0.dtype)

def token_mixing(u, conv_state, ssm_state, kv_bufs, rel_bias, w_in, conv_w, conv_b, dt_bias, a_log,
                 d_skip, ssd_norm, w_ssd_out, w_attn_out, w_o):
    bsz, seqlen, _ = u.shape
    z, xbc, dt_raw, q, k, v, g_ssd, g_attn = split_cols(u @ w_in, IN_SIZES)
    xbc_full = jnp.concatenate([conv_state.astype(xbc.dtype), xbc], axis=1)
    new_conv = xbc_full[:, -(CONV_WIDTH - 1):]
    conv = conv_b + sum(xbc_full[:, i:i + seqlen] * conv_w[i] for i in range(CONV_WIDTH))
    conv = jax.nn.silu(conv)
    xs, bmat, cmat = split_cols(conv, (D_INNER, SSD_GROUPS * D_STATE, SSD_GROUPS * D_STATE))
    dt = jax.nn.softplus(dt_raw.astype(jnp.float32) + dt_bias.astype(jnp.float32))
    a_head = -jnp.exp(a_log.astype(jnp.float32))
    xs5 = xs.reshape(bsz, seqlen, SSD_GROUPS, SSD_HPG, SSD_HEAD_DIM)
    y, new_ssm = ssd_scan(xs5, dt.reshape(bsz, seqlen, SSD_GROUPS, SSD_HPG),
                          a_head.reshape(SSD_GROUPS, SSD_HPG),
                          bmat.reshape(bsz, seqlen, SSD_GROUPS, D_STATE),
                          cmat.reshape(bsz, seqlen, SSD_GROUPS, D_STATE),
                          ssm_state.reshape(bsz, SSD_GROUPS, SSD_HPG, SSD_HEAD_DIM, D_STATE))
    y = y + d_skip.reshape(SSD_GROUPS, SSD_HPG)[:, :, None].astype(y.dtype) * xs5
    y = grouped_rmsnorm(y.reshape(bsz, seqlen, D_INNER) * jax.nn.silu(z), ssd_norm, SSD_GROUPS)
    ssd_out = y @ w_ssd_out
    q = q.reshape(bsz, seqlen, ATTN_HEADS, ATTN_HEAD_DIM)
    k = k.reshape(bsz, seqlen, ATTN_HEADS, ATTN_HEAD_DIM)
    v = v.reshape(bsz, seqlen, ATTN_HEADS, ATTN_HEAD_DIM)
    outs, lses, new_kv = [], [], []
    for gi in range(N_DIL_GROUPS):
        hsl = slice(gi * HEADS_PER_GROUP, (gi + 1) * HEADS_PER_GROUP)
        qg, kg, vg, bias_g = q[:, :, hsl], k[:, :, hsl], v[:, :, hsl], rel_bias[:, hsl]
        if kv_bufs is None:
            o, lse = dilated_attn_prompt(qg, kg, vg, bias_g, DILATIONS[gi], WINDOWS[gi])
            rows = jnp.stack([kg, vg], axis=2)[:, -min(WINDOWS[gi], seqlen):]
        else:
            o, lse = dilated_attn_sample(qg, kg, vg, kv_bufs[gi], bias_g, DILATIONS[gi], WINDOWS[gi])
            rows = jnp.stack([kg, vg], axis=2)
        outs.append(o)
        lses.append(lse)
        new_kv.append(rows)
    wts = jax.nn.softmax(jnp.stack(lses, axis=0), axis=0)
    o = jnp.sum(wts[..., None] * jnp.stack(outs, axis=0).astype(jnp.float32), axis=0)
    attn_out = o.astype(u.dtype).reshape(bsz, seqlen, ATTN_OUT_WIDTH) @ w_attn_out
    merged = jax.nn.sigmoid(g_ssd) * ssd_out + jax.nn.sigmoid(g_attn) * attn_out
    new_ssm = new_ssm.reshape(bsz, SSD_HEADS, SSD_HEAD_DIM, D_STATE)
    return merged @ w_o, new_conv, new_ssm, new_kv

def trunk_layer(x, conv_state, ssm_state, kv_bufs, rel_bias, lw):
    (f1n, f1w13, f1w2, mn, w_in, conv_w, conv_b, dt_bias, a_log, d_skip, ssd_norm,
     w_ssd_out, w_attn_out, w_o, f2n, f2w13, f2w2) = lw
    x = x + FFN_RES * swiglu(rmsnorm(x, f1n), f1w13, f1w2)
    mix, new_conv, new_ssm, new_kv = token_mixing(rmsnorm(x, mn), conv_state, ssm_state, kv_bufs, rel_bias,
                                                  w_in, conv_w, conv_b, dt_bias, a_log, d_skip, ssd_norm,
                                                  w_ssd_out, w_attn_out, w_o)
    x = x + mix
    x = x + FFN_RES * swiglu(rmsnorm(x, f2n), f2w13, f2w2)
    return x, new_conv, new_ssm, new_kv

def setup_inputs(seed: int = 0) -> dict:
    key = jax.random.key(seed)
    ks = iter(jax.random.split(key, 32))

    def nrm(shape, scale):
        return jax.random.normal(next(ks), shape, jnp.float32) * scale

    def gain(shape):
        return 1.0 + nrm(shape, 0.02)

    x_prompt = nrm((BATCH, SEQ, D_MODEL), 1.0)
    x_sample = nrm((DEC_BATCH, DEC_SEQ, D_MODEL), 1.0)
    kv_tail = (2, HEADS_PER_GROUP, ATTN_HEAD_DIM)
    cache_kv_w128 = nrm((DEPTH, DEC_BATCH, min(WINDOWS[0], PAST_LEN)) + kv_tail, 1.0)
    cache_kv_w512 = nrm((DEPTH, DEC_BATCH, min(WINDOWS[1], PAST_LEN)) + kv_tail, 1.0)
    cache_kv_w2048 = nrm((DEPTH, DEC_BATCH, min(WINDOWS[2], PAST_LEN)) + kv_tail, 1.0)
    state_conv = nrm((DEPTH, DEC_BATCH, CONV_WIDTH - 1, CONV_DIM), 1.0)
    state_ssm = nrm((DEPTH, DEC_BATCH, SSD_HEADS, SSD_HEAD_DIM, D_STATE), 0.1)
    rel_bias = nrm((REL_BUCKETS, ATTN_HEADS), 0.5)
    ffn1_norm = gain((DEPTH, D_MODEL))
    ffn1_w13 = nrm((DEPTH, D_MODEL, 2 * D_FF), D_MODEL ** -0.5)
    ffn1_w2 = nrm((DEPTH, D_FF, D_MODEL), D_FF ** -0.5)
    mix_norm = gain((DEPTH, D_MODEL))
    w_in = nrm((DEPTH, D_MODEL, IN_WIDTH), D_MODEL ** -0.5)
    conv_w = nrm((DEPTH, CONV_WIDTH, CONV_DIM), CONV_WIDTH ** -0.5)
    conv_b = nrm((DEPTH, CONV_DIM), 0.02)
    dt0 = jnp.exp(jax.random.uniform(next(ks), (DEPTH, SSD_HEADS), jnp.float32,
                                     math.log(1e-3), math.log(1e-1)))
    dt_bias = dt0 + jnp.log(-jnp.expm1(-dt0))
    a_log = jnp.log(jax.random.uniform(next(ks), (DEPTH, SSD_HEADS), jnp.float32, 1.0, 16.0))
    d_skip = 1.0 + nrm((DEPTH, SSD_HEADS), 0.02)
    ssd_norm = gain((DEPTH, D_INNER))
    w_ssd_out = nrm((DEPTH, D_INNER, D_MODEL), D_INNER ** -0.5)
    w_attn_out = nrm((DEPTH, ATTN_OUT_WIDTH, D_MODEL), ATTN_OUT_WIDTH ** -0.5)
    w_o = nrm((DEPTH, D_MODEL, D_MODEL), D_MODEL ** -0.5)
    ffn2_norm = gain((DEPTH, D_MODEL))
    ffn2_w13 = nrm((DEPTH, D_MODEL, 2 * D_FF), D_MODEL ** -0.5)
    ffn2_w2 = nrm((DEPTH, D_FF, D_MODEL), D_FF ** -0.5)
    final_norm = gain((D_MODEL,))
    return {'x_prompt': x_prompt, 'x_sample': x_sample,
            'cache_kv_w128': cache_kv_w128, 'cache_kv_w512': cache_kv_w512, 'cache_kv_w2048': cache_kv_w2048,
            'state_conv': state_conv, 'state_ssm': state_ssm, 'rel_bias': rel_bias,
            'ffn1_norm': ffn1_norm, 'ffn1_w13': ffn1_w13, 'ffn1_w2': ffn1_w2, 'mix_norm': mix_norm,
            'w_in': w_in, 'conv_w': conv_w, 'conv_b': conv_b, 'dt_bias': dt_bias, 'a_log': a_log,
            'd_skip': d_skip, 'ssd_norm': ssd_norm, 'w_ssd_out': w_ssd_out, 'w_attn_out': w_attn_out,
            'w_o': w_o, 'ffn2_norm': ffn2_norm, 'ffn2_w13': ffn2_w13, 'ffn2_w2': ffn2_w2,
            'final_norm': final_norm}

def reference(x_prompt, x_sample, cache_kv_w128, cache_kv_w512, cache_kv_w2048, state_conv, state_ssm,
              rel_bias, ffn1_norm, ffn1_w13, ffn1_w2, mix_norm, w_in, conv_w, conv_b, dt_bias, a_log,
              d_skip, ssd_norm, w_ssd_out, w_attn_out, w_o, ffn2_norm, ffn2_w13, ffn2_w2, final_norm):
    hp, hs = x_prompt, x_sample
    bp = x_prompt.shape[0]
    kv_p = [[], [], []]
    kv_s = [[], [], []]
    conv_p, conv_s, ssm_p, ssm_s = [], [], [], []
    for l in range(DEPTH):
        lw = (ffn1_norm[l], ffn1_w13[l], ffn1_w2[l], mix_norm[l], w_in[l], conv_w[l], conv_b[l],
              dt_bias[l], a_log[l], d_skip[l], ssd_norm[l], w_ssd_out[l], w_attn_out[l], w_o[l],
              ffn2_norm[l], ffn2_w13[l], ffn2_w2[l])
        zc = jnp.zeros((bp, CONV_WIDTH - 1, CONV_DIM), hp.dtype)
        zs = jnp.zeros((bp, SSD_HEADS, SSD_HEAD_DIM, D_STATE), hp.dtype)
        hp, c_p, s_p, kvn_p = trunk_layer(hp, zc, zs, None, rel_bias, lw)
        bufs = (cache_kv_w128[l], cache_kv_w512[l], cache_kv_w2048[l])
        hs, c_s, s_s, kvn_s = trunk_layer(hs, state_conv[l], state_ssm[l], bufs, rel_bias, lw)
        conv_p.append(c_p)
        ssm_p.append(s_p)
        conv_s.append(c_s)
        ssm_s.append(s_s)
        for gi in range(N_DIL_GROUPS):
            kv_p[gi].append(kvn_p[gi])
            kv_s[gi].append(kvn_s[gi])
    y_prompt = rmsnorm(hp, final_norm)
    y_sample = rmsnorm(hs, final_norm)
    return (y_prompt, y_sample,
            jnp.stack(kv_p[0]), jnp.stack(kv_p[1]), jnp.stack(kv_p[2]), jnp.stack(conv_p), jnp.stack(ssm_p),
            jnp.stack(kv_s[0]), jnp.stack(kv_s[1]), jnp.stack(kv_s[2]), jnp.stack(conv_s), jnp.stack(ssm_s))


_drawn_inputs = setup_inputs


def setup_inputs(seed=0):
    import zlib

    import numpy as np

    out = dict(_drawn_inputs(seed))
    spreads = {}
    factors = {'ffn1_norm': 3.839,
     'd_skip': 30.339,
     'ssd_norm': 15.71,
     'ffn2_norm': 5.545,
     'final_norm': 7.755,
     'cache_kv_w128': 3.045,
     'cache_kv_w512': 4.916,
     'cache_kv_w2048': 8.0,
     'rel_bias': 4.272}
    for name, (base, spread) in spreads.items():
        noise = np.random.default_rng([zlib.crc32(name.encode()), seed]).standard_normal(out[name].shape)
        drawn = base * np.exp(spread * noise) if base else spread * noise
        out[name] = __import__('jax').numpy.asarray(drawn.astype(out[name].dtype))
    for name, factor in factors.items():
        out[name] = (out[name] * factor).astype(out[name].dtype)
    return out
```

```python
from contextlib import ExitStack

import numpy as np

import concourse.bass as bass
from concourse import mybir

F32 = mybir.dt.float32
F32R = mybir.dt.float32r
ALU = mybir.AluOpType
ACT = mybir.ActivationFunctionType
AX = mybir.AxisListType

P = 128
D = 1024
KD = D // P
TP = 256
NB, NT = 8, 4
TS = NB * NT
T = TP + TS
FF = 2816
KF = FF // P
DI = 2048
KI = DI // P
CONV = 4096
KC = CONV // P
CW = 4
HEADS = 32
HD = 64
NS = 128
G = 8
HPG = 4
AW = 768
NG = 3
DIL = (1, 4, 16)
REACH = 128
SCALE = HD ** -0.5
EPS = 1e-6
MASKED = -1e30

C_Z = 0
C_XBC = DI
C_DT = C_XBC + CONV
C_Q = C_DT + HEADS
C_G = C_Q + 3 * AW

PADDED = CW - 1 + TP + NB * (CW - 1 + NT)
SEQ0 = CW - 1 + TP
RUN = CW - 1 + NT
CONVED = PADDED - (CW - 1)
PITCH = 320

KEYS = (128, 256, 64)
OLD = sum(KEYS)
NEW = NG * TS
KV_BUFS = 4
W_LINE = 384

UNIT = 2048
PAIRS_W13, PAIRS_W2, PAIRS_QKV, PAIRS_XBC, PAIRS_SIDE, PAIRS_G = 11, 6, 5, 8, 6, 2
PAIRS_SO, PAIRS_AO, PAIRS_WO = 4, 1, 2
M_W13A = 0
M_W2A = M_W13A + PAIRS_W13
M_QKV = M_W2A + PAIRS_W2
M_XBC = M_QKV + PAIRS_QKV
M_SIDE = M_XBC + PAIRS_XBC
M_G = M_SIDE + PAIRS_SIDE
M_SO = M_G + PAIRS_G
M_AO = M_SO + PAIRS_SO
M_WO = M_AO + PAIRS_AO
M_W13B = M_WO + PAIRS_WO
M_W2B = M_W13B + PAIRS_W13
PAIRS = M_W2B + PAIRS_W2
E_W13A = 0
E_QKV = E_W13A + PAIRS_W13
E_XBC = E_QKV + PAIRS_QKV
E_G = E_XBC + PAIRS_XBC
E_W13B = E_G + PAIRS_G
EVACS = E_W13B + PAIRS_W13
R_W2A, R_SO, R_AO, R_WO, R_W2B = 0, 4, 8, 12, 16
ROWS = 20
SIDE_TILES = 3 * G


def side_unit(n):
    return (True, n // 3) if n % 3 == 1 else (False, n - (n + 1) // 3)


def constants():
    f = np.float32
    i = np.arange(P)
    sq = np.zeros((P, 4, P), f)
    sq[:, 0] = np.eye(P)
    sq[:, 1] = 1
    sq[:, 2] = i[:, None] <= i[None]
    sq[:, 3] = i[:, None] > i[None]
    j = np.arange(TS)
    same = j[:, None] // NT == j[None] // NT
    small = np.zeros((TS, 2 * TS + NB), f)
    small[:, :TS] = same & (j[:, None] <= j[None])
    small[:, TS:TS + NB] = j[:, None] // NT == np.arange(NB)[None]
    small[:, TS + NB:] = same & (j[:, None] > j[None])

    def bucket(d):
        big = 16 + np.floor(np.log(np.maximum(d, 1) / 16.0) / np.log(128.0) * 16 + 1e-9).astype(int)
        return np.where(d < 16, d, np.minimum(big, 31))

    line = np.zeros((32, NG, W_LINE), f)
    line_mask = np.full((HPG, NG, W_LINE), MASKED, f)
    d = 255 - np.arange(W_LINE)
    for g, dil in enumerate(DIL):
        ok = (d >= 0) & (d % dil == 0) & (d // dil <= REACH)
        line[bucket(np.maximum(d, 0))[ok], g, np.nonzero(ok)[0]] = 1
        line_mask[:, g, ok] = 0
    hot = np.zeros((P, OLD + NEW), f)
    mask = np.full((P, OLD + NEW), MASKED, f)
    row_q, row_b = i % NT, i // (HPG * NT)

    def key(col, q, dist):
        hot[32 * q + bucket(np.array(dist)), col] = 1

    col = 0
    for g, dil in enumerate(DIL):
        for n in range(KEYS[g]):
            at = n if g < 2 else 16 * (n // NT) + n % NT
            for q in range(NT):
                dist = (KEYS[g] if g < 2 else 256) + q - at
                if dist % dil == 0 and dist // dil <= REACH:
                    key(col, q, dist)
                    mask[row_q == q, col] = 0
            col += 1
    for g, dil in enumerate(DIL):
        for n in range(TS):
            for q in range(NT):
                dist = q - n % NT
                if dist >= 0 and dist % dil == 0:
                    key(col, q, dist)
                    mask[(row_q == q) & (row_b == n // NT), col] = 0
            col += 1
    delta = np.zeros((P, P), f)
    delta[:] = (i[:, None] // 32) == (i[None] % NT)
    return {"c_square": sq, "c_small": small, "c_line": line, "c_line_mask": line_mask,
            "c_hot": hot, "c_mask": mask, "c_delta": delta}


class Signal:

    def __init__(self, sem, per, credit=0):
        self.sem, self.per, self.credit = sem, per, credit

    def at(self, layer, n):
        return layer * self.per + (n + self.credit)


def trunk(nc, x_prompt, x_sample, cache_kv_w128, cache_kv_w512, cache_kv_w2048, state_conv, state_ssm,
          rel_bias, ffn1_norm, ffn1_w13, ffn1_w2, mix_norm, w_in, conv_w, conv_b, dt_bias, a_log,
          d_skip, ssd_norm, w_ssd_out, w_attn_out, w_o, ffn2_norm, ffn2_w13, ffn2_w2, final_norm,
          c_square, c_small, c_line, c_line_mask, c_hot, c_mask, c_delta,
          y_prompt, y_sample, kv0_prompt, kv1_prompt, kv2_prompt, conv_prompt, ssm_prompt,
          kv0_sample, kv1_sample, kv2_sample, conv_sample, ssm_sample):
    DEPTH = w_in.shape[0]
    kv_prompt = (kv0_prompt, kv1_prompt, kv2_prompt)
    kv_sample = (kv0_sample, kv1_sample, kv2_sample)
    lines_dram = nc.dram_tensor("bias_lines", (NG * HPG, W_LINE), F32, kind="Internal").ap()
    SKEWED = P * (W_LINE + 1)
    skewed = nc.dram_tensor("bias_skewed", (NG * HPG, SKEWED), F32, kind="Internal").ap()

    cursor = [16512]

    def place(name, shape, dt=F32, at=None):
        size = 4 * int(np.prod(shape[1:]))
        size += -size % 32
        if at is None:
            at = cursor[0]
            cursor[0] += size
        assert at + size <= 229344, (name, at + size)
        return nc.alloc_sbuf_tensor_at(name, shape, dt, offset=at)

    raw = [place(f"w_raw{s}", [P, UNIT]) for s in range(2)]
    w_hi = [place(f"w_hi{s}", [P, UNIT], F32R) for s in range(2)]
    w_lo = [place(f"w_lo{s}", [P, UNIT], F32R) for s in range(2)]
    x = place("x", [P, KD, T])
    u_at = cursor[0]
    u_hi = place("u_hi", [P, KD, T], F32R)
    u_lo = place("u_lo", [P, KD, T], F32R)
    mg_hi = place("merged_hi", [P, KD, T], F32R, at=u_at)
    mg_lo = place("merged_lo", [P, KD, T], F32R, at=u_at + 4 * KD * T)
    ao_at = cursor[0]
    ao_hi = place("attn_hi", [P, 2, T], F32R)
    ao_lo = place("attn_lo", [P, 2, T], F32R)
    attn_at = cursor[0]
    attn = place("attn", [P, 2, T])
    silu_z = place("silu_z", [P, 2, T], at=attn_at)
    bias_p = place("bias_prompt", [P, NG * HPG, 2 * P])
    bias_s = place("bias_sample", [P, OLD + NEW])
    square = place("square", [P, 4, P])
    small = place("small", [TS, 2 * TS + NB])
    ident, ones, tri, sgt = (square[:, n, :] for n in range(4))
    tri_sel_s, sel_s, tri_s, sgt_s = (small[:, 0:TS + NB], small[:, TS:TS + NB], small[:, 0:TS],
                                      small[:, TS + NB:])
    vec_a = place("vec_a", [P, P])
    vec_b = place("vec_b", [80, P])
    conv_wt = place("conv_wt", [P, CW * KC])
    vecs = place("vecs", [P, 80])
    V_CONVB, V_F1, V_MIX, V_F2, V_SSD, V_FIN = 0, 32, 40, 48, 56, 72
    rows3 = place("rows3", [P, 3, HEADS])
    a_head = place("a_head", [P, HEADS])
    skip = place("skip", [P, KI])
    eps = place("eps", [P, 1])
    q_diag = place("q_diag", [P, 2 * NG, NB, 2 * NT])
    dt_fm = place("dt_fm", [HEADS, T])
    dt_raw = place("dt_raw", [P, 3, HEADS])
    dt = place("dt", [P, 3, HEADS])
    da = place("da", [P, 3, HEADS])
    dt_w = [place(f"dt_w{n}", [P, 3, HEADS]) for n in range(3)]
    to_end = place("to_end", [P, 4, HEADS])

    F_AT = cursor[0]
    flat = place("flat", [P, KC, PITCH])
    h_hi = place("h_hi", [P, KF, T], F32R, at=F_AT)
    gates = flat[:, KI:2 * KI, 0:T]
    R1 = cursor[0]
    cursor[0] += 39168
    h_lo = place("h_lo", [P, KF, T], F32R, at=R1)
    qkv = place("qkv", [P, 18, T], at=R1)
    conv_in = place("conv_in", [NB * (CW - 1), CONV], at=R1 + 20736)
    kv_p = place("kv_p", [P, 2, NG, 2, 256], at=R1 + 20736)
    kv_s = place("kv_s", [TS, NG, 2, 256], at=R1 + 20736 + 12288)
    conv_out = place("conv_out", [27, CONV], at=R1)
    y_hi = place("y_hi", [P, KI, T], F32R, at=R1)
    y_lo = place("y_lo", [P, KI, T], F32R, at=R1 + 4 * KI * T)
    R2 = cursor[0]

    class Plan:

        def __init__(self, at):
            self.now = at

        def __call__(self, name, shape, dt=F32):
            size = 4 * int(np.prod(shape[1:]))
            size += -size % 32
            at, self.now = self.now, self.now + size
            return place(name, shape, dt, at=at)

    r = Plan(R2)
    x_in = r("x_in", [P, 2, D])
    xs_in = r("xs_in", [TS, D])
    rf = Plan(R1 + 4 * KF * T)
    lines = rf("lines", [HPG, NG, W_LINE])
    line_mask = rf("line_mask", [HPG, NG, W_LINE])
    rf = Plan(F_AT + 4 * KF * T)
    line_hot = rf("line_hot", [32, NG, W_LINE])
    hot = rf("hot", [P, OLD + NEW])
    mask = rf("mask", [P, OLD + NEW])
    delta = rf("delta", [P, NB, HPG, NT])
    rel4 = rf("rel4", [P, NG * HPG])
    rel_q = rf("rel_q", [P, NG, NB, HPG, NT])
    r = Plan(R2)
    full = r("full", [P, KD, T])
    rms = r("rms", [P, T])
    rinv = r("rinv", [P, T])
    silu_a = r("silu_a", [P, 2, T])
    hidden = r("hidden", [P, 2, T])
    y_out = place("y_out", [P, 2, D], at=F_AT)
    y_out_s = place("y_out_s", [TS, D], at=F_AT + 8192)
    r = Plan(R2)
    kv_in = [r(f"kv_in{n}", [P, 4, 256]) for n in range(KV_BUFS)]
    sc_s = place("sc_s", [P, OLD + NEW], at=r.now)
    k_t = [r(f"k_t{n}", [P, 2, OLD]) for n in range(2)]
    st = place("st", [P, 4, P], at=ao_at)
    st_new = place("st_new", [TS, NG, P], at=ao_at + 4 * 4 * P)
    stat_s = [r(f"stat_s{n}", [P, 1]) for n in range(3)]
    r = Plan(R2)
    sc_p = [r(f"sc_p{n}", [P, NG, 2 * P]) for n in range(2)]
    pt_p = [r(f"pt_p{n}", [P, NG, 2, P]) for n in range(2)]
    stat_p = [[r(f"stat_p{n}_{m}", [P, 1]) for m in range(3)] for n in range(2)]
    r = Plan(R2)
    acc = [r(f"acc{n}", [P, 2, PADDED]) for n in range(2)]
    tails = r("tails", [P, KC, 9, CW - 1])
    r = Plan(R2)
    h0 = [r(f"h0_{n}", [P, NB, NS]) for n in range(3)]
    h0_t = r("h0_t", [P, NB, P])
    a_tri = [r(f"a_tri{n}", [P, HPG, P]) for n in range(2)]
    xdt = r("xdt", [P, 2, 256])
    cbm = r("cbm", [P, 2, P])
    r = Plan(R1 + 16384)
    dec = [r(f"dec{n}", [P, HPG, P]) for n in range(2)]
    b_tm = r("b_tm", [P, 2, NS])
    xdte = r("xdte", [P, 3, 256])
    e_off = r("e_off", [P, 2, P])
    a_exp = r("a_exp", [P, 256])
    h_mid = r("h_mid", [P, 256])
    off_t = r("off_t", [P, 2, P])
    h_end = r("h_end", [P, 2, NS])
    xdt_s = r("xdt_s", [TS, 256])
    xdte_s = r("xdte_s", [TS, 256])
    b_tm_s = r("b_tm_s", [TS, NS])
    b_diag = r("b_diag", [TS, NB, NS])
    cbm_s = r("cbm_s", [TS, TS])
    a_tri_s = r("a_tri_s", [TS, HPG, TS])
    dec_s = r("dec_s", [TS, HPG, TS])
    a_exp_s = r("a_exp_s", [TS, 256])
    e_s = r("e_s", [P, 2, TS + NB])
    off_s = r("off_s", [P, 2, TS])
    assert r.now <= R2, r.now - R2
    y_sq = place("y_sq", [P, KI, T], at=R2 + 4 * 1440)
    y_rms = place("y_rms", [P, G, T], at=R2 + 4 * 4 * T)
    merged = place("merged", [P, KD, T], at=R2)
    print_free = 229344 - cursor[0]
    assert print_free > 24000

    ps = nc.alloc_psum_tensor("ps", [P, 8, 512], F32)

    with ExitStack() as ctx:
        def sem(name, per, credit=0):
            return Signal(ctx.enter_context(nc.semaphore(name)), per, credit)

        settled = sem("settled", 0)
        const_in = sem("const_in", 0)
        x_in_ready = sem("x_in_ready", 0)
        start_in = sem("start_in", 0)
        x_turned = sem("x_turned", 0)
        x_first = sem("x_first", 0)
        rel_q_ready = sem("rel_q_ready", 0)
        bias_product = sem("bias_product", 0)
        lines_ready = sem("lines_ready", 0)
        lines_out = sem("lines_out", 0)
        skewed_out = sem("skewed_out", 0)
        bias_in = sem("bias_in", 0)
        zeroed = sem("zeroed", 0)
        raw_in = [sem(f"raw_in{s}", 16 * PAIRS) for s in range(2)]
        hi_ready = [sem(f"hi_ready{s}", PAIRS) for s in range(2)]
        lo_ready = [sem(f"lo_ready{s}", PAIRS, 1) for s in range(2)]
        unit_done = [sem(f"unit_done{s}", PAIRS, 1) for s in range(2)]
        evac = [sem(f"evac{s}", EVACS, 1) for s in range(2)]
        row_evac = sem("row_evac", ROWS)
        vec_in = sem("vec_in", 16 * 10)
        vec_turned = sem("vec_turned", 1, 1)
        vec_ready = sem("vec_ready", 1)
        rows_used = sem("rows_used", 1, 1)
        squared = sem("squared", 3)
        sum_ready = sem("sum_ready", 3)
        rms_ready = sem("rms_ready", 3)
        u_ready = sem("u_ready", 3)
        silu_ready = sem("silu_ready", 2 * PAIRS_W13)
        h_ready = sem("h_ready", 2 * PAIRS_W13)
        conv_state_in = sem("conv_state_in", 16)
        conv_state_turned = sem("conv_state_turned", 1)
        conv_state_ready = sem("conv_state_ready", 1)
        dt_turned = sem("dt_turned", 1)
        dt_exp_asked = sem("dt_exp_asked", 1)
        dt_exp_ready = sem("dt_exp_ready", 1)
        da_ready = sem("da_ready", 1)
        to_end_product = sem("to_end_product", 1)
        to_end_ready = sem("to_end_ready", 1)
        kv_turned = sem("kv_turned", 9)
        kv_copied = sem("kv_copied", 9)
        kv_out = sem("kv_out", 16 * 6)
        q_diag_ready = sem("q_diag_ready", 1)
        cache_in = [sem(f"cache_in{n}", 16 * 3 * 2 * NB // KV_BUFS) for n in range(KV_BUFS)]
        k_turned = sem("k_turned", NB)
        k_t_ready = sem("k_t_ready", NB)
        v_used = sem("v_used", NB)
        scores_t_ready = sem("scores_t_ready", 1)
        st_ready = sem("st_ready", 1)
        sc_s_product = sem("sc_s_product", 1)
        max_s_ready = sem("max_s_ready", 1)
        exp_s_ready = sem("exp_s_ready", 1)
        p_s_ready = sem("p_s_ready", 1)
        pt_s_turned = sem("pt_s_turned", 1)
        pt_s_ready = sem("pt_s_ready", 1)
        o_s_ready = sem("o_s_ready", 1)
        o_s_copied = sem("o_s_copied", 1)
        sc_p_product = sem("sc_p_product", 8)
        sc_p_read = sem("sc_p_read", 8)
        max_p_ready = sem("max_p_ready", 8)
        exp_p_ready = sem("exp_p_ready", 8)
        p_p_ready = sem("p_p_ready", 8)
        pt_p_turned = sem("pt_p_turned", 8)
        pt_p_ready = sem("pt_p_ready", 8)
        o_p_ready = sem("o_p_ready", 8)
        attn_ready = sem("attn_ready", 1)
        conv_ready = sem("conv_ready", 2 * PAIRS_XBC)
        xbc_ready = sem("xbc_ready", 2 * PAIRS_XBC, 2)
        tails_ready = sem("tails_ready", 1)
        tails_turned = sem("tails_turned", 8)
        tails_copied = sem("tails_copied", 8)
        conv_done_out = sem("conv_done_out", 32)
        ssd_turned = sem("ssd_turned", G)
        b_ready = sem("b_ready", G)
        a_tri_ready = sem("a_tri_ready", G)
        seg_product = sem("seg_product", G)
        dec_ready = sem("dec_ready", G)
        xdt_ready = sem("xdt_ready", G)
        b_diag_ready = sem("b_diag_ready", G)
        m_ready = sem("m_ready", G)
        h_mid_product = sem("h_mid_product", G)
        h_mid_ready = sem("h_mid_ready", G)
        y_product = sem("y_product", G)
        y_read = sem("y_read", G)
        h_end_ready = sem("h_end_ready", G)
        h_end_out = sem("h_end_out", 16 * G)
        h0_in = [sem(f"h0_in{n}", 16 * len(range(n, KI, 3))) for n in range(3)]
        h0_turned = sem("h0_turned", KI)
        h0_t_ready = sem("h0_t_ready", KI)
        h0_product = sem("h0_product", KI)
        h_new_ready = sem("h_new_ready", KI)
        h_new_out = [sem(f"h_new_out{n}", 16 * len(range(n, KI, 3))) for n in range(3)]
        side_first = sem("side_first", SIDE_TILES // 2)
        side_taken = sem("side_taken", SIDE_TILES)
        silu_z_ready = sem("silu_z_ready", G)
        z_used = sem("z_used", G)
        gates_ready = sem("gates_ready", 1)
        y_sq_ready = sem("y_sq_ready", 4)
        y_sum_ready = sem("y_sum_ready", 1)
        y_rms_ready = sem("y_rms_ready", 1)
        y_ready = sem("y_ready", PAIRS_SO)
        merged_ready = sem("merged_ready", 1)
        end_squared = sem("end_squared", 0)
        end_sum = sem("end_sum", 0)
        end_rms = sem("end_rms", 0)
        end_normed = sem("end_normed", 0)
        end_turned = sem("end_turned", 0)
        end_copied = sem("end_copied", 0)
        end_out = sem("end_out", 0)

        block = ctx.enter_context(nc.Block())
        TILE_B, TILE_C = KI, KI + G
        SIDE_BANK = 2

        def wait(eng, signal, layer, n):
            eng.wait_ge(signal.sem, signal.at(layer, n))

        def settle(eng):
            eng.sem_inc(settled.sem, 1)

        @block.sync
        def _(sp):
            def unit(s, m, dst, src):
                sp.wait_ge(lo_ready[s].sem, m + 1)
                settle(sp)
                sp.dma_start(dst, src).then_inc(raw_in[s].sem, 16)

            def columns(w, l, first, n=256):
                return w[bass.ds(l, 1), :, bass.ds(first, n)].rearrange("a (k p) n -> p (a k) n", p=P)

            def panel(m, w, l, first0, first1):
                for s, first in enumerate((first0, first1)):
                    unit(s, m, raw[s][:].rearrange("p (k n) -> p k n", k=KD), columns(w, l, first))

            def rows(m, w, l, row0, kt=2):
                for s in range(2):
                    src = w[bass.ds(l, 1), bass.ds(row0 + s * kt * P, kt * P), :]
                    unit(s, m, raw[s][:, 0:kt * D].rearrange("p (k n) -> p k n", k=kt),
                         src.rearrange("a (k p) n -> p (a k) n", p=P))

            sp.dma_start(square[:], c_square).then_inc(const_in.sem, 16)
            sp.dma_start(x_in[:], x_prompt[0].rearrange("(c p) d -> p c d", p=P)).then_inc(x_in_ready.sem, 16)
            sp.dma_start(xs_in[:], x_sample.rearrange("b t d -> (b t) d")).then_inc(x_in_ready.sem, 16)
            sp.dma_start(small[:], c_small).then_inc(const_in.sem, 16)

            with sp.Fori(0, DEPTH) as l:
                sp.wait_ge(vec_turned.sem, l + 1)
                settle(sp)
                sp.dma_start(vec_a[:], conv_w[bass.ds(l, 1)].rearrange("a i (t c) -> (a i t) c", c=P))\
                    .then_inc(vec_in.sem, 16)
                for row, v in ((V_CONVB, conv_b), (V_F1, ffn1_norm), (V_MIX, mix_norm), (V_F2, ffn2_norm),
                               (V_SSD, ssd_norm)):
                    n = v.shape[1] // P
                    sp.dma_start(vec_b[row:row + n, :], v[bass.ds(l, 1)].rearrange("a (t c) -> (a t) c", c=P))\
                        .then_inc(vec_in.sem, 16)
                sp.dma_start(vec_b[V_FIN:V_FIN + KD, :], final_norm.rearrange("(t c) -> t c", c=P))\
                    .then_inc(vec_in.sem, 16)
                sp.wait_ge(rows_used.sem, l + 1)
                settle(sp)
                for n, v in enumerate((dt_bias, a_log, d_skip)):
                    sp.dma_start(rows3[:, n, :], v[bass.ds(l, 1)].broadcast_to((P, HEADS)))\
                        .then_inc(vec_in.sem, 16)
                m = l * PAIRS
                with sp.Fori(0, PAIRS_W13) as i:
                    panel(m + (M_W13A + i), ffn1_w13, l, i * 256, FF + i * 256)
                with sp.Fori(0, PAIRS_W2 - 1) as i:
                    rows(m + (M_W2A + i), ffn1_w2, l, i * 512)
                rows(m + (M_W2A + PAIRS_W2 - 1), ffn1_w2, l, (PAIRS_W2 - 1) * 512, 1)
                unit(0, m + M_QKV, raw[0][:].rearrange("p (k n) -> p k n", k=KD)[:, :, 0:P], columns(w_in, l, C_DT, P))
                unit(1, m + M_QKV, raw[1][:].rearrange("p (k n) -> p k n", k=KD), columns(w_in, l, C_Q))
                panel(m + (M_QKV + 1), w_in, l, C_Q + 256, C_Q + 512)
                sp.wait_ge(lines_out.sem, 16)
                wait(sp, row_evac, l, R_W2A + 4)
                settle(sp)
                sp.dma_start(conv_in[:], state_conv[bass.ds(l, 1)].rearrange("a b i c -> (a b i) c"))\
                    .then_inc(conv_state_in.sem, 16)
                panel(m + (M_QKV + 2), w_in, l, C_Q + 768, C_Q + 1024)

                def cache(n):
                    b, kv = n % NB, n // NB
                    if n == 0:
                        wait(sp, u_ready, l, 2)
                    elif KV_BUFS <= n < KV_BUFS + NB:
                        wait(sp, k_turned, l, n - KV_BUFS + 1)
                    elif n >= KV_BUFS + NB:
                        wait(sp, v_used, l, n - KV_BUFS - NB + 1)
                    settle(sp)
                    buf, s = kv_in[n % KV_BUFS], cache_in[n % KV_BUFS].sem
                    sp.dma_start(buf[:, 0, :], cache_kv_w128[bass.ds(l, 1), b, :, kv]
                                 .rearrange("a p h e -> (a p) (h e)")).then_inc(s, 16)
                    sp.dma_start(buf[:, 1:3, :], cache_kv_w512[bass.ds(l, 1), b, :, kv]
                                 .rearrange("a (t p) h e -> p (a t) (h e)", p=P)).then_inc(s, 16)
                    sp.dma_start(buf[0:64, 3, :], cache_kv_w2048[bass.ds(l, 1), b, :, kv]
                                 .rearrange("a (m r) h e -> (a m) r (h e)", r=16)[:, 0:NT])\
                        .then_inc(s, 16)

                for n in range(KV_BUFS):
                    cache(n)
                with sp.Fori(3, PAIRS_QKV) as i:
                    panel(m + (M_QKV + i), w_in, l, C_Q - 256 + i * 512, C_Q + i * 512)
                for i in range(2):
                    panel(m + (M_XBC + i), w_in, l, C_XBC + i * 512, C_XBC + 256 + i * 512)
                for n in range(KV_BUFS, 2 * NB):
                    cache(n)
                with sp.Fori(2, PAIRS_XBC) as i:
                    panel(m + (M_XBC + i), w_in, l, C_XBC + i * 512, C_XBC + 256 + i * 512)

                def side(n):
                    gate, j = side_unit(n)
                    unit(n % 2, m + (M_SIDE + n // 2), raw[n % 2][:].rearrange("p (k n) -> p k n", k=KD),
                         columns(w_in, l, (C_G if gate else C_Z) + 256 * j))

                def states(t):
                    if t >= 3:
                        wait(sp, h_new_out[t % 3], l, 16 * (t // 3))
                    settle(sp)
                    src = state_ssm[bass.ds(l, 1), :, 2 * t:2 * t + 2].rearrange("a b h p n -> (a h p) b n")
                    sp.dma_start(h0[t % 3][:], src).then_inc(h0_in[t % 3].sem, 16)

                for n in range(4):
                    side(n)
                wait(sp, tails_turned, l, 8)
                wait(sp, xbc_ready, l, 2 * PAIRS_XBC)
                for t in range(3):
                    states(t)
                for g in range(G):
                    for t in range(2 * g + 3, min(2 * g + 5, KI)):
                        states(t)
                    for n in range(3 * g // 2 + 4, (3 * g + 3) // 2 + 4):
                        if n < 2 * PAIRS_SIDE:
                            side(n)
                        else:
                            j = n - 2 * PAIRS_SIDE + G // 2
                            unit(n % 2, m + (M_SIDE + n // 2), raw[n % 2][:].rearrange("p (k n) -> p k n", k=KD),
                                 columns(w_in, l, C_G + 256 * j))
                with sp.Fori(0, PAIRS_SO) as i:
                    rows(m + (M_SO + i), w_ssd_out, l, i * 512)
                rows(m + M_AO, w_attn_out, l, 0, 1)
                with sp.Fori(0, PAIRS_WO) as i:
                    rows(m + (M_WO + i), w_o, l, i * 512)
                with sp.Fori(0, PAIRS_W13) as i:
                    panel(m + (M_W13B + i), ffn2_w13, l, i * 256, FF + i * 256)
                with sp.Fori(0, PAIRS_W2 - 1) as i:
                    rows(m + (M_W2B + i), ffn2_w2, l, i * 512)
                rows(m + (M_W2B + PAIRS_W2 - 1), ffn2_w2, l, (PAIRS_W2 - 1) * 512, 1)
            for s in range(2):
                unit(s, DEPTH * PAIRS, raw[s][:, 0:8], w_o[0, 0:P, 0:8])
            sp.wait_ge(end_copied.sem, 2)
            sp.dma_start(y_prompt[0].rearrange("(c p) d -> p c d", p=P), y_out[:]).then_inc(end_out.sem, 16)
            sp.dma_start(y_sample.rearrange("b t d -> (b t) d"), y_out_s[:]).then_inc(end_out.sem, 16)
            sp.wait_ge(end_out.sem, 32)
            for s in range(2):
                sp.wait_ge(raw_in[s].sem, 16 * (DEPTH * PAIRS + 1))

        @block.scalar
        def _(act):
            def high(m):
                for s in range(2):
                    high_unit(s, m)

            def high_unit(s, m):
                act.wait_ge(raw_in[s].sem, m * 16 + 16)
                act.wait_ge(unit_done[s].sem, m + 1)
                act.activation(w_hi[s][:], raw[s][:], ACT.Copy).then_inc(hi_ready[s].sem, 1)

            def norm(l, n, ready, count):
                wait(act, ready, l, count)
                act.activation(full[:], x[:], ACT.Square).then_inc(squared.sem, 1)
                wait(act, sum_ready, l, n)
                act.activation(rms[:], ps[:, 4, 0:T], ACT.Sqrt, bias=eps[:], scale=1.0 / D)\
                    .then_inc(rms_ready.sem, 1)

            def swiglu(l, m0, e0, n0):
                def body(i):
                    high_unit(0, l * PAIRS + (m0 + 1 + i))
                    act.wait_ge(unit_done[0].sem, l * PAIRS + (m0 + 2 + i))
                    act.wait_ge(evac[1].sem, l * EVACS + (e0 + 1 + i))
                    act.activation(silu_a[:], ps[:, 0:2, 0:T], ACT.Silu).then_inc(evac[0].sem, 1)
                    high_unit(1, l * PAIRS + (m0 + 1 + i))
                with act.Fori(0, PAIRS_W13) as i:
                    body(i)
                with act.Fori(0, PAIRS_W2) as i:
                    high(l * PAIRS + (M_W2A - M_W13A + m0 + 1 + i))

            for dst, src in ((delta[:], c_delta.rearrange("p (b i q) -> p b i q", b=NB, i=HPG)), (hot[:], c_hot),
                             (line_hot[:], c_line), (line_mask[:], c_line_mask), (mask[:], c_mask)):
                act.dma_start(dst, src).then_inc(start_in.sem, 16)
            for q in range(NT):
                act.dma_start(rel4[32 * q:32 * q + 32, :], rel_bias).then_inc(start_in.sem, 16)
            act.wait_ge(zeroed.sem, 1)
            high(0)
            with act.Fori(0, DEPTH) as l:
                m = l * PAIRS
                act.wait_ge(x_first.sem, 4)
                act.wait_ge(row_evac.sem, l * ROWS)
                act.activation(full[:], x[:], ACT.Square).then_inc(squared.sem, 1)
                wait(act, sum_ready, l, 1)
                act.activation(rms[:], ps[:, 4, 0:T], ACT.Sqrt, bias=eps[:], scale=1.0 / D)\
                    .then_inc(rms_ready.sem, 1)
                swiglu(l, M_W13A, E_W13A, 0)
                norm(l, 2, row_evac, R_W2A + 4)

                high_unit(0, m + (M_QKV + 1))
                act.wait_ge(unit_done[0].sem, m + (M_QKV + 2))
                act.activation(dt_fm[:], ps[0:HEADS, 0, 0:T], ACT.Copy).then_inc(evac[0].sem, 1)
                high_unit(1, m + (M_QKV + 1))
                act.wait_ge(unit_done[1].sem, m + (M_QKV + 2))
                act.activation(qkv[:, 0:2, :], ps[:, 2:4, 0:T], ACT.Copy).then_inc(evac[1].sem, 1)
                with act.Fori(1, PAIRS_QKV) as i:
                    for s in range(2):
                        high_unit(s, m + (M_QKV + 1 + i))
                        act.wait_ge(unit_done[s].sem, m + (M_QKV + 2 + i))
                        act.activation(qkv[:, bass.ds(i * 4 + (2 * s - 2), 2), :], ps[:, 2 * s:2 * s + 2, 0:T],
                                       ACT.Copy).then_inc(evac[s].sem, 1)
                wait(act, dt_exp_asked, l, 1)
                act.activation(dt_w[0][:], dt_w[1][:], ACT.Exp)
                act.activation(a_head[:], rows3[:, 1, :], ACT.Exp).then_inc(dt_exp_ready.sem, 1)
                wait(act, to_end_product, l, 1)
                act.activation(to_end[:, 0:3, :], ps[:, 4, 128:224].rearrange("p (c h) -> p c h", c=3), ACT.Exp)
                act.activation(to_end[0:TS, 3, :], ps[0:TS, 4, 224:256], ACT.Exp).then_inc(to_end_ready.sem, 1)

                for b in range(NB):
                    wait(act, k_turned, l, b + 1)
                    act.activation(k_t[b % 2][:, 0, :], ps[:, 4 + 2 * (b % 2), 0:OLD], ACT.Copy)
                    act.activation(k_t[b % 2][:, 1, :], ps[:, 5 + 2 * (b % 2), 0:OLD], ACT.Copy)\
                        .then_inc(k_t_ready.sem, 1)
                wait(act, scores_t_ready, l, 1)
                act.activation(st[:, 0:3, :], ps[:, 0, 0:3 * P].rearrange("p (k c) -> p k c", k=3), ACT.Copy)
                act.activation(st[0:64, 3, :], ps[0:64, 0, 3 * P:4 * P], ACT.Copy)
                act.activation(st_new[:], ps[0:TS, 1, 0:3 * P].rearrange("p (k c) -> p k c", k=3), ACT.Copy)\
                    .then_inc(st_ready.sem, 1)
                wait(act, max_s_ready, l, 1)
                act.activation(sc_s[:], sc_s[:], ACT.Exp, bias=stat_s[0][:], accum_out=stat_s[1][:])\
                    .then_inc(exp_s_ready.sem, 1)
                wait(act, pt_s_turned, l, 1)
                act.activation(st[:, 0:3, :], ps[:, 4, 0:3 * P].rearrange("p (k c) -> p k c", k=3), ACT.Copy)
                act.activation(st[0:64, 3, :], ps[0:64, 4, 3 * P:4 * P], ACT.Copy)
                act.activation(st_new[:], ps[0:TS, 5, 0:3 * P].rearrange("p (k c) -> p k c", k=3), ACT.Copy)\
                    .then_inc(pt_s_ready.sem, 1)

                for n in range(2 * HPG):
                    k = n % 2 + 1
                    wait(act, max_p_ready, l, n + 1)
                    act.activation(sc_p[n % 2][:, :, 0:k * P], sc_p[n % 2][:, :, 0:k * P], ACT.Exp,
                                   bias=stat_p[n % 2][0][:], accum_out=stat_p[n % 2][1][:])\
                        .then_inc(exp_p_ready.sem, 1)
                    wait(act, pt_p_turned, l, n + 1)
                    src = ps[:, 4:6, 0:NG * P].rearrange("p k (g c) -> p k g c", g=NG)
                    act.activation(pt_p[n % 2][:, :, 0:k, :].rearrange("p g k c -> p k g c"), src[:, 0:k],
                                   ACT.Copy).then_inc(pt_p_ready.sem, 1)

                with act.Fori(0, PAIRS_XBC) as i:
                    for s in range(2):
                        high_unit(s, m + (M_XBC + 1 + i))
                        tile = i * 4 + 2 * s
                        act.wait_ge(unit_done[s].sem, m + (M_XBC + 2 + i))
                        act.activation(flat[:, bass.ds(tile, 2), SEQ0:PADDED].rearrange("p t (b c) -> p t b c", c=RUN)
                                       [:, :, :, CW - 1:], ps[:, 2 * s:2 * s + 2, TP:T]
                                       .rearrange("p t (b c) -> p t b c", c=NT), ACT.Copy)
                        act.activation(flat[:, bass.ds(tile, 2), CW - 1:SEQ0], ps[:, 2 * s:2 * s + 2, 0:TP],
                                       ACT.Copy).then_inc(evac[s].sem, 1)
                        act.wait_ge(conv_ready.sem, l * 2 * PAIRS_XBC + i * 2 + (s + 1))
                        act.activation(flat[:, bass.ds(tile, 2), 0:TP], acc[s][:, :, 0:TP], ACT.Silu)
                        act.activation(flat[:, bass.ds(tile, 2), TP:T].rearrange("p t (b c) -> p t b c", c=NT),
                                       acc[s][:, :, SEQ0:PADDED].rearrange("p t (b c) -> p t b c", c=RUN)
                                       [:, :, :, 0:NT], ACT.Silu).then_inc(xbc_ready.sem, 1)
                for n in range(8):
                    wait(act, tails_turned, l, n + 1)
                    act.activation(conv_out[:, n * 512:(n + 1) * 512], ps[0:27, n, :], ACT.Copy)\
                        .then_inc(tails_copied.sem, 1)

                def side(q):
                    n, half = q // 2, q % 2
                    gate, j = side_unit(n)
                    if half:
                        act.wait_ge(unit_done[n % 2].sem, m + (M_SIDE + n // 2 + 2))
                    else:
                        wait(act, side_first, l, n + 1)
                    if not gate and not half and j:
                        wait(act, z_used, l, j)
                    dst = gates[:, 2 * j + half, :] if gate else silu_z[:, half, :]
                    act.activation(dst, ps[:, SIDE_BANK, 0:T], ACT.Copy).then_inc(side_taken.sem, 1)
                    if half and not gate:
                        act.drain()
                        act.activation(silu_z[:], silu_z[:], ACT.Silu).then_inc(silu_z_ready.sem, 1)
                    if half:
                        high_unit(n % 2, m + (M_SIDE + n // 2 + 1))

                wait(act, kv_out, l, 16 * 6)
                for g in range(G):
                    wait(act, ssd_turned, l, g + 1)
                    for c in range(2):
                        act.activation(b_tm[:, c, :], ps[:, 7, c * P:(c + 1) * P], ACT.Copy)
                    act.activation(b_tm_s[:], ps[0:TS, 7, 256:384], ACT.Copy).then_inc(b_ready.sem, 1)
                    wait(act, seg_product, l, g + 1)
                    for c in range(2):
                        act.activation(dec[c][:], ps[:, 4 + c, :].rearrange("p (h c) -> p h c", h=HPG), ACT.Exp)
                    act.activation(dec_s[:], ps[0:TS, 6, 336:464].rearrange("p (h c) -> p h c", h=HPG), ACT.Exp)
                    act.activation(e_off[:], ps[:, 6, 0:256].rearrange("p (t c) -> p t c", t=2), ACT.Exp)
                    act.activation(e_s[:], ps[:, 6, 256:336].rearrange("p (t c) -> p t c", t=2), ACT.Exp)\
                        .then_inc(dec_ready.sem, 1)
                    wait(act, h_mid_product, l, g + 1)
                    act.activation(h_mid[:], ps[:, 7, 0:256], ACT.Copy).then_inc(h_mid_ready.sem, 1)
                    side(3 * g)
                    wait(act, y_product, l, g + 1)
                    if g:
                        wait(act, h_end_out, l, 16 * g)
                    act.activation(h_end[:], ps[:, 7, 256:512].rearrange("p (t n) -> p t n", t=2), ACT.Copy)\
                        .then_inc(h_end_ready.sem, 1)
                    for t in (2 * g, 2 * g + 1):
                        wait(act, h0_turned, l, t + 1)
                        act.activation(h0_t[:], ps[:, 4:6, :].rearrange("p k (b c) -> p (k b) c", c=P), ACT.Copy)\
                            .then_inc(h0_t_ready.sem, 1)
                    side(3 * g + 1)
                    side(3 * g + 2)

                wait(act, z_used, l, G)
                for n in (3, 2, 1, 0):
                    if n == 1:
                        for j in range(3):
                            wait(act, h_new_out[j], l, h_new_out[j].per)
                    act.activation(y_sq[:, 4 * n:4 * n + 4, :], flat[:, 4 * n:4 * n + 4, 0:T], ACT.Square)\
                        .then_inc(y_sq_ready.sem, 1)

                def gate_pair(i):
                    for s in range(2):
                        high_unit(s, m + (M_G + 1 + i))
                        act.wait_ge(unit_done[s].sem, m + (M_G + 2 + i))
                        tile = KD + i * 4 + 2 * s
                        act.activation(gates[:, tile:tile + 2, :], ps[:, 2 * s:2 * s + 2, 0:T], ACT.Sigmoid)\
                            .then_inc(evac[s].sem, 1)

                gate_pair(0)
                wait(act, y_sum_ready, l, 1)
                act.activation(y_rms[:], ps[:, :, 0:T], ACT.Sqrt, bias=eps[:], scale=1.0 / 256)\
                    .then_inc(y_rms_ready.sem, 1)
                gate_pair(1)
                act.activation(gates[:, 0:KD, :], gates[:, 0:KD, :], ACT.Sigmoid).then_inc(gates_ready.sem, 1)
                with act.Fori(0, PAIRS_SO + PAIRS_AO + PAIRS_WO) as i:
                    high(m + (M_SO + 1 + i))
                norm(l, 3, row_evac, R_WO + 4)
                swiglu(l, M_W13B, E_W13B, PAIRS_W13)

            act.wait_ge(row_evac.sem, DEPTH * ROWS)
            act.activation(full[:], x[:], ACT.Square).then_inc(end_squared.sem, 1)
            act.wait_ge(end_sum.sem, 1)
            act.activation(rms[:], ps[:, 4, 0:T], ACT.Sqrt, bias=eps[:], scale=1.0 / D).then_inc(end_rms.sem, 1)
            act.wait_ge(end_turned.sem, 1)
            for c in range(2):
                last = act.activation(y_out[:, c, :].rearrange("p (k c) -> p k c", k=2),
                                      ps[:, 2 * c:2 * c + 2, :], ACT.Copy)
            last.then_inc(end_copied.sem, 1)

        @block.vector
        def _(dve):
            def low_unit(s, m):
                dve.wait_ge(hi_ready[s].sem, m + 1)
                dve.tensor_tensor(w_lo[s][:], raw[s][:], w_hi[s][:].bitcast(F32), ALU.subtract)\
                    .then_inc(lo_ready[s].sem, 1)

            def low(m):
                for s in range(2):
                    low_unit(s, m)

            def split(hi, lo, src):
                dve.drain()
                dve.tensor_copy(hi, src)
                dve.drain()
                return dve.tensor_tensor(lo, src, hi.bitcast(F32), ALU.subtract)

            def normed(gain):
                dve.reciprocal(rinv[:], rms[:])
                dve.drain()
                for k in range(KD):
                    dve.scalar_tensor_tensor(out=full[:, k, :], in0=x[:, k, :], scalar=vecs[:, gain + k:gain + k + 1],
                                             in1=rinv[:], op0=ALU.mult, op1=ALU.mult)

            def norm(l, n, gain):
                wait(dve, rms_ready, l, n)
                normed(gain)
                split(u_hi[:], u_lo[:], full[:]).then_inc(u_ready.sem, 1)

            def swiglu(l, m0, e0, n0):
                with dve.Fori(0, PAIRS_W13) as i:
                    low(l * PAIRS + (m0 + 1 + i))
                    dve.drain()
                    dve.wait_ge(evac[0].sem, l * EVACS + (e0 + 2 + i))
                    dve.wait_ge(unit_done[1].sem, l * PAIRS + (m0 + 2 + i))
                    dve.tensor_tensor(hidden[:], silu_a[:], ps[:, 2:4, 0:T], ALU.mult).then_inc(evac[1].sem, 1)
                    split(h_hi[:, bass.ds(i * 2, 2), :], h_lo[:, bass.ds(i * 2, 2), :], hidden[:])\
                        .then_inc(h_ready.sem, 1)
                with dve.Fori(0, PAIRS_W2) as i:
                    low(l * PAIRS + (m0 + PAIRS_W13 + 1 + i))
                add_to_x(l, m0 + PAIRS_W13 + PAIRS_W2, 0.5)

            def add_to_x(l, m_end, factor):
                wait(dve, unit_done[1], l, m_end)
                for o in range(0, KD, 2):
                    dve.scalar_tensor_tensor(out=x[:, o:o + 2, :], in0=ps[:, o:o + 2, 0:T], scalar=factor,
                                             in1=x[:, o:o + 2, :], op0=ALU.mult, op1=ALU.add)\
                        .then_inc(row_evac.sem, 1)

            dve.memset(eps[:], EPS)
            dve.memset(q_diag[:], 0.0)
            dve.memset(dt_raw[:], 0.0)
            dve.memset(to_end[:], 0.0)
            dve.drain().then_inc(zeroed.sem, 1)
            for o in range(0, KD, 2):
                dve.wait_ge(x_turned.sem, o // 2 + 1)
                dve.tensor_copy(x[:, o:o + 2, :], ps[:, o:o + 2, 0:T]).then_inc(x_first.sem, 1)
            dve.wait_ge(bias_product.sem, 1)
            dve.tensor_tensor(bias_s[:, 0:OLD], ps[:, 0, 0:OLD], mask[:, 0:OLD], ALU.add)
            dve.tensor_tensor(bias_s[:, OLD:], ps[:, 1, 0:NEW], mask[:, OLD:], ALU.add)
            dve.tensor_tensor(lines[:, 0:2], ps[0:HPG, 2:4, 0:W_LINE], line_mask[:, 0:2], ALU.add)
            dve.tensor_tensor(lines[:, 2], ps[0:HPG, 7, 0:W_LINE], line_mask[:, 2], ALU.add)\
                .then_inc(lines_ready.sem, 1)

            with dve.Fori(0, DEPTH) as l:
                m = l * PAIRS
                wait(dve, vec_turned, l, 1)
                dve.tensor_copy(conv_wt[:], ps[:, 5, 0:P])
                dve.tensor_copy(vecs[:], ps[:, 6, 0:80]).then_inc(vec_ready.sem, 1)
                dve.drain()
                norm(l, 1, V_F1)
                swiglu(l, M_W13A, E_W13A, 0)
                norm(l, 2, V_MIX)
                with dve.Fori(0, PAIRS_QKV) as i:
                    low(m + (M_QKV + 1 + i))

                wait(dve, vec_in, l, 160)
                wait(dve, dt_turned, l, 1)
                bias3 = rows3[:, 0, :].unsqueeze(1).broadcast_to((P, 3, HEADS))
                dve.tensor_copy(dt_raw[:, 0:2, :], ps[:, 4, 0:2 * HEADS].rearrange("p (c h) -> p c h", c=2))
                dve.tensor_copy(dt_raw[0:TS, 2, :], ps[0:TS, 4, 2 * HEADS:3 * HEADS])
                for half in range(2):
                    h = slice(64 * half, 64 * half + 64)
                    dve.tensor_copy(skip[h, :], rows3[h, 2, half::2])
                dve.drain()
                dve.tensor_tensor(dt_w[2][:], dt_raw[:], bias3, ALU.add)
                dve.drain()
                dve.scalar_tensor_tensor(out=dt_w[1][:], in0=dt_w[2][:], scalar=-1.0, in1=dt_w[2][:],
                                         op0=ALU.mult, op1=ALU.min).then_inc(dt_exp_asked.sem, 1)
                wait(dve, dt_exp_ready, l, 1)
                y_, z_, z2 = dt_w[0], dt_w[1], dt
                dve.tensor_scalar(z_[:], y_[:], 2.0, None, ALU.add)
                dve.drain()
                dve.reciprocal(z_[:], z_[:])
                dve.drain()
                dve.tensor_tensor(z_[:], z_[:], y_[:], ALU.mult)
                dve.drain()
                dve.tensor_tensor(z2[:], z_[:], z_[:], ALU.mult)
                dve.drain()
                dve.tensor_scalar(y_[:], z2[:], 1.0 / 17, None, ALU.mult)
                for odd in (15, 13, 11, 9, 7, 5, 3):
                    dve.drain()
                    dve.scalar_tensor_tensor(out=y_[:], in0=y_[:], scalar=1.0 / odd, in1=z2[:],
                                             op0=ALU.add, op1=ALU.mult)
                dve.drain()
                dve.scalar_tensor_tensor(out=y_[:], in0=y_[:], scalar=1.0, in1=z_[:], op0=ALU.add, op1=ALU.mult)
                dve.tensor_scalar(dt_w[2][:], dt_w[2][:], 0.0, None, ALU.max)
                dve.drain()
                dve.scalar_tensor_tensor(out=dt[:], in0=y_[:], scalar=2.0, in1=dt_w[2][:], op0=ALU.mult, op1=ALU.add)
                dve.drain()
                dve.scalar_tensor_tensor(out=da[:], in0=dt[:], scalar=-1.0,
                                         in1=a_head[:].unsqueeze(1).broadcast_to((P, 3, HEADS)),
                                         op0=ALU.mult, op1=ALU.mult).then_inc(da_ready.sem, 1)

                for half in range(2):
                    h = slice(64 * half, 64 * half + 64)
                    last = dve.tensor_copy(q_diag[h, :, :, NT * half:NT * half + NT],
                                           qkv[h, 0:6, TP:T].rearrange("p t (b q) -> p t b q", q=NT))
                last.then_inc(q_diag_ready.sem, 1)
                wait(dve, conv_state_turned, l, 1)
                dve.memset(flat[:, :, 0:CW - 1], 0.0)
                for t in range(0, KC, 16):
                    last = dve.tensor_copy(flat[:, t:t + 16, SEQ0:PADDED].rearrange("p t (b c) -> p t b c", c=RUN)
                                           [:, :, :, 0:CW - 1],
                                           ps[:, t // 16, 0:16 * 24].rearrange("p (t b c) -> p t b c", b=NB, c=CW - 1))
                last.then_inc(conv_state_ready.sem, 1)
                for n in range(9):
                    wait(dve, kv_turned, l, n + 1)
                    g, c = n // 3, n % 3
                    if c < 2:
                        dst, src = kv_p[:, c, g], ps[:, n % 4, :]
                    else:
                        dst, src = kv_s[:, g], ps[0:TS, n % 4, :]
                    dve.tensor_copy(dst, src.rearrange("p (k e) -> p k e", k=2)).then_inc(kv_copied.sem, 1)

                wait(dve, sc_s_product, l, 1)
                dve.scalar_tensor_tensor(out=sc_s[:, 0:OLD], in0=ps[:, 2, 0:OLD], scalar=SCALE, in1=bias_s[:, 0:OLD],
                                         op0=ALU.mult, op1=ALU.add)
                dve.scalar_tensor_tensor(out=sc_s[:, OLD:], in0=ps[:, 3, 0:NEW], scalar=SCALE, in1=bias_s[:, OLD:],
                                         op0=ALU.mult, op1=ALU.add)
                dve.drain()
                dve.tensor_reduce(stat_s[2][:], sc_s[:], AX.X, ALU.max)
                dve.drain()
                dve.tensor_scalar(stat_s[0][:], stat_s[2][:], -1.0, None, ALU.mult).then_inc(max_s_ready.sem, 1)
                wait(dve, exp_s_ready, l, 1)
                dve.reciprocal(stat_s[2][:], stat_s[1][:])
                dve.drain()
                dve.tensor_scalar(sc_s[:], sc_s[:], stat_s[2][:], None, ALU.mult).then_inc(p_s_ready.sem, 1)
                wait(dve, o_s_ready, l, 1)
                for pair in range(2):
                    for half in range(2):
                        h = slice(64 * half, 64 * half + 64)
                        src = ps[h, 6 + pair, 0:64].rearrange("p (b c) -> p b c", b=NB)
                        last = dve.tensor_copy(attn[h, pair, TP:T].rearrange("p (b q) -> p b q", q=NT),
                                               src[:, :, NT * half:NT * half + NT])
                last.then_inc(o_s_copied.sem, 1)

                wait(dve, bias_in, 0, 16 * 12)

                def scores(n):
                    i, c, k = n // 2, n % 2, n % 2 + 1
                    bias = bias_p[:].rearrange("p (g i) c -> p g i c", g=NG)[:, :, i, (1 - c) * P:]
                    banks = 2 * (n % 2)
                    wait(dve, sc_p_product, l, n + 1)
                    dve.scalar_tensor_tensor(out=sc_p[n % 2][:, 0:2, 0:k * P],
                                             in0=ps[:, banks, :].rearrange("p (g c) -> p g c", g=2)[:, :, 0:k * P],
                                             scalar=SCALE, in1=bias[:, 0:2], op0=ALU.mult, op1=ALU.add)
                    dve.scalar_tensor_tensor(out=sc_p[n % 2][:, 2, 0:k * P], in0=ps[:, banks + 1, 0:k * P],
                                             scalar=SCALE, in1=bias[:, 2], op0=ALU.mult, op1=ALU.add)\
                        .then_inc(sc_p_read.sem, 1)
                    dve.drain()
                    dve.tensor_reduce(stat_p[n % 2][2][:], sc_p[n % 2][:, :, 0:k * P], AX.XY, ALU.max)
                    dve.drain()
                    dve.tensor_scalar(stat_p[n % 2][0][:], stat_p[n % 2][2][:], -1.0, None, ALU.mult)\
                        .then_inc(max_p_ready.sem, 1)

                def weights(n):
                    k = n % 2 + 1
                    wait(dve, exp_p_ready, l, n + 1)
                    dve.reciprocal(stat_p[n % 2][2][:], stat_p[n % 2][1][:])
                    dve.drain()
                    dve.tensor_scalar(sc_p[n % 2][:, :, 0:k * P], sc_p[n % 2][:, :, 0:k * P], stat_p[n % 2][2][:], None,
                                      ALU.mult).then_inc(p_p_ready.sem, 1)

                def outputs(n):
                    i, c = n // 2, n % 2
                    h = slice(64 * (i % 2), 64 * (i % 2) + 64)
                    wait(dve, o_p_ready, l, n + 1)
                    return dve.tensor_copy(attn[h, i // 2, c * P:(c + 1) * P], ps[h, 6 + n % 2, 0:P])

                scores(0)
                for n in range(2 * HPG):
                    weights(n)
                    if n + 1 < 2 * HPG:
                        if n >= 1:
                            wait(dve, pt_p_turned, l, n)
                        scores(n + 1)
                    if n >= 1:
                        outputs(n - 1)
                outputs(2 * HPG - 1)
                split(ao_hi[:], ao_lo[:], attn[:]).then_inc(attn_ready.sem, 1)

                with dve.Fori(0, PAIRS_XBC) as i:
                    for s in range(2):
                        tile = i * 4 + 2 * s
                        dve.wait_ge(evac[s].sem, l * EVACS + (E_XBC + 2 + i))
                        dve.wait_ge(xbc_ready.sem, l * 2 * PAIRS_XBC + i * 2 + (s + 1))
                        dve.tensor_copy(tails[:, bass.ds(tile, 2)],
                                        flat[:, bass.ds(tile, 2), TP:TP + 9 * RUN]
                                        .rearrange("p t (j c) -> p t j c", c=RUN)[:, :, :, 0:CW - 1])
                        for w in range(CW):
                            for t in range(2):
                                src = flat[:, bass.ds(tile + t, 1), w:w + CONVED].rearrange("p t c -> p (t c)")
                                dst = acc[s][:, t, 0:CONVED]
                                tap = conv_wt[:, bass.ds(tile + (w * KC + t), 1)]
                                if w == 0:
                                    dve.tensor_scalar(dst, src, tap, vecs[:, bass.ds(tile + (V_CONVB + t), 1)],
                                                      ALU.mult, ALU.add)
                                else:
                                    last = dve.scalar_tensor_tensor(out=dst, in0=src, scalar=tap, in1=dst,
                                                                    op0=ALU.mult, op1=ALU.add)
                            if w < CW - 1:
                                dve.drain()
                        last.then_inc(conv_ready.sem, 1)
                dve.drain().then_inc(tails_ready.sem, 1)

                wait(dve, to_end_ready, l, 1)
                wait(dve, kv_out, l, 16 * 6)

                def times_z(g):
                    wait(dve, silu_z_ready, l, g + 1)
                    rows_y = flat[:, 2 * g:2 * g + 2, 0:T]
                    dve.tensor_tensor(rows_y, rows_y, silu_z[:], ALU.mult).then_inc(z_used.sem, 1)

                for g in range(G):
                    heads = slice(HPG * g, HPG * g + HPG)
                    if g:
                        wait(dve, seg_product, l, g)
                    for c in range(2):
                        for h in range(HPG):
                            dve.tensor_scalar(a_tri[c][:, h, :], tri, da[:, c, HPG * g + h:HPG * g + h + 1], None,
                                              ALU.mult)
                    for h in range(HPG):
                        dve.tensor_scalar(a_tri_s[:, h, :], tri_s, da[0:TS, 2, HPG * g + h:HPG * g + h + 1], None,
                                          ALU.mult)
                    dve.tensor_copy(a_exp[:].rearrange("p (h e) -> p h e", h=HPG),
                                    da[:, 1, heads].unsqueeze(2).broadcast_to((P, HPG, HD)))
                    dve.tensor_copy(a_exp_s[:].rearrange("p (h e) -> p h e", h=HPG),
                                    da[0:TS, 2, heads].unsqueeze(2).broadcast_to((TS, HPG, HD)))\
                        .then_inc(a_tri_ready.sem, 1)
                    wait(dve, ssd_turned, l, g + 1)
                    if g:
                        wait(dve, h0_product, l, 2 * g)
                    for c in range(2):
                        dve.tensor_tensor(xdt[:, c, :].rearrange("p (h e) -> p h e", h=HPG),
                                          ps[:, c, 0:256].rearrange("p (h e) -> p h e", h=HPG),
                                          dt[:, c, heads].unsqueeze(2).broadcast_to((P, HPG, HD)), ALU.mult)
                        dve.tensor_tensor(cbm[:, c, :], ps[:, 3, c * P:(c + 1) * P], tri, ALU.mult)
                    dve.tensor_tensor(xdt_s[:].rearrange("p (h e) -> p h e", h=HPG),
                                      ps[0:TS, 1, 256:512].rearrange("p (h e) -> p h e", h=HPG),
                                      dt[0:TS, 2, heads].unsqueeze(2).broadcast_to((TS, HPG, HD)), ALU.mult)
                    dve.tensor_tensor(cbm_s[:], ps[0:TS, 3, 256:256 + TS], tri_s, ALU.mult)
                    dve.drain()
                    for n, c in ((0, 0), (1, 1), (2, 0)):
                        dve.tensor_tensor(xdte[:, n, :].rearrange("p (h e) -> p h e", h=HPG),
                                          xdt[:, c, :].rearrange("p (h e) -> p h e", h=HPG),
                                          to_end[:, n, heads].unsqueeze(2).broadcast_to((P, HPG, HD)), ALU.mult)
                    dve.tensor_tensor(xdte_s[:].rearrange("p (h e) -> p h e", h=HPG),
                                      xdt_s[:].rearrange("p (h e) -> p h e", h=HPG),
                                      to_end[0:TS, 3, heads].unsqueeze(2).broadcast_to((TS, HPG, HD)), ALU.mult)\
                        .then_inc(xdt_ready.sem, 1)
                    if g:
                        times_z(g - 1)
                    wait(dve, b_ready, l, g + 1)
                    dve.tensor_tensor(b_diag[:], b_tm_s[:].unsqueeze(1).broadcast_to((TS, NB, NS)),
                                      sel_s.unsqueeze(2).broadcast_to((TS, NB, NS)), ALU.mult)\
                        .then_inc(b_diag_ready.sem, 1)
                    wait(dve, dec_ready, l, g + 1)
                    for c in range(2):
                        dve.tensor_tensor(dec[c][:], dec[c][:], cbm[:, c, :].unsqueeze(1).broadcast_to((P, HPG, P)),
                                          ALU.mult)
                    dve.tensor_tensor(dec_s[:], dec_s[:], cbm_s[:].unsqueeze(1).broadcast_to((TS, HPG, TS)), ALU.mult)\
                        .then_inc(m_ready.sem, 1)
                    wait(dve, y_product, l, g + 1)
                    off = ps[:, 1, 0:256].rearrange("p (t c) -> p t c", t=2)
                    dve.tensor_tensor(off_t[:], off, e_off[:], ALU.mult)
                    dve.drain()
                    dve.tensor_tensor(off_t[:], off_t[:], ps[:, 0, 256:512].rearrange("p (t c) -> p t c", t=2), ALU.add)
                    dve.drain()
                    for t in range(2):
                        tile = 2 * g + t
                        d_t = skip[:, tile:tile + 1]
                        dve.scalar_tensor_tensor(out=flat[:, tile, 0:P], in0=flat[:, tile, 0:P], scalar=d_t,
                                                 in1=ps[:, 0, t * P:(t + 1) * P], op0=ALU.mult, op1=ALU.add)
                        dve.scalar_tensor_tensor(out=flat[:, tile, P:TP], in0=flat[:, tile, P:TP], scalar=d_t,
                                                 in1=off_t[:, t, :], op0=ALU.mult, op1=ALU.add)
                    for t in range(2):
                        tile = 2 * g + t
                        wait(dve, h0_product, l, tile + 1)
                        for b in range(NB):
                            dve.scalar_tensor_tensor(out=h0[tile % 3][:, b, :], in0=h0[tile % 3][:, b, :],
                                                     scalar=e_s[:, t, TS + b:TS + b + 1],
                                                     in1=ps[:, 6 + b // 4, (b % 4) * NS:(b % 4 + 1) * NS],
                                                     op0=ALU.mult, op1=ALU.add)
                        dve.drain().then_inc(h_new_ready.sem, 1)
                        dve.tensor_tensor(off_s[:, t, :], ps[:, 3 - 2 * t, 320:320 + TS], e_s[:, t, 0:TS],
                                          ALU.mult)
                        dve.drain()
                        dve.tensor_tensor(off_s[:, t, :], off_s[:, t, :], ps[:, 3, 352 + t * 64:352 + t * 64 + TS],
                                          ALU.add)
                        dve.drain()
                        last = dve.scalar_tensor_tensor(out=flat[:, tile, TP:T], in0=flat[:, tile, TP:T],
                                                        scalar=skip[:, tile:tile + 1], in1=off_s[:, t, :],
                                                        op0=ALU.mult, op1=ALU.add)
                    last.then_inc(y_read.sem, 1)
                dve.drain().then_inc(rows_used.sem, 1)
                times_z(G - 1)
                wait(dve, y_rms_ready, l, 1)
                wait(dve, conv_done_out, l, 32)
                wait(dve, h_end_out, l, 16 * G)
                dve.reciprocal(y_rms[:], y_rms[:])
                for n in range(PAIRS_SO):
                    tiles = slice(4 * n, 4 * n + 4)
                    dve.drain()
                    for t in range(4 * n, 4 * n + 4):
                        dve.scalar_tensor_tensor(out=flat[:, t, 0:T], in0=flat[:, t, 0:T],
                                                 scalar=vecs[:, V_SSD + t:V_SSD + t + 1], in1=y_rms[:, t // 2, :],
                                                 op0=ALU.mult, op1=ALU.mult)
                    split(y_hi[:, tiles], y_lo[:, tiles], flat[:, tiles, 0:T]).then_inc(y_ready.sem, 1)

                wait(dve, unit_done[1], l, M_AO)
                wait(dve, gates_ready, l, 1)
                for o in range(0, KD, 2):
                    dve.tensor_tensor(merged[:, o:o + 2, :], ps[:, o:o + 2, 0:T], gates[:, o:o + 2, :], ALU.mult)\
                        .then_inc(row_evac.sem, 1)
                wait(dve, unit_done[1], l, M_AO + 1)
                for o in range(0, KD, 2):
                    dve.tensor_tensor(gates[:, KD + o:KD + o + 2, :], ps[:, o:o + 2, 0:T],
                                      gates[:, KD + o:KD + o + 2, :], ALU.mult).then_inc(row_evac.sem, 1)
                dve.drain()
                dve.tensor_tensor(merged[:], merged[:], gates[:, KD:, :], ALU.add)
                split(mg_hi[:], mg_lo[:], merged[:]).then_inc(merged_ready.sem, 1)
                add_to_x(l, M_WO + PAIRS_WO, 1.0)
                norm(l, 3, V_F2)
                swiglu(l, M_W13B, E_W13B, PAIRS_W13)

            dve.wait_ge(end_rms.sem, 1)
            normed(V_FIN)
            dve.drain().then_inc(end_normed.sem, 1)
            dve.wait_ge(end_turned.sem, 2)
            dve.tensor_copy(y_out_s[:].rearrange("p (k c) -> p k c", k=2), ps[0:TS, 5:7, :])\
                .then_inc(end_copied.sem, 1)

        @block.gpsimd
        def _(pool):
            def low_unit(s, m):
                pool.wait_ge(hi_ready[s].sem, m + 1)
                pool.tensor_tensor(w_lo[s][:], raw[s][:], w_hi[s][:].bitcast(F32), ALU.subtract)\
                    .then_inc(lo_ready[s].sem, 1)

            for s in range(2):
                pool.sem_inc(lo_ready[s].sem, 1)
                pool.sem_inc(unit_done[s].sem, 1)
                pool.sem_inc(evac[s].sem, 1)
            pool.sem_inc(vec_turned.sem, 1)
            pool.sem_inc(rows_used.sem, 1)
            pool.sem_inc(xbc_ready.sem, 2)
            pool.wait_ge(start_in.sem, 16 * 9)
            for g in range(NG):
                last = pool.tensor_tensor(rel_q[:, g], delta[:], rel4[:, 4 * g:4 * g + 4].unsqueeze(1).unsqueeze(3)
                                          .broadcast_to((P, NB, HPG, NT)), ALU.mult)
            last.then_inc(rel_q_ready.sem, 1)
            for s in range(2):
                low_unit(s, 0)
            pool.wait_ge(lines_ready.sem, 1)
            pool.dma_start(lines_dram.rearrange("(g i) w -> i g w", g=NG), lines[:]).then_inc(lines_out.sem, 16)
            pool.wait_ge(lines_out.sem, 16)
            pool.dma_start(skewed.rearrange("h (p w) -> h p w", p=P)[:, :, 0:W_LINE],
                           bass.AP(lines_dram.tensor, lines_dram.offset,
                                   [[W_LINE, NG * HPG], [0, P], [1, W_LINE]])).then_inc(skewed_out.sem, 16)
            pool.wait_ge(skewed_out.sem, 16)
            for h in range(NG * HPG):
                src = skewed[h, 0:P * W_LINE].rearrange("(p w) -> p w", p=P)[:, P - 1:P - 1 + 2 * P]
                pool.dma_start(bias_p[:, h, :], src).then_inc(bias_in.sem, 16)
            with pool.Fori(0, DEPTH) as l:
                m = l * PAIRS
                wait(pool, kv_copied, l, 9)
                for g in range(NG):
                    c0 = 1 if g == 0 else 0
                    dst = kv_prompt[g][bass.ds(l, 1), 0].rearrange("a (c p) k h e -> p (a c) (k h e)", p=P)
                    pool.dma_start(dst, kv_p[:, c0:, g].rearrange("p c k e -> p c (k e)"))\
                        .then_inc(kv_out.sem, 16)
                    dst = kv_sample[g][bass.ds(l, 1)].rearrange("a b t k h e -> (a b t) (k h e)")
                    pool.dma_start(dst, kv_s[:, g].rearrange("p k e -> p (k e)")).then_inc(kv_out.sem, 16)
                with pool.Fori(0, PAIRS_XBC) as i:
                    for s in range(2):
                        low_unit(s, m + (M_XBC + 1 + i))
                wait(pool, tails_copied, l, 8)
                pool.dma_start(conv_prompt[bass.ds(l, 1), 0].rearrange("a i c -> (a i) c"), conv_out[0:3, :])\
                    .then_inc(conv_done_out.sem, 16)
                pool.dma_start(conv_sample[bass.ds(l, 1)].rearrange("a b i c -> (a b i) c"), conv_out[3:27, :])\
                    .then_inc(conv_done_out.sem, 16)

                def side_low(n):
                    low_unit(n % 2, m + (M_SIDE + n // 2))

                for g in range(G):
                    if g % 2:
                        side_low(3 * g // 2 + 2)
                    wait(pool, h_end_ready, l, g + 1)
                    dst = ssm_prompt[bass.ds(l, 1), 0, HPG * g:HPG * g + HPG]\
                        .rearrange("a h p n -> (a h p) n")\
                        .rearrange("(t q) n -> q t n", t=2)
                    pool.dma_start(dst, h_end[:]).then_inc(h_end_out.sem, 16)
                    for t in (2 * g, 2 * g + 1):
                        wait(pool, h_new_ready, l, t + 1)
                        dst = ssm_sample[bass.ds(l, 1), :, 2 * t:2 * t + 2].rearrange("a b h p n -> (a h p) b n")
                        pool.dma_start(dst, h0[t % 3][:]).then_inc(h_new_out[t % 3].sem, 16)
                    side_low((3 * g + 1) // 2 + 2)
                with pool.Fori(PAIRS_SIDE, PAIRS_SIDE + PAIRS_G + PAIRS_SO + PAIRS_AO + PAIRS_WO) as i:
                    for s in range(2):
                        low_unit(s, m + (M_SIDE + 1 + i))
            for signal in (kv_out, conv_done_out, h_end_out, *h_new_out):
                pool.wait_ge(signal.sem, DEPTH * signal.per)

        @block.tensor
        def _(pe):
            def product(out, s, at, hi, lo, first, last):
                wh, wl = w_hi[s][:, at:at + P], w_lo[s][:, at:at + P]
                pe.matmul(out, wh, hi, start=first, stop=False)
                pe.matmul(out, wh, lo, start=False, stop=False)
                return pe.matmul(out, wl, hi, start=False, stop=last)

            def panel_unit(s, m, tiles=2, k_tiles=KD):
                pe.wait_ge(lo_ready[s].sem, m + 2)
                for o in range(tiles):
                    for k in range(KD):
                        last = product(ps[:, 2 * s + o, 0:T], s, k * 256 + o * P, u_hi[:, k, :], u_lo[:, k, :],
                                       k == 0, k == KD - 1)
                last.then_inc(unit_done[s].sem, 1)

            def panels(l, m0, e0, n):
                settle(pe)
                with pe.Fori(0, n) as i:
                    for s in range(2):
                        pe.wait_ge(evac[s].sem, l * EVACS + (e0 + 1 + i))
                        panel_unit(s, l * PAIRS + (m0 + i))

            def row_unit(s, m, k0, kt, hi, lo, first, last, k_reg=None):
                pe.wait_ge(lo_ready[s].sem, m + 2)
                for k in range(kt):
                    for o in range(KD):
                        if k_reg is None:
                            h, w = hi[:, k0 + k, :], lo[:, k0 + k, :]
                        else:
                            h, w = (v[:, bass.ds(k_reg + (k0 + k), 1), :].rearrange("p a t -> p (a t)")
                                    for v in (hi, lo))
                        end = product(ps[:, o, 0:T], s, k * D + o * P, h, w, first and k == 0, last and k == kt - 1)
                end.then_inc(unit_done[s].sem, 1)

            def rows(l, m0, n, hi, lo, tail=0, parts=None):
                def ready(i):
                    if parts:
                        pe.wait_ge(parts.sem, parts.at(l, i + 1))

                ready(0)
                row_unit(0, l * PAIRS + m0, 0, 2, hi, lo, True, False)
                row_unit(1, l * PAIRS + m0, 2, 2, hi, lo, False, n == 1 and not tail)
                stop = n if tail else n - 1
                if stop > 1:
                    with pe.Fori(1, stop) as i:
                        ready(i)
                        for s in range(2):
                            row_unit(s, l * PAIRS + (m0 + i), 2 * s, 2, hi, lo, False, False, i * 4)
                if not tail and n > 1:
                    ready(n - 1)
                    row_unit(0, l * PAIRS + (m0 + n - 1), 4 * (n - 1), 2, hi, lo, False, False)
                    row_unit(1, l * PAIRS + (m0 + n - 1), 4 * (n - 1) + 2, 2, hi, lo, False, True)
                if tail:
                    row_unit(0, l * PAIRS + (m0 + n), 4 * n, 1, hi, lo, False, False)
                    row_unit(1, l * PAIRS + (m0 + n), 4 * n + 1, 1, hi, lo, False, True)

            def column_sums(bank, src, tiles):
                for n, k in enumerate(tiles):
                    last = pe.matmul(ps[:, bank, 0:T], ones, src[:, k, :], start=(n == 0), stop=(n == len(tiles) - 1))
                return last

            def norm(l, n):
                wait(pe, squared, l, n)
                column_sums(4, full, range(KD)).then_inc(sum_ready.sem, 1)

            def swiglu(l, m0, e0, u, h):
                wait(pe, u_ready, l, u)
                panels(l, m0, e0, PAIRS_W13)
                wait(pe, evac[0], l, e0 + PAIRS_W13)
                wait(pe, h_ready, l, h)
                rows(l, m0 + PAIRS_W13, PAIRS_W2 - 1, h_hi, h_lo, tail=1)

            def turn(out, src):
                p = src.shape[0]
                return pe.transpose(out, src, square[0:p, 0, 0:p])

            pe.wait_ge(const_in.sem, 32)
            pe.wait_ge(x_in_ready.sem, 32)
            for k in range(KD):
                for c in range(2):
                    turn(ps[:, k, c * P:(c + 1) * P], x_in[:, c, k * P:(k + 1) * P])
                last = turn(ps[:, k, TP:T], xs_in[:, k * P:(k + 1) * P])
                if k % 2:
                    last.then_inc(x_turned.sem, 1)
            pe.wait_ge(x_first.sem, 4)
            pe.wait_ge(rel_q_ready.sem, 1)
            col = 0
            for g in range(NG):
                lhs = rel_q[:, g].rearrange("p b i q -> p (b i q)")
                pe.matmul(ps[:, 0, col:col + KEYS[g]], lhs, hot[:, col:col + KEYS[g]], start=True, stop=True)
                new = OLD + g * TS
                pe.matmul(ps[:, 1, g * TS:(g + 1) * TS], lhs, hot[:, new:new + TS], start=True, stop=True)
                last = pe.matmul(ps[0:HPG, (2, 3, 7)[g], 0:W_LINE], rel4[0:32, 4 * g:4 * g + 4], line_hot[:, g, :],
                                 start=True, stop=True)
                col += KEYS[g]
            last.then_inc(bias_product.sem, 1)

            with pe.Fori(0, DEPTH) as l:
                m = l * PAIRS
                wait(pe, vec_in, l, 160)
                pe.wait_ge(row_evac.sem, l * ROWS)
                turn(ps[:, 5, 0:P], vec_a[:])
                turn(ps[:, 6, 0:80], vec_b[:]).then_inc(vec_turned.sem, 1)
                norm(l, 1)
                pe.wait_ge(lines_ready.sem, 1)
                swiglu(l, M_W13A, E_W13A, 1, PAIRS_W13)
                wait(pe, row_evac, l, R_W2A + 4)
                norm(l, 2)
                wait(pe, u_ready, l, 2)
                pe.wait_ge(lo_ready[0].sem, m + (M_QKV + 2))
                for k in range(KD):
                    last = product(ps[:, 0, 0:T], 0, k * 256, u_hi[:, k, :], u_lo[:, k, :], k == 0, k == KD - 1)
                last.then_inc(unit_done[0].sem, 1)
                panel_unit(1, m + M_QKV)
                with pe.Fori(1, PAIRS_QKV) as i:
                    for s in range(2):
                        pe.wait_ge(evac[s].sem, l * EVACS + (E_QKV + 1 + i))
                        panel_unit(s, m + (M_QKV + i))

                wait(pe, evac[0], l, E_QKV + PAIRS_QKV)
                wait(pe, evac[1], l, E_QKV + PAIRS_QKV)
                settle(pe)
                for c in range(2):
                    turn(ps[:, 4, c * HEADS:(c + 1) * HEADS], dt_fm[:, c * P:(c + 1) * P])
                turn(ps[0:TS, 4, 2 * HEADS:3 * HEADS], dt_fm[:, TP:T]).then_inc(dt_turned.sem, 1)
                wait(pe, conv_state_in, l, 16)
                settle(pe)
                for t in range(KC):
                    last = turn(ps[:, t // 16, (t % 16) * 24:(t % 16 + 1) * 24], conv_in[:, t * P:(t + 1) * P])
                last.then_inc(conv_state_turned.sem, 1)
                wait(pe, da_ready, l, 1)
                pe.matmul(ps[:, 4, 128:160], sgt, da[:, 0, :], start=True, stop=True)
                pe.matmul(ps[:, 4, 160:192], sgt, da[:, 1, :], start=True, stop=True)
                pe.matmul(ps[:, 4, 192:224], sgt, da[:, 0, :], start=True, stop=False)
                pe.matmul(ps[:, 4, 192:224], ones, da[:, 1, :], start=False, stop=True)
                pe.matmul(ps[0:TS, 4, 224:256], sgt_s, da[0:TS, 2, :], start=True, stop=True)\
                    .then_inc(to_end_product.sem, 1)
                wait(pe, conv_state_ready, l, 1)
                for n in range(9):
                    g, c = n // 3, n % 3
                    if n >= 4:
                        wait(pe, kv_copied, l, n - 3)
                    cols = slice(c * P, (c + 1) * P) if c < 2 else slice(TP, T)
                    for kv in range(2):
                        for j in range(2):
                            at = kv * 256 + j * P
                            last = turn(ps[0:(P if c < 2 else TS), n % 4, at:at + P],
                                        qkv[:, 6 + 6 * kv + 2 * g + j, cols])
                    last.then_inc(kv_turned.sem, 1)

                wait(pe, kv_copied, l, 9)
                wait(pe, q_diag_ready, l, 1)
                wait(pe, to_end_ready, l, 1)

                def k_turn(b):
                    wait(pe, cache_in[b % KV_BUFS], l, 48 * (b // KV_BUFS + 1))
                    if b >= 2:
                        wait(pe, k_t_ready, l, b - 1)
                    for pair in range(2):
                        bank = 4 + 2 * (b % 2) + pair
                        for kt in range(4):
                            rows_k = P if kt < 3 else 64
                            last = turn(ps[:, bank, kt * P:kt * P + rows_k],
                                        kv_in[b % KV_BUFS][0:rows_k, kt, pair * P:(pair + 1) * P])
                    last.then_inc(k_turned.sem, 1)

                def k_scores(b):
                    wait(pe, k_t_ready, l, b + 1)
                    for pair in range(2):
                        for kt in range(4):
                            rows_k, g = (P, (kt + 1) // 2) if kt < 3 else (64, 2)
                            at = kt * P + b * 16 + pair * 8
                            pe.matmul(ps[0:rows_k, 0, at:at + 8], k_t[b % 2][:, pair, kt * P:kt * P + rows_k],
                                      q_diag[:, 2 * g + pair, b, :], start=True, stop=True)

                k_turn(0)
                for b in range(NB):
                    if b + 1 < NB:
                        k_turn(b + 1)
                    k_scores(b)
                for g in range(NG):
                    for pair in range(2):
                        tile = 2 * g + pair
                        out = ps[0:TS, 1, g * P:(g + 1) * P].rearrange("p (b x c) -> p b x c", b=NB, x=2)
                        last = pe.matmul(out[:, :, pair, :], qkv[:, 6 + tile, TP:T], q_diag[:, tile], start=True,
                                         stop=True)
                last.then_inc(scores_t_ready.sem, 1)
                wait(pe, st_ready, l, 1)
                for kt in range(4):
                    rows_k = P if kt < 3 else 64
                    turn(ps[:, 2, kt * P:kt * P + rows_k], st[0:rows_k, kt, :])
                for g in range(NG):
                    last = turn(ps[:, 3, g * TS:(g + 1) * TS], st_new[:, g, :])
                last.then_inc(sc_s_product.sem, 1)
                wait(pe, p_s_ready, l, 1)
                for kt in range(4):
                    rows_k = P if kt < 3 else 64
                    turn(ps[0:rows_k, 4, kt * P:(kt + 1) * P], sc_s[:, kt * P:kt * P + rows_k])
                for g in range(NG):
                    last = turn(ps[0:TS, 5, g * P:(g + 1) * P], sc_s[:, OLD + g * TS:OLD + (g + 1) * TS])
                last.then_inc(pt_s_turned.sem, 1)
                wait(pe, pt_s_ready, l, 1)
                for pair in range(2):
                    for g in range(NG):
                        rhs = st_new[:, g, :].rearrange("p (b x c) -> p b x c", b=NB, x=2)[:, :, pair, :]
                        pe.matmul(ps[:, 6 + pair, 0:64], kv_s[:, g, 1, pair * P:(pair + 1) * P], rhs,
                                  start=(g == 0), stop=False)
                for b in range(NB):
                    wait(pe, cache_in[b % KV_BUFS], l, 48 * ((NB + b) // KV_BUFS + 1))
                    for pair in range(2):
                        for kt in range(4):
                            rows_k = P if kt < 3 else 64
                            at = b * 16 + pair * 8
                            last = pe.matmul(ps[:, 6 + pair, b * 8:b * 8 + 8],
                                             kv_in[b % KV_BUFS][0:rows_k, kt, pair * P:(pair + 1) * P],
                                             st[0:rows_k, kt, at:at + 8], start=False, stop=(kt == 3 and b == NB - 1))
                    last.then_inc(v_used.sem, 1)
                pe.drain().then_inc(o_s_ready.sem, 1)

                wait(pe, o_s_copied, l, 1)

                def scores(n):
                    i, c, k = n // 2, n % 2, n % 2 + 1
                    if n >= 2:
                        wait(pe, sc_p_read, l, n - 1)
                    half = slice(64 * (i % 2), 64 * (i % 2) + 64)
                    for g in range(NG):
                        tile = 2 * g + i // 2
                        bank = 2 * (n % 2) + g // 2
                        at = (g % 2) * 256
                        last = pe.matmul(ps[:, bank, at:at + k * P], qkv[half, tile, c * P:(c + 1) * P],
                                         qkv[half, 6 + tile, 0:k * P], start=True, stop=True)
                    last.then_inc(sc_p_product.sem, 1)

                def mix(n):
                    i, c, k = n // 2, n % 2, n % 2 + 1
                    wait(pe, p_p_ready, l, n + 1)
                    for g in range(NG):
                        for kt in range(k):
                            last = turn(ps[:, 4 + kt, g * P:(g + 1) * P], sc_p[n % 2][:, g, kt * P:(kt + 1) * P])
                    last.then_inc(pt_p_turned.sem, 1)
                    wait(pe, pt_p_ready, l, n + 1)
                    half = slice(64 * (i % 2), 64 * (i % 2) + 64)
                    for g in range(NG):
                        for kt in range(k):
                            last = pe.matmul(ps[half, 6 + n % 2, 0:P], kv_p[:, kt, g, 1, i * HD:(i + 1) * HD],
                                             pt_p[n % 2][:, g, kt, :], start=(g == 0 and kt == 0),
                                             stop=(g == NG - 1 and kt == k - 1))
                    last.then_inc(o_p_ready.sem, 1)

                scores(0)
                for n in range(2 * HPG):
                    if n + 1 < 2 * HPG:
                        scores(n + 1)
                    mix(n)
                panels(l, M_XBC, E_XBC, PAIRS_XBC)
                wait(pe, tails_ready, l, 1)
                wait(pe, evac[1], l, E_XBC + PAIRS_XBC)
                wait(pe, attn_ready, l, 1)
                for n in range(8):
                    for t in range(4 * n, 4 * n + 4):
                        last = turn(ps[0:27, n, (t % 4) * P:(t % 4 + 1) * P],
                                    tails[:, t].rearrange("p j c -> p (j c)"))
                    last.then_inc(tails_turned.sem, 1)

                def side(q):
                    n, s, half = q // 2, q // 2 % 2, q % 2
                    if q:
                        wait(pe, side_taken, l, q)
                    if not half:
                        pe.wait_ge(lo_ready[s].sem, m + (M_SIDE + n // 2 + 2))
                    for k in range(KD):
                        last = product(ps[:, SIDE_BANK, 0:T], s, k * 256 + half * P, u_hi[:, k, :], u_lo[:, k, :],
                                       k == 0, k == KD - 1)
                    last.then_inc(unit_done[s].sem if half else side_first.sem, 1)

                wait(pe, xbc_ready, l, 2 * PAIRS_XBC)
                wait(pe, tails_copied, l, 8)
                for g in range(G):
                    fb, fc = flat[:, TILE_B + g, :], flat[:, TILE_C + g, :]
                    if g:
                        wait(pe, y_read, l, g)
                        wait(pe, h_end_ready, l, g)
                    for c in range(3):
                        cols = slice(c * P, (c + 1) * P) if c < 2 else slice(TP, T)
                        n = P if c < 2 else TS
                        for t in range(2):
                            at = t * P + (256 if c == 2 else 0)
                            turn(ps[0:n, min(c, 1), at:at + P], flat[:, 2 * g + t, cols])
                        turn(ps[0:n, 7, c * P:(c + 1) * P], fb[:, cols])
                        last = pe.matmul(ps[0:n, 3, c * P:c * P + n], fb[:, cols], fc[:, cols], start=True, stop=True)
                    last.then_inc(ssd_turned.sem, 1)
                    wait(pe, a_tri_ready, l, g + 1)
                    if g:
                        wait(pe, h0_t_ready, l, 2 * g)
                    for c in range(2):
                        pe.matmul(ps[:, 4 + c, :], sgt, a_tri[c][:].rearrange("p h c -> p (h c)"), start=True, stop=True)
                    pe.matmul(ps[0:TS, 6, 336:464], sgt_s, a_tri_s[:].rearrange("p h c -> p (h c)"), start=True,
                              stop=True)
                    for t in range(2):
                        pe.matmul(ps[:, 6, t * P:(t + 1) * P], a_exp[:, t * P:(t + 1) * P], tri, start=True, stop=True)
                        last = pe.matmul(ps[:, 6, 256 + t * 40:256 + (t + 1) * 40], a_exp_s[:, t * P:(t + 1) * P],
                                         tri_sel_s, start=True, stop=True)
                    last.then_inc(seg_product.sem, 1)
                    wait(pe, xdt_ready, l, g + 1)
                    wait(pe, b_ready, l, g + 1)
                    pe.matmul(ps[:, 7, 0:256], b_tm[:, 0, :], xdte[:, 0, :], start=True, stop=True)\
                        .then_inc(h_mid_product.sem, 1)
                    side(3 * g)
                    wait(pe, m_ready, l, g + 1)
                    for c in range(2):
                        for h in range(HPG):
                            half = slice(64 * (h % 2), 64 * (h % 2) + 64)
                            at = c * 256 + (h // 2) * P
                            pe.matmul(ps[half, 0, at:at + P], xdt[:, c, h * HD:(h + 1) * HD], dec[c][:, h, :],
                                      start=True, stop=True)
                    for h in range(HPG):
                        half = slice(64 * (h % 2), 64 * (h % 2) + 64)
                        at = 352 + (h // 2) * 64
                        pe.matmul(ps[half, 3, at:at + TS], xdt_s[:, h * HD:(h + 1) * HD], dec_s[:, h, :], start=True,
                                  stop=True)
                    wait(pe, h_mid_ready, l, g + 1)
                    for t in range(2):
                        pe.matmul(ps[:, 1, t * P:(t + 1) * P], h_mid[:, t * P:(t + 1) * P], fc[:, P:TP], start=True,
                                  stop=True)
                    for t in range(2):
                        out = ps[:, 7, 256 + t * P:256 + (t + 1) * P]
                        pe.matmul(out, xdte[:, 2, t * P:(t + 1) * P], b_tm[:, 0, :], start=True, stop=False)
                        last = pe.matmul(out, xdte[:, 1, t * P:(t + 1) * P], b_tm[:, 1, :], start=False, stop=True)
                    last.then_inc(y_product.sem, 1)
                    wait(pe, b_diag_ready, l, g + 1)
                    for t in range(2):
                        tile = 2 * g + t
                        wait(pe, h0_in[tile % 3], l, 16 * (tile // 3 + 1))
                        if t:
                            wait(pe, h0_t_ready, l, tile)
                        for b in range(NB):
                            last = turn(ps[:, 4 + b // 4, (b % 4) * P:(b % 4 + 1) * P], h0[tile % 3][:, b, :])
                        last.then_inc(h0_turned.sem, 1)
                        if t:
                            side(3 * g + 1)
                        wait(pe, h_end_ready, l, g + 1)
                        if t:
                            wait(pe, h_new_ready, l, tile)
                        for n in range(2):
                            pe.matmul(ps[:, 6 + n, :], xdte_s[:, t * P:(t + 1) * P],
                                      b_diag[:, 4 * n:4 * n + 4, :].rearrange("p b n -> p (b n)"), start=True, stop=True)
                        wait(pe, h0_t_ready, l, tile + 1)
                        for b in range(NB):
                            last = pe.matmul(ps[:, 3 - 2 * t, 320 + b * NT:320 + (b + 1) * NT], h0_t[:, b, :],
                                             fc[:, TP + b * NT:TP + (b + 1) * NT], start=True, stop=True)
                        last.then_inc(h0_product.sem, 1)
                    side(3 * g + 2)
                wait(pe, y_read, l, G)
                wait(pe, h_new_ready, l, KI)
                wait(pe, side_taken, l, SIDE_TILES)
                panels(l, M_G, E_G, 1)
                for n in (3, 2, 1, 0):
                    wait(pe, y_sq_ready, l, 4 - n)
                    if n == 1:
                        wait(pe, evac[0], l, E_G + 1)
                        wait(pe, evac[1], l, E_G + 1)
                    for g in (2 * n, 2 * n + 1):
                        last = column_sums(g, y_sq, (2 * g, 2 * g + 1))
                last.then_inc(y_sum_ready.sem, 1)
                wait(pe, y_rms_ready, l, 1)
                panels(l, M_G + 1, E_G + 1, PAIRS_G - 1)
                wait(pe, evac[0], l, E_G + PAIRS_G)
                wait(pe, evac[1], l, E_G + PAIRS_G)
                rows(l, M_SO, PAIRS_SO, y_hi, y_lo, parts=y_ready)
                wait(pe, row_evac, l, R_SO + 4)
                row_unit(0, m + M_AO, 0, 1, ao_hi, ao_lo, True, False)
                row_unit(1, m + M_AO, 1, 1, ao_hi, ao_lo, False, True)
                wait(pe, row_evac, l, R_AO + 4)
                wait(pe, merged_ready, l, 1)
                rows(l, M_WO, PAIRS_WO, mg_hi, mg_lo)
                wait(pe, row_evac, l, R_WO + 4)
                norm(l, 3)
                swiglu(l, M_W13B, E_W13B, 3, 2 * PAIRS_W13)

            pe.wait_ge(row_evac.sem, DEPTH * ROWS)
            pe.wait_ge(end_squared.sem, 1)
            column_sums(4, full, range(KD)).then_inc(end_sum.sem, 1)
            pe.wait_ge(end_normed.sem, 1)
            for c in range(2):
                for k in range(KD):
                    last = turn(ps[:, 2 * c + k // 4, (k % 4) * P:(k % 4 + 1) * P], full[:, k, c * P:(c + 1) * P])
            last.then_inc(end_turned.sem, 1)
            for k in range(KD):
                last = turn(ps[0:TS, 5 + k // 4, (k % 4) * P:(k % 4 + 1) * P], full[:, k, TP:T])
            last.then_inc(end_turned.sem, 1)


_INS = ['x_prompt', 'x_sample', 'cache_kv_w128', 'cache_kv_w512', 'cache_kv_w2048', 'state_conv', 'state_ssm',
        'rel_bias', 'ffn1_norm', 'ffn1_w13', 'ffn1_w2', 'mix_norm', 'w_in', 'conv_w', 'conv_b', 'dt_bias',
        'a_log', 'd_skip', 'ssd_norm', 'w_ssd_out', 'w_attn_out', 'w_o', 'ffn2_norm', 'ffn2_w13', 'ffn2_w2',
        'final_norm']


def _outs(depth):
    return [(1, TP, D), (NB, NT, D),
            (depth, 1, 128, 2, 4, HD), (depth, 1, 256, 2, 4, HD), (depth, 1, 256, 2, 4, HD),
            (depth, 1, CW - 1, CONV), (depth, 1, HEADS, HD, NS),
            (depth, NB, NT, 2, 4, HD), (depth, NB, NT, 2, 4, HD), (depth, NB, NT, 2, 4, HD),
            (depth, NB, CW - 1, CONV), (depth, NB, HEADS, HD, NS)]


def build(nc, inputs):
    arrays, args = {}, []
    given = {name: np.ascontiguousarray(inputs[name]) for name in _INS}
    given.update(constants())
    for name, a in given.items():
        arrays[f"in_{name}_dram"] = a
        args.append(nc.dram_tensor(f"in_{name}_dram", a.shape, mybir.dt.from_np(a.dtype), kind="ExternalInput").ap())
    outs = _outs(given["w_in"].shape[0])
    for i, shape in enumerate(outs):
        args.append(nc.dram_tensor(f"out_{i}_dram", shape, F32, kind="ExternalOutput").ap())
    trunk(nc, *args)
    return arrays, len(outs)


def kernel(**inputs):
    import concourse.bacc as _bacc
    from concourse.bass_utils import run_bass_kernel_spmd as _run

    nc = _bacc.Bacc("TRN2", target_bir_lowering=False, num_devices=1)
    arrays, n = build(nc, inputs)
    r = _run(nc, [arrays], core_ids=[0])
    return tuple(r.results[0][f"out_{i}_dram"] for i in range(n))
```

```python
from contextlib import ExitStack

import numpy as np

import concourse.bass as bass
from concourse import mybir

F32 = mybir.dt.float32
F32R = mybir.dt.float32r
ALU = mybir.AluOpType
ACT = mybir.ActivationFunctionType
AX = mybir.AxisListType

P = 128
D = 1024
KD = D // P
TP = 256
NB, NT = 8, 4
TS = NB * NT
T = TP + TS
FF = 2816
KF = FF // P
DI = 2048
KI = DI // P
CONV = 4096
KC = CONV // P
CW = 4
HEADS = 32
HD = 64
NS = 128
G = 8
HPG = 4
AW = 768
NG = 3
DIL = (1, 4, 16)
REACH = 128
SCALE = HD ** -0.5
EPS = 1e-6
MASKED = -1e30

C_Z = 0
C_XBC = DI
C_DT = C_XBC + CONV
C_Q = C_DT + HEADS
C_G = C_Q + 3 * AW

PADDED = CW - 1 + TP + NB * (CW - 1 + NT)
SEQ0 = CW - 1 + TP
RUN = CW - 1 + NT
CONVED = PADDED - (CW - 1)
PITCH = 320

KEYS = (128, 256, 64)
OLD = sum(KEYS)
NEW = NG * TS
KV_BUFS = 4
W_LINE = 384

UNIT = 2048
PAIRS_W13, PAIRS_W2, PAIRS_QKV, PAIRS_XBC, PAIRS_SIDE, PAIRS_G = 11, 6, 5, 8, 6, 2
PAIRS_SO, PAIRS_AO, PAIRS_WO = 4, 1, 2
M_W13A = 0
M_W2A = M_W13A + PAIRS_W13
M_QKV = M_W2A + PAIRS_W2
M_XBC = M_QKV + PAIRS_QKV
M_SIDE = M_XBC + PAIRS_XBC
M_G = M_SIDE + PAIRS_SIDE
M_AO = M_G + PAIRS_G
M_SO = M_AO + PAIRS_AO
M_WO = M_SO + PAIRS_SO
M_W13B = M_WO + PAIRS_WO
M_W2B = M_W13B + PAIRS_W13
PAIRS = M_W2B + PAIRS_W2
E_W13A = 0
E_QKV = E_W13A + PAIRS_W13
E_G = E_QKV + PAIRS_QKV
E_W13B = E_G + PAIRS_G
EVACS = E_W13B + PAIRS_W13
R_W2A, R_AO, R_SO, R_WO, R_W2B = 0, 4, 8, 12, 16
ROWS = 20
XBC_KEYS = (2, 1, 2, 1, 2, 1, 2, 1)
XBC_SOFTMAX = (1, 2, 1)
XBC_VALUES = (2, 1, 1, 1, 2, 1, 1, 1)
XBC_PROMPT = (0, 1, 1, 1, 1, 1, 1, 0)
XBC_UNITS = 2 * PAIRS_XBC
assert sum(XBC_KEYS + XBC_SOFTMAX + XBC_VALUES + XBC_PROMPT) == KC
SIDE_TILES = 3 * G


def side_unit(n):
    return (True, n // 3) if n % 3 == 1 else (False, n - (n + 1) // 3)


def constants():
    f = np.float32
    i = np.arange(P)
    sq = np.zeros((P, 4, P), f)
    sq[:, 0] = np.eye(P)
    sq[:, 1] = 1
    sq[:, 2] = i[:, None] <= i[None]
    sq[:, 3] = i[:, None] > i[None]
    j = np.arange(TS)
    same = j[:, None] // NT == j[None] // NT
    small = np.zeros((TS, 2 * TS + NB), f)
    small[:, :TS] = same & (j[:, None] <= j[None])
    small[:, TS:TS + NB] = j[:, None] // NT == np.arange(NB)[None]
    small[:, TS + NB:] = same & (j[:, None] > j[None])

    def bucket(d):
        big = 16 + np.floor(np.log(np.maximum(d, 1) / 16.0) / np.log(128.0) * 16 + 1e-9).astype(int)
        return np.where(d < 16, d, np.minimum(big, 31))

    line = np.zeros((32, NG, W_LINE), f)
    line_mask = np.full((HPG, NG, W_LINE), MASKED, f)
    d = 255 - np.arange(W_LINE)
    for g, dil in enumerate(DIL):
        ok = (d >= 0) & (d % dil == 0) & (d // dil <= REACH)
        line[bucket(np.maximum(d, 0))[ok], g, np.nonzero(ok)[0]] = 1
        line_mask[:, g, ok] = 0
    hot = np.zeros((P, OLD + NEW), f)
    mask = np.full((P, OLD + NEW), MASKED, f)
    row_q, row_b = i % NT, i // (HPG * NT)

    def key(col, q, dist):
        hot[32 * q + bucket(np.array(dist)), col] = 1

    col = 0
    for g, dil in enumerate(DIL):
        for n in range(KEYS[g]):
            at = n if g < 2 else 16 * (n // NT) + n % NT
            for q in range(NT):
                dist = (KEYS[g] if g < 2 else 256) + q - at
                if dist % dil == 0 and dist // dil <= REACH:
                    key(col, q, dist)
                    mask[row_q == q, col] = 0
            col += 1
    for g, dil in enumerate(DIL):
        for n in range(TS):
            for q in range(NT):
                dist = q - n % NT
                if dist >= 0 and dist % dil == 0:
                    key(col, q, dist)
                    mask[(row_q == q) & (row_b == n // NT), col] = 0
            col += 1
    delta = np.zeros((P, P), f)
    delta[:] = (i[:, None] // 32) == (i[None] % NT)
    return {"c_square": sq, "c_small": small, "c_line": line, "c_line_mask": line_mask,
            "c_hot": hot, "c_mask": mask, "c_delta": delta}


class Signal:

    def __init__(self, sem, per, credit=0):
        self.sem, self.per, self.credit = sem, per, credit

    def at(self, layer, n):
        return layer * self.per + (n + self.credit)


def trunk(nc, x_prompt, x_sample, cache_kv_w128, cache_kv_w512, cache_kv_w2048, state_conv, state_ssm,
          rel_bias, ffn1_norm, ffn1_w13, ffn1_w2, mix_norm, w_in, conv_w, conv_b, dt_bias, a_log,
          d_skip, ssd_norm, w_ssd_out, w_attn_out, w_o, ffn2_norm, ffn2_w13, ffn2_w2, final_norm,
          c_square, c_small, c_line, c_line_mask, c_hot, c_mask, c_delta,
          y_prompt, y_sample, kv0_prompt, kv1_prompt, kv2_prompt, conv_prompt, ssm_prompt,
          kv0_sample, kv1_sample, kv2_sample, conv_sample, ssm_sample):
    DEPTH = w_in.shape[0]
    kv_prompt = (kv0_prompt, kv1_prompt, kv2_prompt)
    kv_sample = (kv0_sample, kv1_sample, kv2_sample)
    lines_dram = nc.dram_tensor("bias_lines", (NG * HPG, W_LINE), F32, kind="Internal").ap()
    SKEWED = P * (W_LINE + 1)
    skewed = nc.dram_tensor("bias_skewed", (NG * HPG, SKEWED), F32, kind="Internal").ap()

    cursor = [16512]

    def place(name, shape, dt=F32, at=None):
        size = 4 * int(np.prod(shape[1:]))
        size += -size % 32
        if at is None:
            at = cursor[0]
            cursor[0] += size
        assert at + size <= 229344, (name, at + size)
        return nc.alloc_sbuf_tensor_at(name, shape, dt, offset=at)

    raw = [place(f"w_raw{s}", [P, UNIT]) for s in range(2)]
    w_hi = [place(f"w_hi{s}", [P, UNIT], F32R) for s in range(2)]
    w_lo = [place(f"w_lo{s}", [P, UNIT], F32R) for s in range(2)]
    x = place("x", [P, KD, T])
    u_at = cursor[0]
    u_hi = place("u_hi", [P, KD, T], F32R)
    u_lo = place("u_lo", [P, KD, T], F32R)
    mg_hi = place("merged_hi", [P, KD, T], F32R, at=u_at)
    mg_lo = place("merged_lo", [P, KD, T], F32R, at=u_at + 4 * KD * T)
    ao_at = cursor[0]
    ao_hi = place("attn_hi", [P, 2, T], F32R)
    ao_lo = place("attn_lo", [P, 2, T], F32R)
    attn_at = cursor[0]
    attn = place("attn", [P, 2, T])
    silu_z = place("silu_z", [P, 2, T], at=attn_at)
    bias_p = place("bias_prompt", [P, NG * HPG, 2 * P])
    bias_s = place("bias_sample", [P, OLD + NEW])
    square = place("square", [P, 4, P])
    small = place("small", [TS, 2 * TS + NB])
    ident, ones, tri, sgt = (square[:, n, :] for n in range(4))
    tri_sel_s, sel_s, tri_s, sgt_s = (small[:, 0:TS + NB], small[:, TS:TS + NB], small[:, 0:TS],
                                      small[:, TS + NB:])
    vec_a = place("vec_a", [P, P])
    vec_b = place("vec_b", [80, P])
    conv_wt = place("conv_wt", [P, CW * KC])
    vecs = place("vecs", [P, 80])
    V_CONVB, V_F1, V_MIX, V_F2, V_SSD, V_FIN = 0, 32, 40, 48, 56, 72
    rows3 = place("rows3", [P, 3, HEADS])
    a_head = place("a_head", [P, HEADS])
    skip = place("skip", [P, KI])
    eps = place("eps", [P, 1])
    warm = place("warm", [P, 1])
    q_diag = place("q_diag", [P, 2 * NG, NB, 2 * NT])
    dt_fm = place("dt_fm", [HEADS, T])
    dt_raw = place("dt_raw", [P, 3, HEADS])
    dt = place("dt", [P, 3, HEADS])
    da = place("da", [P, 3, HEADS])
    dt_w = [place(f"dt_w{n}", [P, 3, HEADS]) for n in range(3)]
    to_end = place("to_end", [P, 4, HEADS])

    F_AT = cursor[0]
    flat = place("flat", [P, KC, PITCH])
    h_hi = place("h_hi", [P, KF, T], F32R, at=F_AT)
    gates = flat[:, KI:2 * KI, 0:T]
    R1 = cursor[0]
    cursor[0] += 39168
    h_lo = place("h_lo", [P, KF, T], F32R, at=R1)
    qkv = place("qkv", [P, 18, T], at=R1)
    conv_in = place("conv_in", [NB * (CW - 1), CONV], at=R1 + 20736)
    kv_p = place("kv_p", [P, 2, NG, 2, 256], at=R1 + 20736)
    kv_s = place("kv_s", [TS, NG, 2, 256], at=R1 + 20736 + 12288)
    conv_out = place("conv_out", [27, CONV], at=R1)
    y_hi = place("y_hi", [P, KI, T], F32R, at=R1)
    y_lo = place("y_lo", [P, KI, T], F32R, at=R1 + 4 * KI * T)
    R2 = cursor[0]

    class Plan:

        def __init__(self, at):
            self.now = at

        def __call__(self, name, shape, dt=F32):
            size = 4 * int(np.prod(shape[1:]))
            size += -size % 32
            at, self.now = self.now, self.now + size
            return place(name, shape, dt, at=at)

    r = Plan(R2)
    x_in = r("x_in", [P, 2, D])
    xs_in = r("xs_in", [TS, D])
    rf = Plan(R1 + 4 * KF * T)
    lines = rf("lines", [HPG, NG, W_LINE])
    line_mask = rf("line_mask", [HPG, NG, W_LINE])
    rf = Plan(F_AT + 4 * KF * T)
    line_hot = rf("line_hot", [32, NG, W_LINE])
    hot = rf("hot", [P, OLD + NEW])
    mask = rf("mask", [P, OLD + NEW])
    delta = rf("delta", [P, NB, HPG, NT])
    rel4 = rf("rel4", [P, NG * HPG])
    rel_q = rf("rel_q", [P, NG, NB, HPG, NT])
    r = Plan(R2)
    full = r("full", [P, KD, T])
    rms = r("rms", [P, T])
    rinv = r("rinv", [P, T])
    silu_a = r("silu_a", [P, 2, T])
    hidden = r("hidden", [P, 2, T])
    y_out = place("y_out", [P, 2, D], at=F_AT)
    y_out_s = place("y_out_s", [TS, D], at=F_AT + 8192)
    r = Plan(R2)
    kv_in = [r(f"kv_in{n}", [P, 4, 256]) for n in range(KV_BUFS)]
    sc_s = place("sc_s", [P, OLD + NEW], at=r.now)
    k_t = [r(f"k_t{n}", [P, 2, OLD]) for n in range(2)]
    st = place("st", [P, 4, P], at=ao_at)
    st_new = place("st_new", [TS, NG, P], at=ao_at + 4 * 4 * P)
    stat_s = [r(f"stat_s{n}", [P, 1]) for n in range(3)]
    r = Plan(R2)
    sc_p = [r(f"sc_p{n}", [P, NG, 2 * P]) for n in range(2)]
    pt_p = [r(f"pt_p{n}", [P, NG, 2, P]) for n in range(2)]
    stat_p = [[r(f"stat_p{n}_{m}", [P, 1]) for m in range(3)] for n in range(2)]
    acc = place("acc", [P, 2, PADDED], at=R1 + 4 * 12 * T)
    tails = place("tails", [P, KC, 9, CW - 1], at=R1 + 16384)
    assert 4 * KC * 27 + 16384 <= 4 * 18 * T
    r = Plan(R2)
    h0 = [r(f"h0_{n}", [P, NB, NS]) for n in range(3)]
    h0_t = r("h0_t", [P, NB, P])
    a_tri = [r(f"a_tri{n}", [P, HPG, P]) for n in range(2)]
    xdt = r("xdt", [P, 2, 256])
    cbm = r("cbm", [P, 2, P])
    r = Plan(R1 + 16384)
    dec = [r(f"dec{n}", [P, HPG, P]) for n in range(2)]
    b_tm = r("b_tm", [P, 2, NS])
    xdte = r("xdte", [P, 3, 256])
    e_off = r("e_off", [P, 2, P])
    a_exp = r("a_exp", [P, 256])
    h_mid = r("h_mid", [P, 256])
    off_t = r("off_t", [P, 2, P])
    h_end = r("h_end", [P, 2, NS])
    xdt_s = r("xdt_s", [TS, 256])
    xdte_s = r("xdte_s", [TS, 256])
    b_tm_s = r("b_tm_s", [TS, NS])
    b_diag = r("b_diag", [TS, NB, NS])
    cbm_s = r("cbm_s", [TS, TS])
    a_tri_s = r("a_tri_s", [TS, HPG, TS])
    dec_s = r("dec_s", [TS, HPG, TS])
    a_exp_s = r("a_exp_s", [TS, 256])
    e_s = r("e_s", [P, 2, TS + NB])
    off_s = r("off_s", [P, 2, TS])
    assert r.now <= R2, r.now - R2
    y_sq = place("y_sq", [P, KI, T], at=R2 + 4 * 1440)
    y_rms = place("y_rms", [P, G, T], at=R2 + 4 * 4 * T)
    merged = place("merged", [P, KD, T], at=R2)
    print_free = 229344 - cursor[0]
    assert print_free > 24000

    ps = nc.alloc_psum_tensor("ps", [P, 8, 512], F32)

    with ExitStack() as ctx:
        def sem(name, per, credit=0):
            return Signal(ctx.enter_context(nc.semaphore(name)), per, credit)

        settled = sem("settled", 0)
        const_in = sem("const_in", 0)
        x_in_ready = sem("x_in_ready", 0)
        start_in = sem("start_in", 0)
        x_turned = sem("x_turned", 0)
        x_first = sem("x_first", 0)
        rel_q_ready = sem("rel_q_ready", 0)
        bias_product = sem("bias_product", 0)
        lines_ready = sem("lines_ready", 0)
        lines_out = sem("lines_out", 0)
        skewed_out = sem("skewed_out", 0)
        bias_in = sem("bias_in", 0)
        zeroed = sem("zeroed", 0)
        raw_in = [sem(f"raw_in{s}", 16 * PAIRS) for s in range(2)]
        hi_ready = [sem(f"hi_ready{s}", PAIRS) for s in range(2)]
        lo_ready = [sem(f"lo_ready{s}", PAIRS, 1) for s in range(2)]
        unit_done = [sem(f"unit_done{s}", PAIRS, 1) for s in range(2)]
        evac = [sem(f"evac{s}", EVACS, 1) for s in range(2)]
        row_evac = sem("row_evac", ROWS, 4)
        vec_in = sem("vec_in", 16 * 10)
        vec_turned = sem("vec_turned", 1, 1)
        vec_ready = sem("vec_ready", 1)
        rows_used = sem("rows_used", 1, 1)
        squared = sem("squared", 3 * 4)
        sum_ready = sem("sum_ready", 3)
        rms_ready = sem("rms_ready", 3)
        normed_half = sem("normed_half", 3 * 2)
        u_hi_ready = sem("u_hi_ready", 3 * 2)
        u_ready = sem("u_ready", 3 * 2)
        silu_ready = sem("silu_ready", 2 * PAIRS_W13)
        h_ready = sem("h_ready", 2 * PAIRS_W13)
        conv_state_in = sem("conv_state_in", 16)
        conv_state_turned = sem("conv_state_turned", 1)
        conv_state_ready = sem("conv_state_ready", 1)
        dt_turned = sem("dt_turned", 1)
        dt_exp_asked = sem("dt_exp_asked", 1)
        dt_exp_ready = sem("dt_exp_ready", 1)
        da_ready = sem("da_ready", 1)
        to_end_product = sem("to_end_product", 1)
        to_end_ready = sem("to_end_ready", 1)
        kv_turned = sem("kv_turned", 9)
        kv_copied = sem("kv_copied", 9)
        kv_out = sem("kv_out", 16 * 6)
        q_diag_ready = sem("q_diag_ready", 1)
        cache_in = [sem(f"cache_in{n}", 16 * 3 * 2 * NB // KV_BUFS) for n in range(KV_BUFS)]
        k_turned = sem("k_turned", NB)
        k_t_ready = sem("k_t_ready", NB)
        v_used = sem("v_used", NB)
        scores_t_ready = sem("scores_t_ready", 1)
        st_ready = sem("st_ready", 1)
        sc_s_product = sem("sc_s_product", 1)
        max_s_ready = sem("max_s_ready", 1)
        exp_s_ready = sem("exp_s_ready", 1)
        p_s_ready = sem("p_s_ready", 1)
        pt_s_turned = sem("pt_s_turned", 1)
        pt_s_ready = sem("pt_s_ready", 1)
        o_s_ready = sem("o_s_ready", 1)
        o_s_copied = sem("o_s_copied", 1)
        sc_p_product = sem("sc_p_product", 8)
        sc_p_read = sem("sc_p_read", 8)
        max_p_ready = sem("max_p_ready", 8)
        exp_p_ready = sem("exp_p_ready", 8)
        p_p_ready = sem("p_p_ready", 8)
        pt_p_turned = sem("pt_p_turned", 8)
        pt_p_ready = sem("pt_p_ready", 8)
        o_p_ready = sem("o_p_ready", 8)
        attn_ready = sem("attn_ready", 1)
        xbc_first = sem("xbc_first", XBC_UNITS)
        xbc_taken = sem("xbc_taken", KC)
        conv_ready = sem("conv_ready", XBC_UNITS)
        xbc_ready = sem("xbc_ready", XBC_UNITS)
        tails_ready = sem("tails_ready", XBC_UNITS)
        tails_turned = sem("tails_turned", 8)
        tails_copied = sem("tails_copied", 8)
        conv_done_out = sem("conv_done_out", 32)
        ssd_turned = sem("ssd_turned", G)
        b_ready = sem("b_ready", G)
        a_tri_ready = sem("a_tri_ready", G)
        seg_product = sem("seg_product", G)
        dec_ready = sem("dec_ready", G)
        xdt_ready = sem("xdt_ready", G)
        b_diag_ready = sem("b_diag_ready", G)
        m_ready = sem("m_ready", G)
        h_mid_product = sem("h_mid_product", G)
        h_mid_ready = sem("h_mid_ready", G)
        y_product = sem("y_product", G)
        y_read = sem("y_read", G)
        h_end_ready = sem("h_end_ready", G)
        h_end_out = sem("h_end_out", 16 * G)
        h0_in = [sem(f"h0_in{n}", 16 * len(range(n, KI, 3))) for n in range(3)]
        h0_turned = sem("h0_turned", KI)
        h0_t_ready = sem("h0_t_ready", KI)
        h0_product = sem("h0_product", KI)
        h_new_ready = sem("h_new_ready", KI)
        h_new_out = [sem(f"h_new_out{n}", 16 * len(range(n, KI, 3))) for n in range(3)]
        side_first = sem("side_first", SIDE_TILES // 2)
        side_taken = sem("side_taken", SIDE_TILES)
        silu_z_ready = sem("silu_z_ready", G)
        z_used = sem("z_used", G)
        gates_ready = sem("gates_ready", 1)
        y_sq_ready = sem("y_sq_ready", 4)
        y_sum_ready = sem("y_sum_ready", 1)
        y_rms_ready = sem("y_rms_ready", 1)
        y_ready = sem("y_ready", PAIRS_SO)
        merged_ready = sem("merged_ready", PAIRS_WO)
        end_squared = sem("end_squared", 0)
        end_sum = sem("end_sum", 0)
        end_rms = sem("end_rms", 0)
        end_normed = sem("end_normed", 0)
        end_turned = sem("end_turned", 0)
        end_copied = sem("end_copied", 0)
        end_out = sem("end_out", 0)

        block = ctx.enter_context(nc.Block())
        TILE_B, TILE_C = KI, KI + G
        XBC_BANK = 2
        SIDE_BANK = 2

        def wait(eng, signal, layer, n):
            eng.wait_ge(signal.sem, signal.at(layer, n))

        def settle(eng):
            eng.sem_inc(settled.sem, 1)

        @block.sync
        def _(sp):
            def unit(s, m, dst, src):
                sp.wait_ge(lo_ready[s].sem, m + 1)
                settle(sp)
                sp.dma_start(dst, src).then_inc(raw_in[s].sem, 16)

            def columns(w, l, first, n=256):
                return w[bass.ds(l, 1), :, bass.ds(first, n)].rearrange("a (k p) n -> p (a k) n", p=P)

            def panel(m, w, l, first0, first1):
                for s, first in enumerate((first0, first1)):
                    unit(s, m, raw[s][:].rearrange("p (k n) -> p k n", k=KD), columns(w, l, first))

            def rows(m, w, l, row0, kt=2):
                for s in range(2):
                    src = w[bass.ds(l, 1), bass.ds(row0 + s * kt * P, kt * P), :]
                    unit(s, m, raw[s][:, 0:kt * D].rearrange("p (k n) -> p k n", k=kt),
                         src.rearrange("a (k p) n -> p (a k) n", p=P))

            sp.dma_start(square[:], c_square).then_inc(const_in.sem, 16)
            sp.dma_start(x_in[:], x_prompt[0].rearrange("(c p) d -> p c d", p=P)).then_inc(x_in_ready.sem, 16)
            sp.dma_start(xs_in[:], x_sample.rearrange("b t d -> (b t) d")).then_inc(x_in_ready.sem, 16)
            sp.dma_start(small[:], c_small).then_inc(const_in.sem, 16)

            with sp.Fori(0, DEPTH) as l:
                sp.wait_ge(vec_turned.sem, l + 1)
                settle(sp)
                sp.dma_start(vec_a[:], conv_w[bass.ds(l, 1)].rearrange("a i (t c) -> (a i t) c", c=P))\
                    .then_inc(vec_in.sem, 16)
                for row, v in ((V_CONVB, conv_b), (V_F1, ffn1_norm), (V_MIX, mix_norm), (V_F2, ffn2_norm),
                               (V_SSD, ssd_norm)):
                    n = v.shape[1] // P
                    sp.dma_start(vec_b[row:row + n, :], v[bass.ds(l, 1)].rearrange("a (t c) -> (a t) c", c=P))\
                        .then_inc(vec_in.sem, 16)
                sp.dma_start(vec_b[V_FIN:V_FIN + KD, :], final_norm.rearrange("(t c) -> t c", c=P))\
                    .then_inc(vec_in.sem, 16)
                sp.wait_ge(rows_used.sem, l + 1)
                settle(sp)
                for n, v in enumerate((dt_bias, a_log, d_skip)):
                    sp.dma_start(rows3[:, n, :], v[bass.ds(l, 1)].broadcast_to((P, HEADS)))\
                        .then_inc(vec_in.sem, 16)
                m = l * PAIRS
                with sp.Fori(0, PAIRS_W13) as i:
                    panel(m + (M_W13A + i), ffn1_w13, l, i * 256, FF + i * 256)
                with sp.Fori(0, PAIRS_W2 - 1) as i:
                    rows(m + (M_W2A + i), ffn1_w2, l, i * 512)
                rows(m + (M_W2A + PAIRS_W2 - 1), ffn1_w2, l, (PAIRS_W2 - 1) * 512, 1)
                unit(0, m + M_QKV, raw[0][:].rearrange("p (k n) -> p k n", k=KD)[:, :, 0:P], columns(w_in, l, C_DT, P))
                unit(1, m + M_QKV, raw[1][:].rearrange("p (k n) -> p k n", k=KD), columns(w_in, l, C_Q))
                panel(m + (M_QKV + 1), w_in, l, C_Q + 256, C_Q + 512)
                sp.wait_ge(lines_out.sem, 16)
                wait(sp, row_evac, l, R_W2A + 4)
                settle(sp)
                sp.dma_start(conv_in[:], state_conv[bass.ds(l, 1)].rearrange("a b i c -> (a b i) c"))\
                    .then_inc(conv_state_in.sem, 16)
                panel(m + (M_QKV + 2), w_in, l, C_Q + 768, C_Q + 1024)

                def cache(n):
                    b, kv = n % NB, n // NB
                    if n == 0:
                        wait(sp, u_ready, l, 4)
                    elif KV_BUFS <= n < KV_BUFS + NB:
                        wait(sp, k_turned, l, n - KV_BUFS + 1)
                    elif n >= KV_BUFS + NB:
                        wait(sp, v_used, l, n - KV_BUFS - NB + 1)
                    settle(sp)
                    buf, s = kv_in[n % KV_BUFS], cache_in[n % KV_BUFS].sem
                    sp.dma_start(buf[:, 0, :], cache_kv_w128[bass.ds(l, 1), b, :, kv]
                                 .rearrange("a p h e -> (a p) (h e)")).then_inc(s, 16)
                    sp.dma_start(buf[:, 1:3, :], cache_kv_w512[bass.ds(l, 1), b, :, kv]
                                 .rearrange("a (t p) h e -> p (a t) (h e)", p=P)).then_inc(s, 16)
                    sp.dma_start(buf[0:64, 3, :], cache_kv_w2048[bass.ds(l, 1), b, :, kv]
                                 .rearrange("a (m r) h e -> (a m) r (h e)", r=16)[:, 0:NT])\
                        .then_inc(s, 16)

                for n in range(KV_BUFS):
                    cache(n)
                with sp.Fori(3, PAIRS_QKV) as i:
                    panel(m + (M_QKV + i), w_in, l, C_Q - 256 + i * 512, C_Q + i * 512)

                def xbc(n):
                    unit(n % 2, m + (M_XBC + n // 2), raw[n % 2][:].rearrange("p (k n) -> p k n", k=KD),
                         columns(w_in, l, C_XBC + 256 * n))

                for n in range(4):
                    xbc(n)
                n, b, tiles = 4, KV_BUFS + 1, 0
                cache(KV_BUFS)
                for count in XBC_KEYS:
                    if b < KV_BUFS + NB:
                        cache(b)
                        b += 1
                    tiles += count
                    while n < tiles // 2 + 4:
                        xbc(n)
                        n += 1
                tiles += sum(XBC_SOFTMAX)
                for count in XBC_VALUES:
                    while n < min(tiles // 2 + 4, XBC_UNITS):
                        xbc(n)
                        n += 1
                    if b < 2 * NB:
                        cache(b)
                        b += 1
                    tiles += count
                while n < XBC_UNITS:
                    xbc(n)
                    n += 1

                def side(n):
                    gate, j = side_unit(n)
                    unit(n % 2, m + (M_SIDE + n // 2), raw[n % 2][:].rearrange("p (k n) -> p k n", k=KD),
                         columns(w_in, l, (C_G if gate else C_Z) + 256 * j))

                def states(t):
                    if t >= 3:
                        wait(sp, h_new_out[t % 3], l, 16 * (t // 3))
                    settle(sp)
                    src = state_ssm[bass.ds(l, 1), :, 2 * t:2 * t + 2].rearrange("a b h p n -> (a h p) b n")
                    sp.dma_start(h0[t % 3][:], src).then_inc(h0_in[t % 3].sem, 16)

                for n in range(4):
                    side(n)
                wait(sp, tails_turned, l, 8)
                wait(sp, xbc_ready, l, XBC_UNITS)
                for t in range(3):
                    states(t)
                for g in range(G):
                    for t in range(2 * g + 3, min(2 * g + 5, KI)):
                        states(t)
                    for n in range(3 * g // 2 + 4, (3 * g + 3) // 2 + 4):
                        if n < 2 * PAIRS_SIDE:
                            side(n)
                        else:
                            j = n - 2 * PAIRS_SIDE + G // 2
                            unit(n % 2, m + (M_SIDE + n // 2), raw[n % 2][:].rearrange("p (k n) -> p k n", k=KD),
                                 columns(w_in, l, C_G + 256 * j))
                rows(m + M_AO, w_attn_out, l, 0, 1)
                with sp.Fori(0, PAIRS_SO) as i:
                    rows(m + (M_SO + i), w_ssd_out, l, i * 512)
                with sp.Fori(0, PAIRS_WO) as i:
                    rows(m + (M_WO + i), w_o, l, i * 512)
                with sp.Fori(0, PAIRS_W13) as i:
                    panel(m + (M_W13B + i), ffn2_w13, l, i * 256, FF + i * 256)
                with sp.Fori(0, PAIRS_W2 - 1) as i:
                    rows(m + (M_W2B + i), ffn2_w2, l, i * 512)
                rows(m + (M_W2B + PAIRS_W2 - 1), ffn2_w2, l, (PAIRS_W2 - 1) * 512, 1)
            for s in range(2):
                unit(s, DEPTH * PAIRS, raw[s][:, 0:8], w_o[0, 0:P, 0:8])
            sp.wait_ge(end_copied.sem, 2)
            sp.dma_start(y_prompt[0].rearrange("(c p) d -> p c d", p=P), y_out[:]).then_inc(end_out.sem, 16)
            sp.dma_start(y_sample.rearrange("b t d -> (b t) d"), y_out_s[:]).then_inc(end_out.sem, 16)
            sp.wait_ge(end_out.sem, 32)
            for s in range(2):
                sp.wait_ge(raw_in[s].sem, 16 * (DEPTH * PAIRS + 1))

        @block.scalar
        def _(act):
            def high(m):
                for s in range(2):
                    high_unit(s, m)

            def high_unit(s, m):
                act.wait_ge(raw_in[s].sem, m * 16 + 16)
                act.wait_ge(unit_done[s].sem, m + 1)
                act.activation(w_hi[s][:], raw[s][:], ACT.Copy).then_inc(hi_ready[s].sem, 1)

            def norm(l, n, ready):
                for o in range(4):
                    wait(act, row_evac, l, ready + o + 1)
                    act.activation(full[:, 2 * o:2 * o + 2, :], x[:, 2 * o:2 * o + 2, :], ACT.Square)\
                        .then_inc(squared.sem, 1)
                act.activation(warm[:], eps[:], ACT.Sqrt)
                wait(act, sum_ready, l, n)
                act.activation(rms[:], ps[:, 0, 0:T], ACT.Sqrt, bias=eps[:], scale=1.0 / D)\
                    .then_inc(rms_ready.sem, 1)
                for half in range(2):
                    tiles = slice(4 * half, 4 * half + 4)
                    wait(act, normed_half, l, 2 * n - 1 + half)
                    act.activation(u_hi[:, tiles], full[:, tiles], ACT.Copy).then_inc(u_hi_ready.sem, 1)

            def swiglu(l, m0, e0, n0):
                def body(i):
                    high_unit(0, l * PAIRS + (m0 + 1 + i))
                    act.wait_ge(unit_done[0].sem, l * PAIRS + (m0 + 2 + i))
                    act.wait_ge(evac[1].sem, l * EVACS + (e0 + 1 + i))
                    act.activation(silu_a[:], ps[:, 0:2, 0:T], ACT.Silu).then_inc(evac[0].sem, 1)
                    high_unit(1, l * PAIRS + (m0 + 1 + i))
                with act.Fori(0, PAIRS_W13) as i:
                    body(i)
                with act.Fori(0, PAIRS_W2) as i:
                    high(l * PAIRS + (M_W2A - M_W13A + m0 + 1 + i))

            for dst, src in ((delta[:], c_delta.rearrange("p (b i q) -> p b i q", b=NB, i=HPG)), (hot[:], c_hot),
                             (line_hot[:], c_line), (line_mask[:], c_line_mask), (mask[:], c_mask)):
                act.dma_start(dst, src).then_inc(start_in.sem, 16)
            for q in range(NT):
                act.dma_start(rel4[32 * q:32 * q + 32, :], rel_bias).then_inc(start_in.sem, 16)
            act.wait_ge(zeroed.sem, 1)
            high(0)
            with act.Fori(0, DEPTH) as l:
                m = l * PAIRS
                act.wait_ge(x_first.sem, 4)
                norm(l, 1, R_W2B - ROWS)
                swiglu(l, M_W13A, E_W13A, 0)
                norm(l, 2, R_W2A)

                high_unit(0, m + (M_QKV + 1))
                act.wait_ge(unit_done[0].sem, m + (M_QKV + 2))
                act.activation(dt_fm[:], ps[0:HEADS, 0, 0:T], ACT.Copy).then_inc(evac[0].sem, 1)
                high_unit(1, m + (M_QKV + 1))
                act.wait_ge(unit_done[1].sem, m + (M_QKV + 2))
                act.activation(qkv[:, 0:2, :], ps[:, 2:4, 0:T], ACT.Copy).then_inc(evac[1].sem, 1)
                with act.Fori(1, PAIRS_QKV) as i:
                    for s in range(2):
                        high_unit(s, m + (M_QKV + 1 + i))
                        act.wait_ge(unit_done[s].sem, m + (M_QKV + 2 + i))
                        act.activation(qkv[:, bass.ds(i * 4 + (2 * s - 2), 2), :], ps[:, 2 * s:2 * s + 2, 0:T],
                                       ACT.Copy).then_inc(evac[s].sem, 1)
                wait(act, dt_exp_asked, l, 1)
                act.activation(dt_w[0][:], dt_w[1][:], ACT.Exp)
                act.activation(a_head[:], rows3[:, 1, :], ACT.Exp).then_inc(dt_exp_ready.sem, 1)
                wait(act, to_end_product, l, 1)
                act.activation(to_end[:, 0:3, :], ps[:, 4, 128:224].rearrange("p (c h) -> p c h", c=3), ACT.Exp)
                act.activation(to_end[0:TS, 3, :], ps[0:TS, 4, 224:256], ACT.Exp).then_inc(to_end_ready.sem, 1)

                def xbc_silu(n):
                    wait(act, conv_ready, l, n + 1)
                    tiles = slice(2 * n, 2 * n + 2)
                    act.activation(flat[:, tiles, 0:TP], acc[:, :, 0:TP], ACT.Silu)
                    act.activation(flat[:, tiles, TP:T].rearrange("p t (b c) -> p t b c", c=NT),
                                   acc[:, :, SEQ0:PADDED].rearrange("p t (b c) -> p t b c", c=RUN)
                                   [:, :, :, 0:NT], ACT.Silu).then_inc(xbc_ready.sem, 1)

                def xbc(q):
                    n, bank = q // 2, XBC_BANK + q % 2
                    if q % 2:
                        act.wait_ge(unit_done[n % 2].sem, m + (M_XBC + n // 2 + 2))
                    else:
                        wait(act, xbc_first, l, n + 1)
                    act.activation(flat[:, q, SEQ0:PADDED].rearrange("p (b c) -> p b c", c=RUN)[:, :, CW - 1:],
                                   ps[:, bank, TP:T].rearrange("p (b c) -> p b c", c=NT), ACT.Copy)
                    act.activation(flat[:, q, CW - 1:SEQ0], ps[:, bank, 0:TP], ACT.Copy).then_inc(xbc_taken.sem, 1)
                    if q % 2:
                        high_unit(n % 2, m + (M_XBC + n // 2 + 1))
                        if n:
                            xbc_silu(n - 1)
                    return q + 1

                def key_tiles(b):
                    wait(act, k_turned, l, b + 1)
                    act.activation(k_t[b % 2][:, 0, :], ps[:, 4 + 2 * (b % 2), 0:OLD], ACT.Copy)
                    act.activation(k_t[b % 2][:, 1, :], ps[:, 5 + 2 * (b % 2), 0:OLD], ACT.Copy)\
                        .then_inc(k_t_ready.sem, 1)

                q = 0
                key_tiles(0)
                for b in range(NB):
                    if b + 1 < NB:
                        key_tiles(b + 1)
                    for _ in range(XBC_KEYS[b]):
                        q = xbc(q)
                wait(act, scores_t_ready, l, 1)
                act.activation(st[:, 0:3, :], ps[:, 0, 0:3 * P].rearrange("p (k c) -> p k c", k=3), ACT.Copy)
                act.activation(st[0:64, 3, :], ps[0:64, 0, 3 * P:4 * P], ACT.Copy)
                act.activation(st_new[:], ps[0:TS, 1, 0:3 * P].rearrange("p (k c) -> p k c", k=3), ACT.Copy)\
                    .then_inc(st_ready.sem, 1)
                for _ in range(XBC_SOFTMAX[0]):
                    q = xbc(q)
                wait(act, max_s_ready, l, 1)
                act.activation(sc_s[:], sc_s[:], ACT.Exp, bias=stat_s[0][:], accum_out=stat_s[1][:])\
                    .then_inc(exp_s_ready.sem, 1)
                for _ in range(XBC_SOFTMAX[1]):
                    q = xbc(q)
                wait(act, pt_s_turned, l, 1)
                act.activation(st[:, 0:3, :], ps[:, 4, 0:3 * P].rearrange("p (k c) -> p k c", k=3), ACT.Copy)
                act.activation(st[0:64, 3, :], ps[0:64, 4, 3 * P:4 * P], ACT.Copy)
                act.activation(st_new[:], ps[0:TS, 5, 0:3 * P].rearrange("p (k c) -> p k c", k=3), ACT.Copy)\
                    .then_inc(pt_s_ready.sem, 1)
                for _ in range(XBC_SOFTMAX[2] + sum(XBC_VALUES)):
                    q = xbc(q)

                for n in range(2 * HPG):
                    k = n % 2 + 1
                    wait(act, max_p_ready, l, n + 1)
                    act.activation(sc_p[n % 2][:, :, 0:k * P], sc_p[n % 2][:, :, 0:k * P], ACT.Exp,
                                   bias=stat_p[n % 2][0][:], accum_out=stat_p[n % 2][1][:])\
                        .then_inc(exp_p_ready.sem, 1)
                    wait(act, pt_p_turned, l, n + 1)
                    src = ps[:, 4:6, 0:NG * P].rearrange("p k (g c) -> p k g c", g=NG)
                    act.activation(pt_p[n % 2][:, :, 0:k, :].rearrange("p g k c -> p k g c"), src[:, 0:k],
                                   ACT.Copy).then_inc(pt_p_ready.sem, 1)
                    for _ in range(XBC_PROMPT[n]):
                        q = xbc(q)
                xbc_silu(XBC_UNITS - 1)
                act.drain()
                for n in range(8):
                    wait(act, tails_turned, l, n + 1)
                    act.activation(conv_out[:, n * 512:(n + 1) * 512], ps[0:27, n, :], ACT.Copy)\
                        .then_inc(tails_copied.sem, 1)

                def side(q):
                    n, half = q // 2, q % 2
                    gate, j = side_unit(n)
                    if half:
                        act.wait_ge(unit_done[n % 2].sem, m + (M_SIDE + n // 2 + 2))
                    else:
                        wait(act, side_first, l, n + 1)
                    if not gate and not half and j:
                        wait(act, z_used, l, j)
                    dst = gates[:, 2 * j + half, :] if gate else silu_z[:, half, :]
                    act.activation(dst, ps[:, SIDE_BANK, 0:T], ACT.Copy).then_inc(side_taken.sem, 1)
                    if half and not gate:
                        act.drain()
                        act.activation(silu_z[:], silu_z[:], ACT.Silu).then_inc(silu_z_ready.sem, 1)
                    if half:
                        high_unit(n % 2, m + (M_SIDE + n // 2 + 1))

                wait(act, kv_out, l, 16 * 6)
                for g in range(G):
                    wait(act, ssd_turned, l, g + 1)
                    for c in range(2):
                        act.activation(b_tm[:, c, :], ps[:, 7, c * P:(c + 1) * P], ACT.Copy)
                    act.activation(b_tm_s[:], ps[0:TS, 7, 256:384], ACT.Copy).then_inc(b_ready.sem, 1)
                    wait(act, seg_product, l, g + 1)
                    for c in range(2):
                        act.activation(dec[c][:], ps[:, 4 + c, :].rearrange("p (h c) -> p h c", h=HPG), ACT.Exp)
                    act.activation(dec_s[:], ps[0:TS, 6, 336:464].rearrange("p (h c) -> p h c", h=HPG), ACT.Exp)
                    act.activation(e_off[:], ps[:, 6, 0:256].rearrange("p (t c) -> p t c", t=2), ACT.Exp)
                    act.activation(e_s[:], ps[:, 6, 256:336].rearrange("p (t c) -> p t c", t=2), ACT.Exp)\
                        .then_inc(dec_ready.sem, 1)
                    wait(act, h_mid_product, l, g + 1)
                    act.activation(h_mid[:], ps[:, 7, 0:256], ACT.Copy).then_inc(h_mid_ready.sem, 1)
                    side(3 * g)
                    wait(act, y_product, l, g + 1)
                    if g:
                        wait(act, h_end_out, l, 16 * g)
                    act.activation(h_end[:], ps[:, 7, 256:512].rearrange("p (t n) -> p t n", t=2), ACT.Copy)\
                        .then_inc(h_end_ready.sem, 1)
                    for t in (2 * g, 2 * g + 1):
                        wait(act, h0_turned, l, t + 1)
                        act.activation(h0_t[:], ps[:, 4:6, :].rearrange("p k (b c) -> p (k b) c", c=P), ACT.Copy)\
                            .then_inc(h0_t_ready.sem, 1)
                    side(3 * g + 1)
                    side(3 * g + 2)

                wait(act, z_used, l, G)
                for n in (3, 2, 1, 0):
                    if n == 1:
                        for j in range(3):
                            wait(act, h_new_out[j], l, h_new_out[j].per)
                    act.activation(y_sq[:, 4 * n:4 * n + 4, :], flat[:, 4 * n:4 * n + 4, 0:T], ACT.Square)\
                        .then_inc(y_sq_ready.sem, 1)

                def gate_pair(i):
                    for s in range(2):
                        high_unit(s, m + (M_G + 1 + i))
                        act.wait_ge(unit_done[s].sem, m + (M_G + 2 + i))
                        tile = KD + i * 4 + 2 * s
                        act.activation(gates[:, tile:tile + 2, :], ps[:, 2 * s:2 * s + 2, 0:T], ACT.Sigmoid)\
                            .then_inc(evac[s].sem, 1)

                gate_pair(0)
                wait(act, y_sum_ready, l, 1)
                act.activation(y_rms[:], ps[:, :, 0:T], ACT.Sqrt, bias=eps[:], scale=1.0 / 256)\
                    .then_inc(y_rms_ready.sem, 1)
                gate_pair(1)
                act.activation(gates[:, 0:KD, :], gates[:, 0:KD, :], ACT.Sigmoid).then_inc(gates_ready.sem, 1)
                with act.Fori(0, PAIRS_SO + PAIRS_AO + PAIRS_WO) as i:
                    high(m + (M_AO + 1 + i))
                norm(l, 3, R_WO)
                swiglu(l, M_W13B, E_W13B, PAIRS_W13)

            wait(act, row_evac, DEPTH, 0)
            act.activation(full[:], x[:], ACT.Square).then_inc(end_squared.sem, 1)
            act.wait_ge(end_sum.sem, 1)
            act.activation(rms[:], ps[:, 4, 0:T], ACT.Sqrt, bias=eps[:], scale=1.0 / D).then_inc(end_rms.sem, 1)
            act.wait_ge(end_turned.sem, 1)
            for c in range(2):
                last = act.activation(y_out[:, c, :].rearrange("p (k c) -> p k c", k=2),
                                      ps[:, 2 * c:2 * c + 2, :], ACT.Copy)
            last.then_inc(end_copied.sem, 1)

        @block.vector
        def _(dve):
            def low_unit(s, m):
                dve.wait_ge(hi_ready[s].sem, m + 1)
                dve.tensor_tensor(w_lo[s][:], raw[s][:], w_hi[s][:].bitcast(F32), ALU.subtract)\
                    .then_inc(lo_ready[s].sem, 1)

            def low(m):
                for s in range(2):
                    low_unit(s, m)

            def split(hi, lo, src):
                dve.drain()
                dve.tensor_copy(hi, src)
                dve.drain()
                return dve.tensor_tensor(lo, src, hi.bitcast(F32), ALU.subtract)

            def normed(gain):
                dve.reciprocal(rinv[:], rms[:])
                dve.drain()
                for k in range(KD):
                    dve.scalar_tensor_tensor(out=full[:, k, :], in0=x[:, k, :], scalar=vecs[:, gain + k:gain + k + 1],
                                             in1=rinv[:], op0=ALU.mult, op1=ALU.mult)

            def norm(l, n, gain):
                wait(dve, rms_ready, l, n)
                dve.reciprocal(rinv[:], rms[:])
                dve.drain()
                for k in range(KD):
                    last = dve.scalar_tensor_tensor(out=full[:, k, :], in0=x[:, k, :],
                                                    scalar=vecs[:, gain + k:gain + k + 1], in1=rinv[:],
                                                    op0=ALU.mult, op1=ALU.mult)
                    if k % 4 == 3:
                        last.then_inc(normed_half.sem, 1)
                for half in range(2):
                    tiles = slice(4 * half, 4 * half + 4)
                    wait(dve, u_hi_ready, l, 2 * n - 1 + half)
                    dve.tensor_tensor(u_lo[:, tiles], full[:, tiles], u_hi[:, tiles].bitcast(F32), ALU.subtract)\
                        .then_inc(u_ready.sem, 1)

            def swiglu(l, m0, e0, n0):
                with dve.Fori(0, PAIRS_W13) as i:
                    low(l * PAIRS + (m0 + 1 + i))
                    dve.drain()
                    dve.wait_ge(evac[0].sem, l * EVACS + (e0 + 2 + i))
                    dve.wait_ge(unit_done[1].sem, l * PAIRS + (m0 + 2 + i))
                    dve.tensor_tensor(hidden[:], silu_a[:], ps[:, 2:4, 0:T], ALU.mult).then_inc(evac[1].sem, 1)
                    split(h_hi[:, bass.ds(i * 2, 2), :], h_lo[:, bass.ds(i * 2, 2), :], hidden[:])\
                        .then_inc(h_ready.sem, 1)
                with dve.Fori(0, PAIRS_W2) as i:
                    low(l * PAIRS + (m0 + PAIRS_W13 + 1 + i))
                add_to_x(l, m0 + PAIRS_W13 + PAIRS_W2, 0.5)

            def add_to_x(l, m_end, factor):
                wait(dve, unit_done[1], l, m_end)
                for o in range(0, KD, 2):
                    dve.scalar_tensor_tensor(out=x[:, o:o + 2, :], in0=ps[:, o:o + 2, 0:T], scalar=factor,
                                             in1=x[:, o:o + 2, :], op0=ALU.mult, op1=ALU.add)\
                        .then_inc(row_evac.sem, 1)

            dve.memset(eps[:], EPS)
            dve.memset(q_diag[:], 0.0)
            dve.memset(dt_raw[:], 0.0)
            dve.memset(to_end[:], 0.0)
            dve.drain().then_inc(zeroed.sem, 1)
            for o in range(0, KD, 2):
                dve.wait_ge(x_turned.sem, o // 2 + 1)
                dve.tensor_copy(x[:, o:o + 2, :], ps[:, o:o + 2, 0:T]).then_inc(x_first.sem, 1)
            dve.wait_ge(bias_product.sem, 1)
            dve.tensor_tensor(bias_s[:, 0:OLD], ps[:, 4, 0:OLD], mask[:, 0:OLD], ALU.add)
            dve.tensor_tensor(bias_s[:, OLD:], ps[:, 1, 0:NEW], mask[:, OLD:], ALU.add)
            dve.tensor_tensor(lines[:, 0:2], ps[0:HPG, 2:4, 0:W_LINE], line_mask[:, 0:2], ALU.add)
            dve.tensor_tensor(lines[:, 2], ps[0:HPG, 7, 0:W_LINE], line_mask[:, 2], ALU.add)\
                .then_inc(lines_ready.sem, 1)

            with dve.Fori(0, DEPTH) as l:
                m = l * PAIRS
                wait(dve, vec_turned, l, 1)
                dve.tensor_copy(conv_wt[:], ps[:, 5, 0:P])
                dve.tensor_copy(vecs[:], ps[:, 6, 0:80]).then_inc(vec_ready.sem, 1)
                dve.drain()
                norm(l, 1, V_F1)
                swiglu(l, M_W13A, E_W13A, 0)
                norm(l, 2, V_MIX)
                with dve.Fori(0, PAIRS_QKV) as i:
                    low(m + (M_QKV + 1 + i))

                wait(dve, vec_in, l, 160)
                wait(dve, dt_turned, l, 1)
                bias3 = rows3[:, 0, :].unsqueeze(1).broadcast_to((P, 3, HEADS))
                dve.tensor_copy(dt_raw[:, 0:2, :], ps[:, 4, 0:2 * HEADS].rearrange("p (c h) -> p c h", c=2))
                dve.tensor_copy(dt_raw[0:TS, 2, :], ps[0:TS, 4, 2 * HEADS:3 * HEADS])
                for half in range(2):
                    h = slice(64 * half, 64 * half + 64)
                    dve.tensor_copy(skip[h, :], rows3[h, 2, half::2])
                dve.drain()
                dve.tensor_tensor(dt_w[2][:], dt_raw[:], bias3, ALU.add)
                dve.drain()
                dve.scalar_tensor_tensor(out=dt_w[1][:], in0=dt_w[2][:], scalar=-1.0, in1=dt_w[2][:],
                                         op0=ALU.mult, op1=ALU.min).then_inc(dt_exp_asked.sem, 1)
                wait(dve, dt_exp_ready, l, 1)
                y_, z_, z2 = dt_w[0], dt_w[1], dt
                dve.tensor_scalar(z_[:], y_[:], 2.0, None, ALU.add)
                dve.drain()
                dve.reciprocal(z_[:], z_[:])
                dve.drain()
                dve.tensor_tensor(z_[:], z_[:], y_[:], ALU.mult)
                dve.drain()
                dve.tensor_tensor(z2[:], z_[:], z_[:], ALU.mult)
                dve.drain()
                dve.tensor_scalar(y_[:], z2[:], 1.0 / 17, None, ALU.mult)
                for odd in (15, 13, 11, 9, 7, 5, 3):
                    dve.drain()
                    dve.scalar_tensor_tensor(out=y_[:], in0=y_[:], scalar=1.0 / odd, in1=z2[:],
                                             op0=ALU.add, op1=ALU.mult)
                dve.drain()
                dve.scalar_tensor_tensor(out=y_[:], in0=y_[:], scalar=1.0, in1=z_[:], op0=ALU.add, op1=ALU.mult)
                dve.tensor_scalar(dt_w[2][:], dt_w[2][:], 0.0, None, ALU.max)
                dve.drain()
                dve.scalar_tensor_tensor(out=dt[:], in0=y_[:], scalar=2.0, in1=dt_w[2][:], op0=ALU.mult, op1=ALU.add)
                dve.drain()
                dve.scalar_tensor_tensor(out=da[:], in0=dt[:], scalar=-1.0,
                                         in1=a_head[:].unsqueeze(1).broadcast_to((P, 3, HEADS)),
                                         op0=ALU.mult, op1=ALU.mult).then_inc(da_ready.sem, 1)

                for half in range(2):
                    h = slice(64 * half, 64 * half + 64)
                    last = dve.tensor_copy(q_diag[h, :, :, NT * half:NT * half + NT],
                                           qkv[h, 0:6, TP:T].rearrange("p t (b q) -> p t b q", q=NT))
                last.then_inc(q_diag_ready.sem, 1)
                wait(dve, conv_state_turned, l, 1)
                dve.memset(flat[:, :, 0:CW - 1], 0.0)
                for t in range(0, KC, 16):
                    last = dve.tensor_copy(flat[:, t:t + 16, SEQ0:PADDED].rearrange("p t (b c) -> p t b c", c=RUN)
                                           [:, :, :, 0:CW - 1],
                                           ps[:, t // 16, 0:16 * 24].rearrange("p (t b c) -> p t b c", b=NB, c=CW - 1))
                last.then_inc(conv_state_ready.sem, 1)
                for n in range(9):
                    wait(dve, kv_turned, l, n + 1)
                    g, c = n // 3, n % 3
                    if c < 2:
                        dst, src = kv_p[:, c, g], ps[:, n % 4, :]
                    else:
                        dst, src = kv_s[:, g], ps[0:TS, n % 4, :]
                    dve.tensor_copy(dst, src.rearrange("p (k e) -> p k e", k=2)).then_inc(kv_copied.sem, 1)

                def xbc(n):
                    if n % 2 == 0:
                        low_unit(0, m + (M_XBC + n // 2 + 1))
                    wait(dve, xbc_taken, l, 2 * n + 2)
                    dve.tensor_copy(tails[:, 2 * n:2 * n + 2], flat[:, 2 * n:2 * n + 2, TP:TP + 9 * RUN]
                                    .rearrange("p t (j c) -> p t j c", c=RUN)[:, :, :, 0:CW - 1])\
                        .then_inc(tails_ready.sem, 1)
                    if n:
                        wait(dve, xbc_ready, l, n)
                    for w in range(CW):
                        for t in range(2):
                            tile = 2 * n + t
                            src, dst = flat[:, tile, w:w + CONVED], acc[:, t, 0:CONVED]
                            tap = conv_wt[:, w * KC + tile:w * KC + tile + 1]
                            if w == 0:
                                dve.tensor_scalar(dst, src, tap, vecs[:, V_CONVB + tile:V_CONVB + tile + 1],
                                                  ALU.mult, ALU.add)
                            else:
                                last = dve.scalar_tensor_tensor(out=dst, in0=src, scalar=tap, in1=dst,
                                                                op0=ALU.mult, op1=ALU.add)
                        if w < CW - 1:
                            dve.drain()
                    last.then_inc(conv_ready.sem, 1)

                for n in range(sum(XBC_KEYS) // 2):
                    xbc(n)
                wait(dve, sc_s_product, l, 1)
                dve.scalar_tensor_tensor(out=sc_s[:, 0:OLD], in0=ps[:, 4, 0:OLD], scalar=SCALE, in1=bias_s[:, 0:OLD],
                                         op0=ALU.mult, op1=ALU.add)
                dve.scalar_tensor_tensor(out=sc_s[:, OLD:], in0=ps[:, 5, 0:NEW], scalar=SCALE, in1=bias_s[:, OLD:],
                                         op0=ALU.mult, op1=ALU.add)
                dve.drain()
                dve.tensor_reduce(stat_s[2][:], sc_s[:], AX.X, ALU.max)
                dve.drain()
                dve.tensor_scalar(stat_s[0][:], stat_s[2][:], -1.0, None, ALU.mult).then_inc(max_s_ready.sem, 1)
                wait(dve, exp_s_ready, l, 1)
                dve.reciprocal(stat_s[2][:], stat_s[1][:])
                dve.drain()
                dve.tensor_scalar(sc_s[:], sc_s[:], stat_s[2][:], None, ALU.mult).then_inc(p_s_ready.sem, 1)
                done = sum(XBC_KEYS) // 2
                left = sum(XBC_PROMPT) // 2 + 1
                for n in range(done, XBC_UNITS - left):
                    xbc(n)
                wait(dve, o_s_ready, l, 1)
                for pair in range(2):
                    for half in range(2):
                        h = slice(64 * half, 64 * half + 64)
                        src = ps[h, 6 + pair, 0:64].rearrange("p (b c) -> p b c", b=NB)
                        last = dve.tensor_copy(attn[h, pair, TP:T].rearrange("p (b q) -> p b q", q=NT),
                                               src[:, :, NT * half:NT * half + NT])
                last.then_inc(o_s_copied.sem, 1)

                wait(dve, bias_in, 0, 16 * 12)

                def scores(n):
                    i, c, k = n // 2, n % 2, n % 2 + 1
                    bias = bias_p[:].rearrange("p (g i) c -> p g i c", g=NG)[:, :, i, (1 - c) * P:]
                    wait(dve, sc_p_product, l, n + 1)
                    dve.scalar_tensor_tensor(out=sc_p[n % 2][:, 0:2, 0:k * P],
                                             in0=ps[:, 0, :].rearrange("p (g c) -> p g c", g=2)[:, :, 0:k * P],
                                             scalar=SCALE, in1=bias[:, 0:2], op0=ALU.mult, op1=ALU.add)
                    dve.scalar_tensor_tensor(out=sc_p[n % 2][:, 2, 0:k * P], in0=ps[:, 1, 0:k * P],
                                             scalar=SCALE, in1=bias[:, 2], op0=ALU.mult, op1=ALU.add)\
                        .then_inc(sc_p_read.sem, 1)
                    dve.drain()
                    dve.tensor_reduce(stat_p[n % 2][2][:], sc_p[n % 2][:, :, 0:k * P], AX.XY, ALU.max)
                    dve.drain()
                    dve.tensor_scalar(stat_p[n % 2][0][:], stat_p[n % 2][2][:], -1.0, None, ALU.mult)\
                        .then_inc(max_p_ready.sem, 1)

                def weights(n):
                    k = n % 2 + 1
                    wait(dve, exp_p_ready, l, n + 1)
                    dve.reciprocal(stat_p[n % 2][2][:], stat_p[n % 2][1][:])
                    dve.drain()
                    dve.tensor_scalar(sc_p[n % 2][:, :, 0:k * P], sc_p[n % 2][:, :, 0:k * P], stat_p[n % 2][2][:], None,
                                      ALU.mult).then_inc(p_p_ready.sem, 1)

                def outputs(n):
                    i, c = n // 2, n % 2
                    h = slice(64 * (i % 2), 64 * (i % 2) + 64)
                    wait(dve, o_p_ready, l, n + 1)
                    return dve.tensor_copy(attn[h, i // 2, c * P:(c + 1) * P], ps[h, 6 + n % 2, 0:P])

                scores(0)
                for n in range(2 * HPG):
                    weights(n)
                    if n + 1 < 2 * HPG:
                        if n >= 1:
                            wait(dve, pt_p_turned, l, n)
                        scores(n + 1)
                    if n >= 1:
                        outputs(n - 1)
                    if n % 2 and n < 2 * HPG - 1:
                        xbc(XBC_UNITS - left + n // 2)
                outputs(2 * HPG - 1)
                split(ao_hi[:], ao_lo[:], attn[:]).then_inc(attn_ready.sem, 1)

                xbc(XBC_UNITS - 1)

                wait(dve, to_end_ready, l, 1)
                wait(dve, kv_out, l, 16 * 6)

                def times_z(g):
                    wait(dve, silu_z_ready, l, g + 1)
                    rows_y = flat[:, 2 * g:2 * g + 2, 0:T]
                    dve.tensor_tensor(rows_y, rows_y, silu_z[:], ALU.mult).then_inc(z_used.sem, 1)

                for g in range(G):
                    heads = slice(HPG * g, HPG * g + HPG)
                    if g:
                        wait(dve, seg_product, l, g)
                    for c in range(2):
                        for h in range(HPG):
                            dve.tensor_scalar(a_tri[c][:, h, :], tri, da[:, c, HPG * g + h:HPG * g + h + 1], None,
                                              ALU.mult)
                    for h in range(HPG):
                        dve.tensor_scalar(a_tri_s[:, h, :], tri_s, da[0:TS, 2, HPG * g + h:HPG * g + h + 1], None,
                                          ALU.mult)
                    dve.tensor_copy(a_exp[:].rearrange("p (h e) -> p h e", h=HPG),
                                    da[:, 1, heads].unsqueeze(2).broadcast_to((P, HPG, HD)))
                    dve.tensor_copy(a_exp_s[:].rearrange("p (h e) -> p h e", h=HPG),
                                    da[0:TS, 2, heads].unsqueeze(2).broadcast_to((TS, HPG, HD)))\
                        .then_inc(a_tri_ready.sem, 1)
                    wait(dve, ssd_turned, l, g + 1)
                    if g:
                        wait(dve, h0_product, l, 2 * g)
                    for c in range(2):
                        dve.tensor_tensor(xdt[:, c, :].rearrange("p (h e) -> p h e", h=HPG),
                                          ps[:, c, 0:256].rearrange("p (h e) -> p h e", h=HPG),
                                          dt[:, c, heads].unsqueeze(2).broadcast_to((P, HPG, HD)), ALU.mult)
                        dve.tensor_tensor(cbm[:, c, :], ps[:, 3, c * P:(c + 1) * P], tri, ALU.mult)
                    dve.tensor_tensor(xdt_s[:].rearrange("p (h e) -> p h e", h=HPG),
                                      ps[0:TS, 1, 256:512].rearrange("p (h e) -> p h e", h=HPG),
                                      dt[0:TS, 2, heads].unsqueeze(2).broadcast_to((TS, HPG, HD)), ALU.mult)
                    dve.tensor_tensor(cbm_s[:], ps[0:TS, 3, 256:256 + TS], tri_s, ALU.mult)
                    dve.drain()
                    for n, c in ((0, 0), (1, 1), (2, 0)):
                        dve.tensor_tensor(xdte[:, n, :].rearrange("p (h e) -> p h e", h=HPG),
                                          xdt[:, c, :].rearrange("p (h e) -> p h e", h=HPG),
                                          to_end[:, n, heads].unsqueeze(2).broadcast_to((P, HPG, HD)), ALU.mult)
                    dve.tensor_tensor(xdte_s[:].rearrange("p (h e) -> p h e", h=HPG),
                                      xdt_s[:].rearrange("p (h e) -> p h e", h=HPG),
                                      to_end[0:TS, 3, heads].unsqueeze(2).broadcast_to((TS, HPG, HD)), ALU.mult)\
                        .then_inc(xdt_ready.sem, 1)
                    if g:
                        times_z(g - 1)
                    wait(dve, b_ready, l, g + 1)
                    dve.tensor_tensor(b_diag[:], b_tm_s[:].unsqueeze(1).broadcast_to((TS, NB, NS)),
                                      sel_s.unsqueeze(2).broadcast_to((TS, NB, NS)), ALU.mult)\
                        .then_inc(b_diag_ready.sem, 1)
                    wait(dve, dec_ready, l, g + 1)
                    for c in range(2):
                        dve.tensor_tensor(dec[c][:], dec[c][:], cbm[:, c, :].unsqueeze(1).broadcast_to((P, HPG, P)),
                                          ALU.mult)
                    dve.tensor_tensor(dec_s[:], dec_s[:], cbm_s[:].unsqueeze(1).broadcast_to((TS, HPG, TS)), ALU.mult)\
                        .then_inc(m_ready.sem, 1)
                    wait(dve, y_product, l, g + 1)
                    off = ps[:, 1, 0:256].rearrange("p (t c) -> p t c", t=2)
                    dve.tensor_tensor(off_t[:], off, e_off[:], ALU.mult)
                    dve.drain()
                    dve.tensor_tensor(off_t[:], off_t[:], ps[:, 0, 256:512].rearrange("p (t c) -> p t c", t=2), ALU.add)
                    dve.drain()
                    for t in range(2):
                        tile = 2 * g + t
                        d_t = skip[:, tile:tile + 1]
                        dve.scalar_tensor_tensor(out=flat[:, tile, 0:P], in0=flat[:, tile, 0:P], scalar=d_t,
                                                 in1=ps[:, 0, t * P:(t + 1) * P], op0=ALU.mult, op1=ALU.add)
                        dve.scalar_tensor_tensor(out=flat[:, tile, P:TP], in0=flat[:, tile, P:TP], scalar=d_t,
                                                 in1=off_t[:, t, :], op0=ALU.mult, op1=ALU.add)
                    for t in range(2):
                        tile = 2 * g + t
                        wait(dve, h0_product, l, tile + 1)
                        for b in range(NB):
                            dve.scalar_tensor_tensor(out=h0[tile % 3][:, b, :], in0=h0[tile % 3][:, b, :],
                                                     scalar=e_s[:, t, TS + b:TS + b + 1],
                                                     in1=ps[:, 6 + b // 4, (b % 4) * NS:(b % 4 + 1) * NS],
                                                     op0=ALU.mult, op1=ALU.add)
                        dve.drain().then_inc(h_new_ready.sem, 1)
                        dve.tensor_tensor(off_s[:, t, :], ps[:, 3 - 2 * t, 320:320 + TS], e_s[:, t, 0:TS],
                                          ALU.mult)
                        dve.drain()
                        dve.tensor_tensor(off_s[:, t, :], off_s[:, t, :], ps[:, 3, 352 + t * 64:352 + t * 64 + TS],
                                          ALU.add)
                        dve.drain()
                        last = dve.scalar_tensor_tensor(out=flat[:, tile, TP:T], in0=flat[:, tile, TP:T],
                                                        scalar=skip[:, tile:tile + 1], in1=off_s[:, t, :],
                                                        op0=ALU.mult, op1=ALU.add)
                    last.then_inc(y_read.sem, 1)
                dve.drain().then_inc(rows_used.sem, 1)
                times_z(G - 1)
                wait(dve, y_rms_ready, l, 1)
                wait(dve, conv_done_out, l, 32)
                wait(dve, h_end_out, l, 16 * G)
                dve.reciprocal(y_rms[:], y_rms[:])
                for n in range(PAIRS_SO):
                    tiles = slice(4 * n, 4 * n + 4)
                    dve.drain()
                    for t in range(4 * n, 4 * n + 4):
                        dve.scalar_tensor_tensor(out=flat[:, t, 0:T], in0=flat[:, t, 0:T],
                                                 scalar=vecs[:, V_SSD + t:V_SSD + t + 1], in1=y_rms[:, t // 2, :],
                                                 op0=ALU.mult, op1=ALU.mult)
                    split(y_hi[:, tiles], y_lo[:, tiles], flat[:, tiles, 0:T]).then_inc(y_ready.sem, 1)
                    if n == 1:
                        wait(dve, unit_done[1], l, M_AO + 1)
                        for o in range(0, KD, 2):
                            dve.tensor_tensor(gates[:, KD + o:KD + o + 2, :], ps[:, o:o + 2, 0:T],
                                              gates[:, KD + o:KD + o + 2, :], ALU.mult).then_inc(row_evac.sem, 1)

                wait(dve, gates_ready, l, 1)
                wait(dve, unit_done[1], l, M_SO + PAIRS_SO)
                for o in range(0, KD, 2):
                    dve.tensor_tensor(merged[:, o:o + 2, :], ps[:, o:o + 2, 0:T], gates[:, o:o + 2, :], ALU.mult)\
                        .then_inc(row_evac.sem, 1)
                dve.drain()
                for n in range(PAIRS_WO):
                    tiles = slice(4 * n, 4 * n + 4)
                    dve.tensor_tensor(merged[:, tiles], merged[:, tiles], gates[:, KD + 4 * n:KD + 4 * n + 4, :],
                                      ALU.add)
                    split(mg_hi[:, tiles], mg_lo[:, tiles], merged[:, tiles]).then_inc(merged_ready.sem, 1)
                add_to_x(l, M_WO + PAIRS_WO, 1.0)
                norm(l, 3, V_F2)
                swiglu(l, M_W13B, E_W13B, PAIRS_W13)

            dve.wait_ge(end_rms.sem, 1)
            normed(V_FIN)
            dve.drain().then_inc(end_normed.sem, 1)
            dve.wait_ge(end_turned.sem, 2)
            dve.tensor_copy(y_out_s[:].rearrange("p (k c) -> p k c", k=2), ps[0:TS, 5:7, :])\
                .then_inc(end_copied.sem, 1)

        @block.gpsimd
        def _(pool):
            def low_unit(s, m):
                pool.wait_ge(hi_ready[s].sem, m + 1)
                pool.tensor_tensor(w_lo[s][:], raw[s][:], w_hi[s][:].bitcast(F32), ALU.subtract)\
                    .then_inc(lo_ready[s].sem, 1)

            for s in range(2):
                pool.sem_inc(lo_ready[s].sem, 1)
                pool.sem_inc(unit_done[s].sem, 1)
                pool.sem_inc(evac[s].sem, 1)
            pool.sem_inc(vec_turned.sem, 1)
            pool.sem_inc(rows_used.sem, 1)
            pool.sem_inc(row_evac.sem, 4)
            pool.wait_ge(start_in.sem, 16 * 9)
            for g in range(NG):
                last = pool.tensor_tensor(rel_q[:, g], delta[:], rel4[:, 4 * g:4 * g + 4].unsqueeze(1).unsqueeze(3)
                                          .broadcast_to((P, NB, HPG, NT)), ALU.mult)
            last.then_inc(rel_q_ready.sem, 1)
            for s in range(2):
                low_unit(s, 0)
            pool.wait_ge(lines_ready.sem, 1)
            pool.dma_start(lines_dram.rearrange("(g i) w -> i g w", g=NG), lines[:]).then_inc(lines_out.sem, 16)
            pool.wait_ge(lines_out.sem, 16)
            pool.dma_start(skewed.rearrange("h (p w) -> h p w", p=P)[:, :, 0:W_LINE],
                           bass.AP(lines_dram.tensor, lines_dram.offset,
                                   [[W_LINE, NG * HPG], [0, P], [1, W_LINE]])).then_inc(skewed_out.sem, 16)
            pool.wait_ge(skewed_out.sem, 16)
            for h in range(NG * HPG):
                src = skewed[h, 0:P * W_LINE].rearrange("(p w) -> p w", p=P)[:, P - 1:P - 1 + 2 * P]
                pool.dma_start(bias_p[:, h, :], src).then_inc(bias_in.sem, 16)
            with pool.Fori(0, DEPTH) as l:
                m = l * PAIRS
                wait(pool, kv_copied, l, 9)
                for g in range(NG):
                    c0 = 1 if g == 0 else 0
                    dst = kv_prompt[g][bass.ds(l, 1), 0].rearrange("a (c p) k h e -> p (a c) (k h e)", p=P)
                    pool.dma_start(dst, kv_p[:, c0:, g].rearrange("p c k e -> p c (k e)"))\
                        .then_inc(kv_out.sem, 16)
                    dst = kv_sample[g][bass.ds(l, 1)].rearrange("a b t k h e -> (a b t) (k h e)")
                    pool.dma_start(dst, kv_s[:, g].rearrange("p k e -> p (k e)")).then_inc(kv_out.sem, 16)
                with pool.Fori(0, PAIRS_XBC) as i:
                    low_unit(1, m + (M_XBC + 1 + i))
                wait(pool, tails_copied, l, 8)
                pool.dma_start(conv_prompt[bass.ds(l, 1), 0].rearrange("a i c -> (a i) c"), conv_out[0:3, :])\
                    .then_inc(conv_done_out.sem, 16)
                pool.dma_start(conv_sample[bass.ds(l, 1)].rearrange("a b i c -> (a b i) c"), conv_out[3:27, :])\
                    .then_inc(conv_done_out.sem, 16)

                def side_low(n):
                    low_unit(n % 2, m + (M_SIDE + n // 2))

                for g in range(G):
                    if g % 2:
                        side_low(3 * g // 2 + 2)
                    wait(pool, h_end_ready, l, g + 1)
                    dst = ssm_prompt[bass.ds(l, 1), 0, HPG * g:HPG * g + HPG]\
                        .rearrange("a h p n -> (a h p) n")\
                        .rearrange("(t q) n -> q t n", t=2)
                    pool.dma_start(dst, h_end[:]).then_inc(h_end_out.sem, 16)
                    for t in (2 * g, 2 * g + 1):
                        wait(pool, h_new_ready, l, t + 1)
                        dst = ssm_sample[bass.ds(l, 1), :, 2 * t:2 * t + 2].rearrange("a b h p n -> (a h p) b n")
                        pool.dma_start(dst, h0[t % 3][:]).then_inc(h_new_out[t % 3].sem, 16)
                    side_low((3 * g + 1) // 2 + 2)
                with pool.Fori(PAIRS_SIDE, PAIRS_SIDE + PAIRS_G + PAIRS_SO + PAIRS_AO + PAIRS_WO) as i:
                    for s in range(2):
                        low_unit(s, m + (M_SIDE + 1 + i))
            for signal in (kv_out, conv_done_out, h_end_out, *h_new_out):
                pool.wait_ge(signal.sem, DEPTH * signal.per)

        @block.tensor
        def _(pe):
            def product(out, s, at, hi, lo, first, last):
                wh, wl = w_hi[s][:, at:at + P], w_lo[s][:, at:at + P]
                pe.matmul(out, wh, hi, start=first, stop=False)
                pe.matmul(out, wh, lo, start=False, stop=False)
                return pe.matmul(out, wl, hi, start=False, stop=last)

            def u_half(l, n, half):
                pe.wait_ge(u_ready.sem, u_ready.at(l, 2 * n - 1 + half))

            def panel_unit(s, m, norm=None):
                pe.wait_ge(lo_ready[s].sem, m + 2)
                for o in range(2):
                    for k in range(KD):
                        if norm and o == 0 and k % 4 == 0:
                            u_half(*norm, k // 4)
                        last = product(ps[:, 2 * s + o, 0:T], s, k * 256 + o * P, u_hi[:, k, :], u_lo[:, k, :],
                                       k == 0, k == KD - 1)
                last.then_inc(unit_done[s].sem, 1)

            def panels(l, m0, e0, n, norm=None):
                settle(pe)
                with pe.Fori(0, n) as i:
                    for s in range(2):
                        pe.wait_ge(evac[s].sem, l * EVACS + (e0 + 1 + i))
                        panel_unit(s, l * PAIRS + (m0 + i), None if s else norm)

            def row_unit(s, m, k0, kt, hi, lo, first, last, k_reg=None):
                pe.wait_ge(lo_ready[s].sem, m + 2)
                for k in range(kt):
                    for o in range(KD):
                        if k_reg is None:
                            h, w = hi[:, k0 + k, :], lo[:, k0 + k, :]
                        else:
                            h, w = (v[:, bass.ds(k_reg + (k0 + k), 1), :].rearrange("p a t -> p (a t)")
                                    for v in (hi, lo))
                        end = product(ps[:, o, 0:T], s, k * D + o * P, h, w, first and k == 0, last and k == kt - 1)
                end.then_inc(unit_done[s].sem, 1)

            def rows(l, m0, n, hi, lo, tail=0, parts=None):
                def ready(i):
                    if parts:
                        pe.wait_ge(parts.sem, parts.at(l, i + 1))

                ready(0)
                row_unit(0, l * PAIRS + m0, 0, 2, hi, lo, True, False)
                row_unit(1, l * PAIRS + m0, 2, 2, hi, lo, False, n == 1 and not tail)
                stop = n if tail else n - 1
                if stop > 1:
                    with pe.Fori(1, stop) as i:
                        ready(i)
                        for s in range(2):
                            row_unit(s, l * PAIRS + (m0 + i), 2 * s, 2, hi, lo, False, False, i * 4)
                if not tail and n > 1:
                    ready(n - 1)
                    row_unit(0, l * PAIRS + (m0 + n - 1), 4 * (n - 1), 2, hi, lo, False, False)
                    row_unit(1, l * PAIRS + (m0 + n - 1), 4 * (n - 1) + 2, 2, hi, lo, False, True)
                if tail:
                    row_unit(0, l * PAIRS + (m0 + n), 4 * n, 1, hi, lo, False, False)
                    row_unit(1, l * PAIRS + (m0 + n), 4 * n + 1, 1, hi, lo, False, True)

            def column_sums(bank, src, tiles):
                for n, k in enumerate(tiles):
                    last = pe.matmul(ps[:, bank, 0:T], ones, src[:, k, :], start=(n == 0), stop=(n == len(tiles) - 1))
                return last

            def norm(l, n):
                for o in range(4):
                    wait(pe, squared, l, 4 * n - 3 + o)
                    for k in (2 * o, 2 * o + 1):
                        last = pe.matmul(ps[:, 0, 0:T], ones, full[:, k, :], start=(k == 0), stop=(k == KD - 1))
                last.then_inc(sum_ready.sem, 1)

            def swiglu(l, m0, e0, u, h):
                panels(l, m0, e0, PAIRS_W13, (l, u))
                wait(pe, evac[0], l, e0 + PAIRS_W13)
                wait(pe, h_ready, l, h)
                rows(l, m0 + PAIRS_W13, PAIRS_W2 - 1, h_hi, h_lo, tail=1)

            def turn(out, src):
                p = src.shape[0]
                return pe.transpose(out, src, square[0:p, 0, 0:p])

            pe.wait_ge(const_in.sem, 32)
            pe.wait_ge(x_in_ready.sem, 32)
            for k in range(KD):
                for c in range(2):
                    turn(ps[:, k, c * P:(c + 1) * P], x_in[:, c, k * P:(k + 1) * P])
                last = turn(ps[:, k, TP:T], xs_in[:, k * P:(k + 1) * P])
                if k % 2:
                    last.then_inc(x_turned.sem, 1)
            pe.wait_ge(x_first.sem, 4)
            pe.wait_ge(rel_q_ready.sem, 1)
            col = 0
            for g in range(NG):
                lhs = rel_q[:, g].rearrange("p b i q -> p (b i q)")
                pe.matmul(ps[:, 4, col:col + KEYS[g]], lhs, hot[:, col:col + KEYS[g]], start=True, stop=True)
                new = OLD + g * TS
                pe.matmul(ps[:, 1, g * TS:(g + 1) * TS], lhs, hot[:, new:new + TS], start=True, stop=True)
                last = pe.matmul(ps[0:HPG, (2, 3, 7)[g], 0:W_LINE], rel4[0:32, 4 * g:4 * g + 4], line_hot[:, g, :],
                                 start=True, stop=True)
                col += KEYS[g]
            last.then_inc(bias_product.sem, 1)

            with pe.Fori(0, DEPTH) as l:
                m = l * PAIRS
                norm(l, 1)
                wait(pe, vec_in, l, 160)
                wait(pe, row_evac, l, 0)
                turn(ps[:, 5, 0:P], vec_a[:])
                turn(ps[:, 6, 0:80], vec_b[:]).then_inc(vec_turned.sem, 1)
                pe.wait_ge(lines_ready.sem, 1)
                swiglu(l, M_W13A, E_W13A, 1, PAIRS_W13)
                norm(l, 2)
                wait(pe, row_evac, l, R_W2A + 4)
                pe.wait_ge(lo_ready[0].sem, m + (M_QKV + 2))
                for k in range(KD):
                    if k % 4 == 0:
                        u_half(l, 2, k // 4)
                    last = product(ps[:, 0, 0:T], 0, k * 256, u_hi[:, k, :], u_lo[:, k, :], k == 0, k == KD - 1)
                last.then_inc(unit_done[0].sem, 1)
                panel_unit(1, m + M_QKV)
                with pe.Fori(1, PAIRS_QKV) as i:
                    for s in range(2):
                        pe.wait_ge(evac[s].sem, l * EVACS + (E_QKV + 1 + i))
                        panel_unit(s, m + (M_QKV + i))

                wait(pe, evac[0], l, E_QKV + PAIRS_QKV)
                wait(pe, evac[1], l, E_QKV + PAIRS_QKV)
                settle(pe)
                for c in range(2):
                    turn(ps[:, 4, c * HEADS:(c + 1) * HEADS], dt_fm[:, c * P:(c + 1) * P])
                turn(ps[0:TS, 4, 2 * HEADS:3 * HEADS], dt_fm[:, TP:T]).then_inc(dt_turned.sem, 1)
                wait(pe, conv_state_in, l, 16)
                settle(pe)
                for t in range(KC):
                    last = turn(ps[:, t // 16, (t % 16) * 24:(t % 16 + 1) * 24], conv_in[:, t * P:(t + 1) * P])
                last.then_inc(conv_state_turned.sem, 1)
                wait(pe, da_ready, l, 1)
                pe.matmul(ps[:, 4, 128:160], sgt, da[:, 0, :], start=True, stop=True)
                pe.matmul(ps[:, 4, 160:192], sgt, da[:, 1, :], start=True, stop=True)
                pe.matmul(ps[:, 4, 192:224], sgt, da[:, 0, :], start=True, stop=False)
                pe.matmul(ps[:, 4, 192:224], ones, da[:, 1, :], start=False, stop=True)
                pe.matmul(ps[0:TS, 4, 224:256], sgt_s, da[0:TS, 2, :], start=True, stop=True)\
                    .then_inc(to_end_product.sem, 1)
                wait(pe, conv_state_ready, l, 1)
                for n in range(9):
                    g, c = n // 3, n % 3
                    if n >= 4:
                        wait(pe, kv_copied, l, n - 3)
                    cols = slice(c * P, (c + 1) * P) if c < 2 else slice(TP, T)
                    for kv in range(2):
                        for j in range(2):
                            at = kv * 256 + j * P
                            last = turn(ps[0:(P if c < 2 else TS), n % 4, at:at + P],
                                        qkv[:, 6 + 6 * kv + 2 * g + j, cols])
                    last.then_inc(kv_turned.sem, 1)

                wait(pe, kv_copied, l, 9)
                wait(pe, q_diag_ready, l, 1)
                wait(pe, to_end_ready, l, 1)

                def xbc(q):
                    n, s = q // 2, q // 2 % 2
                    if q >= 2:
                        wait(pe, xbc_taken, l, q - 1)
                    if q % 2 == 0:
                        pe.wait_ge(lo_ready[s].sem, m + (M_XBC + n // 2 + 2))
                    for k in range(KD):
                        last = product(ps[:, XBC_BANK + q % 2, 0:T], s, k * 256 + q % 2 * P, u_hi[:, k, :],
                                       u_lo[:, k, :], k == 0, k == KD - 1)
                    last.then_inc(unit_done[s].sem if q % 2 else xbc_first.sem, 1)
                    return q + 1

                def k_turn(b):
                    wait(pe, cache_in[b % KV_BUFS], l, 48 * (b // KV_BUFS + 1))
                    if b >= 2:
                        wait(pe, k_t_ready, l, b - 1)
                    for pair in range(2):
                        bank = 4 + 2 * (b % 2) + pair
                        for kt in range(4):
                            rows_k = P if kt < 3 else 64
                            last = turn(ps[:, bank, kt * P:kt * P + rows_k],
                                        kv_in[b % KV_BUFS][0:rows_k, kt, pair * P:(pair + 1) * P])
                    last.then_inc(k_turned.sem, 1)

                def k_scores(b):
                    wait(pe, k_t_ready, l, b + 1)
                    for pair in range(2):
                        for kt in range(4):
                            rows_k, g = (P, (kt + 1) // 2) if kt < 3 else (64, 2)
                            at = kt * P + b * 16 + pair * 8
                            pe.matmul(ps[0:rows_k, 0, at:at + 8], k_t[b % 2][:, pair, kt * P:kt * P + rows_k],
                                      q_diag[:, 2 * g + pair, b, :], start=True, stop=True)

                q = 0
                k_turn(0)
                for b in range(NB):
                    if b + 1 < NB:
                        k_turn(b + 1)
                    for _ in range(XBC_KEYS[b]):
                        q = xbc(q)
                    k_scores(b)
                for g in range(NG):
                    for pair in range(2):
                        tile = 2 * g + pair
                        out = ps[0:TS, 1, g * P:(g + 1) * P].rearrange("p (b x c) -> p b x c", b=NB, x=2)
                        last = pe.matmul(out[:, :, pair, :], qkv[:, 6 + tile, TP:T], q_diag[:, tile], start=True,
                                         stop=True)
                last.then_inc(scores_t_ready.sem, 1)
                for _ in range(XBC_SOFTMAX[0]):
                    q = xbc(q)
                wait(pe, st_ready, l, 1)
                for kt in range(4):
                    rows_k = P if kt < 3 else 64
                    turn(ps[:, 4, kt * P:kt * P + rows_k], st[0:rows_k, kt, :])
                for g in range(NG):
                    last = turn(ps[:, 5, g * TS:(g + 1) * TS], st_new[:, g, :])
                last.then_inc(sc_s_product.sem, 1)
                for _ in range(XBC_SOFTMAX[1]):
                    q = xbc(q)
                wait(pe, p_s_ready, l, 1)
                for kt in range(4):
                    rows_k = P if kt < 3 else 64
                    turn(ps[0:rows_k, 4, kt * P:(kt + 1) * P], sc_s[:, kt * P:kt * P + rows_k])
                for g in range(NG):
                    last = turn(ps[0:TS, 5, g * P:(g + 1) * P], sc_s[:, OLD + g * TS:OLD + (g + 1) * TS])
                last.then_inc(pt_s_turned.sem, 1)
                for _ in range(XBC_SOFTMAX[2]):
                    q = xbc(q)
                wait(pe, pt_s_ready, l, 1)
                for pair in range(2):
                    for g in range(NG):
                        rhs = st_new[:, g, :].rearrange("p (b x c) -> p b x c", b=NB, x=2)[:, :, pair, :]
                        pe.matmul(ps[:, 6 + pair, 0:64], kv_s[:, g, 1, pair * P:(pair + 1) * P], rhs,
                                  start=(g == 0), stop=False)
                for b in range(NB):
                    for _ in range(XBC_VALUES[b]):
                        q = xbc(q)
                    wait(pe, cache_in[b % KV_BUFS], l, 48 * ((NB + b) // KV_BUFS + 1))
                    for pair in range(2):
                        for kt in range(4):
                            rows_k = P if kt < 3 else 64
                            at = b * 16 + pair * 8
                            last = pe.matmul(ps[:, 6 + pair, b * 8:b * 8 + 8],
                                             kv_in[b % KV_BUFS][0:rows_k, kt, pair * P:(pair + 1) * P],
                                             st[0:rows_k, kt, at:at + 8], start=False, stop=(kt == 3 and b == NB - 1))
                    last.then_inc(v_used.sem, 1)
                pe.drain().then_inc(o_s_ready.sem, 1)

                wait(pe, o_s_copied, l, 1)

                def scores(n):
                    i, c, k = n // 2, n % 2, n % 2 + 1
                    if n:
                        wait(pe, sc_p_read, l, n)
                    half = slice(64 * (i % 2), 64 * (i % 2) + 64)
                    for g in range(NG):
                        tile = 2 * g + i // 2
                        bank, at = g // 2, (g % 2) * 256
                        last = pe.matmul(ps[:, bank, at:at + k * P], qkv[half, tile, c * P:(c + 1) * P],
                                         qkv[half, 6 + tile, 0:k * P], start=True, stop=True)
                    last.then_inc(sc_p_product.sem, 1)

                def mix(n):
                    i, c, k = n // 2, n % 2, n % 2 + 1
                    wait(pe, p_p_ready, l, n + 1)
                    for g in range(NG):
                        for kt in range(k):
                            last = turn(ps[:, 4 + kt, g * P:(g + 1) * P], sc_p[n % 2][:, g, kt * P:(kt + 1) * P])
                    last.then_inc(pt_p_turned.sem, 1)
                    for t in range(XBC_PROMPT[n]):
                        xbc(q + sum(XBC_PROMPT[:n]) + t)
                    wait(pe, pt_p_ready, l, n + 1)
                    half = slice(64 * (i % 2), 64 * (i % 2) + 64)
                    for g in range(NG):
                        for kt in range(k):
                            last = pe.matmul(ps[half, 6 + n % 2, 0:P], kv_p[:, kt, g, 1, i * HD:(i + 1) * HD],
                                             pt_p[n % 2][:, g, kt, :], start=(g == 0 and kt == 0),
                                             stop=(g == NG - 1 and kt == k - 1))
                    last.then_inc(o_p_ready.sem, 1)

                scores(0)
                for n in range(2 * HPG):
                    if n + 1 < 2 * HPG:
                        scores(n + 1)
                    mix(n)
                wait(pe, tails_ready, l, XBC_UNITS)
                wait(pe, xbc_taken, l, KC)
                wait(pe, attn_ready, l, 1)
                for n in range(8):
                    for t in range(4 * n, 4 * n + 4):
                        last = turn(ps[0:27, n, (t % 4) * P:(t % 4 + 1) * P],
                                    tails[:, t].rearrange("p j c -> p (j c)"))
                    last.then_inc(tails_turned.sem, 1)

                def side(q):
                    n, s, half = q // 2, q // 2 % 2, q % 2
                    if q:
                        wait(pe, side_taken, l, q)
                    if not half:
                        pe.wait_ge(lo_ready[s].sem, m + (M_SIDE + n // 2 + 2))
                    for k in range(KD):
                        last = product(ps[:, SIDE_BANK, 0:T], s, k * 256 + half * P, u_hi[:, k, :], u_lo[:, k, :],
                                       k == 0, k == KD - 1)
                    last.then_inc(unit_done[s].sem if half else side_first.sem, 1)

                wait(pe, xbc_ready, l, XBC_UNITS)
                wait(pe, tails_copied, l, 8)
                for g in range(G):
                    fb, fc = flat[:, TILE_B + g, :], flat[:, TILE_C + g, :]
                    if g:
                        wait(pe, y_read, l, g)
                        wait(pe, h_end_ready, l, g)
                    for c in range(3):
                        cols = slice(c * P, (c + 1) * P) if c < 2 else slice(TP, T)
                        n = P if c < 2 else TS
                        for t in range(2):
                            at = t * P + (256 if c == 2 else 0)
                            turn(ps[0:n, min(c, 1), at:at + P], flat[:, 2 * g + t, cols])
                        turn(ps[0:n, 7, c * P:(c + 1) * P], fb[:, cols])
                        last = pe.matmul(ps[0:n, 3, c * P:c * P + n], fb[:, cols], fc[:, cols], start=True, stop=True)
                    last.then_inc(ssd_turned.sem, 1)
                    wait(pe, a_tri_ready, l, g + 1)
                    if g:
                        wait(pe, h0_t_ready, l, 2 * g)
                    for c in range(2):
                        pe.matmul(ps[:, 4 + c, :], sgt, a_tri[c][:].rearrange("p h c -> p (h c)"), start=True, stop=True)
                    pe.matmul(ps[0:TS, 6, 336:464], sgt_s, a_tri_s[:].rearrange("p h c -> p (h c)"), start=True,
                              stop=True)
                    for t in range(2):
                        pe.matmul(ps[:, 6, t * P:(t + 1) * P], a_exp[:, t * P:(t + 1) * P], tri, start=True, stop=True)
                        last = pe.matmul(ps[:, 6, 256 + t * 40:256 + (t + 1) * 40], a_exp_s[:, t * P:(t + 1) * P],
                                         tri_sel_s, start=True, stop=True)
                    last.then_inc(seg_product.sem, 1)
                    wait(pe, xdt_ready, l, g + 1)
                    wait(pe, b_ready, l, g + 1)
                    pe.matmul(ps[:, 7, 0:256], b_tm[:, 0, :], xdte[:, 0, :], start=True, stop=True)\
                        .then_inc(h_mid_product.sem, 1)
                    side(3 * g)
                    wait(pe, m_ready, l, g + 1)
                    for c in range(2):
                        for h in range(HPG):
                            half = slice(64 * (h % 2), 64 * (h % 2) + 64)
                            at = c * 256 + (h // 2) * P
                            pe.matmul(ps[half, 0, at:at + P], xdt[:, c, h * HD:(h + 1) * HD], dec[c][:, h, :],
                                      start=True, stop=True)
                    for h in range(HPG):
                        half = slice(64 * (h % 2), 64 * (h % 2) + 64)
                        at = 352 + (h // 2) * 64
                        pe.matmul(ps[half, 3, at:at + TS], xdt_s[:, h * HD:(h + 1) * HD], dec_s[:, h, :], start=True,
                                  stop=True)
                    wait(pe, h_mid_ready, l, g + 1)
                    for t in range(2):
                        pe.matmul(ps[:, 1, t * P:(t + 1) * P], h_mid[:, t * P:(t + 1) * P], fc[:, P:TP], start=True,
                                  stop=True)
                    for t in range(2):
                        out = ps[:, 7, 256 + t * P:256 + (t + 1) * P]
                        pe.matmul(out, xdte[:, 2, t * P:(t + 1) * P], b_tm[:, 0, :], start=True, stop=False)
                        last = pe.matmul(out, xdte[:, 1, t * P:(t + 1) * P], b_tm[:, 1, :], start=False, stop=True)
                    last.then_inc(y_product.sem, 1)
                    wait(pe, b_diag_ready, l, g + 1)
                    for t in range(2):
                        tile = 2 * g + t
                        wait(pe, h0_in[tile % 3], l, 16 * (tile // 3 + 1))
                        if t:
                            wait(pe, h0_t_ready, l, tile)
                        for b in range(NB):
                            last = turn(ps[:, 4 + b // 4, (b % 4) * P:(b % 4 + 1) * P], h0[tile % 3][:, b, :])
                        last.then_inc(h0_turned.sem, 1)
                        if t:
                            side(3 * g + 1)
                        wait(pe, h_end_ready, l, g + 1)
                        if t:
                            wait(pe, h_new_ready, l, tile)
                        for n in range(2):
                            pe.matmul(ps[:, 6 + n, :], xdte_s[:, t * P:(t + 1) * P],
                                      b_diag[:, 4 * n:4 * n + 4, :].rearrange("p b n -> p (b n)"), start=True, stop=True)
                        wait(pe, h0_t_ready, l, tile + 1)
                        for b in range(NB):
                            last = pe.matmul(ps[:, 3 - 2 * t, 320 + b * NT:320 + (b + 1) * NT], h0_t[:, b, :],
                                             fc[:, TP + b * NT:TP + (b + 1) * NT], start=True, stop=True)
                        last.then_inc(h0_product.sem, 1)
                    side(3 * g + 2)
                wait(pe, y_read, l, G)
                wait(pe, h_new_ready, l, KI)
                wait(pe, side_taken, l, SIDE_TILES)
                panels(l, M_G, E_G, 1)
                for n in (3, 2, 1, 0):
                    wait(pe, y_sq_ready, l, 4 - n)
                    if n == 1:
                        wait(pe, evac[0], l, E_G + 1)
                        wait(pe, evac[1], l, E_G + 1)
                    for g in (2 * n, 2 * n + 1):
                        last = column_sums(g, y_sq, (2 * g, 2 * g + 1))
                last.then_inc(y_sum_ready.sem, 1)
                wait(pe, y_rms_ready, l, 1)
                panels(l, M_G + 1, E_G + 1, PAIRS_G - 1)
                wait(pe, evac[0], l, E_G + PAIRS_G)
                wait(pe, evac[1], l, E_G + PAIRS_G)
                row_unit(0, m + M_AO, 0, 1, ao_hi, ao_lo, True, False)
                row_unit(1, m + M_AO, 1, 1, ao_hi, ao_lo, False, True)
                wait(pe, row_evac, l, R_AO + 4)
                rows(l, M_SO, PAIRS_SO, y_hi, y_lo, parts=y_ready)
                wait(pe, row_evac, l, R_SO + 4)
                rows(l, M_WO, PAIRS_WO, mg_hi, mg_lo, parts=merged_ready)
                norm(l, 3)
                wait(pe, row_evac, l, R_WO + 4)
                swiglu(l, M_W13B, E_W13B, 3, 2 * PAIRS_W13)

            wait(pe, row_evac, DEPTH, 0)
            pe.wait_ge(end_squared.sem, 1)
            column_sums(4, full, range(KD)).then_inc(end_sum.sem, 1)
            pe.wait_ge(end_normed.sem, 1)
            for c in range(2):
                for k in range(KD):
                    last = turn(ps[:, 2 * c + k // 4, (k % 4) * P:(k % 4 + 1) * P], full[:, k, c * P:(c + 1) * P])
            last.then_inc(end_turned.sem, 1)
            for k in range(KD):
                last = turn(ps[0:TS, 5 + k // 4, (k % 4) * P:(k % 4 + 1) * P], full[:, k, TP:T])
            last.then_inc(end_turned.sem, 1)


_INS = ['x_prompt', 'x_sample', 'cache_kv_w128', 'cache_kv_w512', 'cache_kv_w2048', 'state_conv', 'state_ssm',
        'rel_bias', 'ffn1_norm', 'ffn1_w13', 'ffn1_w2', 'mix_norm', 'w_in', 'conv_w', 'conv_b', 'dt_bias',
        'a_log', 'd_skip', 'ssd_norm', 'w_ssd_out', 'w_attn_out', 'w_o', 'ffn2_norm', 'ffn2_w13', 'ffn2_w2',
        'final_norm']


def _outs(depth):
    return [(1, TP, D), (NB, NT, D),
            (depth, 1, 128, 2, 4, HD), (depth, 1, 256, 2, 4, HD), (depth, 1, 256, 2, 4, HD),
            (depth, 1, CW - 1, CONV), (depth, 1, HEADS, HD, NS),
            (depth, NB, NT, 2, 4, HD), (depth, NB, NT, 2, 4, HD), (depth, NB, NT, 2, 4, HD),
            (depth, NB, CW - 1, CONV), (depth, NB, HEADS, HD, NS)]


def build(nc, inputs):
    arrays, args = {}, []
    given = {name: np.ascontiguousarray(inputs[name]) for name in _INS}
    given.update(constants())
    for name, a in given.items():
        arrays[f"in_{name}_dram"] = a
        args.append(nc.dram_tensor(f"in_{name}_dram", a.shape, mybir.dt.from_np(a.dtype), kind="ExternalInput").ap())
    outs = _outs(given["w_in"].shape[0])
    for i, shape in enumerate(outs):
        args.append(nc.dram_tensor(f"out_{i}_dram", shape, F32, kind="ExternalOutput").ap())
    trunk(nc, *args)
    return arrays, len(outs)


def kernel(**inputs):
    import concourse.bacc as _bacc
    from concourse.bass_utils import run_bass_kernel_spmd as _run

    nc = _bacc.Bacc("TRN2", target_bir_lowering=False, num_devices=1)
    arrays, n = build(nc, inputs)
    r = _run(nc, [arrays], core_ids=[0])
    return tuple(r.results[0][f"out_{i}_dram"] for i in range(n))
```
